# Optimizing a Trainium2 kernel written in Bass

```python
import math
import jax, jax.numpy as jnp
from jax import lax
import numpy as np
import jax
import jax.numpy as jnp

D_MODEL = 1024
BATCH = 1
SEQ = 512
DEPTH = 2

MIX_WIDTH = D_MODEL
PLE_DIM = 256
QBLOCK = 128
EPS = 1e-6
W_A = MIX_WIDTH // 4
POOL_WINDOWS = (2, 4, 8, 16)
N_POOL_GROUPS = 4
POOL_GC = W_A // N_POOL_GROUPS
W_B = MIX_WIDTH - W_A
DV_B = 128
H_B = W_B // DV_B
DK_B = DV_B // 2
B_ROT = DK_B // 4
ROPE_THETA = 500000.0
W_C = MIX_WIDTH // 2
DV_C = 128
H_C = W_C // DV_C
D_NOPE = 128
D_ROPE = 64
DQK_C = D_NOPE + D_ROPE
Q_LORA = 256
KV_LORA = 128
MLA_THETA = 10000.0
W_D = MIX_WIDTH - W_C
DK_D = 128
DV_D = 128
H_D = W_D // DV_D
CONV_K = 4
CHUNK = 64
CONV_CH = H_D * (2 * DK_D + DV_D)
EVEN_WIDTHS = (W_A, W_A, 2 * H_B * DK_B, 2 * H_B * DK_B, H_B * DV_B, W_B)
ODD_WIDTHS = (Q_LORA, KV_LORA, D_ROPE, W_C, CONV_CH, H_D, H_D, W_D)


def _split(z, widths):
    idx = np.cumsum(widths)[:-1].tolist()
    return jnp.split(z, idx, axis=-1)

def rmsnorm(x, g):
    xf = x.astype(jnp.float32)
    y = xf * lax.rsqrt(jnp.mean(xf * xf, axis=-1, keepdims=True) + EPS)
    return (y * g.astype(jnp.float32)).astype(x.dtype)

def l2norm(x):
    xf = x.astype(jnp.float32)
    return xf * lax.rsqrt(jnp.sum(xf * xf, axis=-1, keepdims=True) + EPS)

def rope(x, positions, theta):
    r = x.shape[-1]
    half = r // 2
    inv = jnp.power(jnp.float32(theta), -jnp.arange(half, dtype=jnp.float32) * (2.0 / r))
    ang = positions.astype(jnp.float32)[..., None] * inv
    ang = ang.reshape(ang.shape[:2] + (1,) * (x.ndim - 3) + (half,))
    c, s = jnp.cos(ang), jnp.sin(ang)
    xf = x.astype(jnp.float32)
    x1, x2 = xf[..., :half], xf[..., half:]
    return jnp.concatenate([x1 * c - x2 * s, x2 * c + x1 * s], axis=-1).astype(x.dtype)

def partial_rope(x, positions, rot_dim, theta):
    return jnp.concatenate([rope(x[..., :rot_dim], positions, theta), x[..., rot_dim:]], axis=-1)

def _sweep_query_blocks(block_fn, q):
    B, T = q.shape[:2]
    nb = T // QBLOCK
    qb = jnp.moveaxis(q.reshape((B, nb, QBLOCK) + q.shape[2:]), 1, 0)
    starts = jnp.arange(nb, dtype=jnp.int32) * QBLOCK
    out = lax.map(block_fn, (qb, starts))
    return jnp.moveaxis(out, 0, 1).reshape((B, T) + out.shape[3:])

def multiscale_pool(x):
    B, T, _ = x.shape
    xf = x.astype(jnp.float32).reshape(B, T, N_POOL_GROUPS, POOL_GC)
    S = jnp.pad(jnp.cumsum(xf, axis=1), ((0, 0), (1, 0), (0, 0), (0, 0)))
    t = jnp.arange(T)
    outs = []
    for gi, w in enumerate(POOL_WINDOWS):
        upper = S[:, 1:, gi]
        lower = jnp.pad(S[:, :T + 1 - w, gi], ((0, 0), (w - 1, 0), (0, 0)))
        cnt = jnp.minimum(t + 1, w).astype(jnp.float32)[None, :, None]
        outs.append((upper - lower) / cnt - xf[:, :, gi])
    return jnp.stack(outs, axis=2).astype(x.dtype)

def diff_attention(q, k, v, lam):
    T = k.shape[1]
    scale = q.shape[-1] ** -0.5
    kpos = jnp.arange(T)

    def block(args):
        qb, start = args
        s = jnp.einsum('bqhmd,bkhmd->bhmqk', qb, k).astype(jnp.float32) * scale
        mask = kpos[None, :] <= (start + jnp.arange(QBLOCK))[:, None]
        pr = jax.nn.softmax(jnp.where(mask, s, -jnp.inf), axis=-1)
        a = pr[:, :, 0] - lam * pr[:, :, 1]
        return jnp.einsum('bhqk,bkhe->bqhe', a.astype(v.dtype), v)

    return _sweep_query_blocks(block, q)

def causal_attention(q, k, v):
    T = k.shape[1]
    scale = q.shape[-1] ** -0.5
    kpos = jnp.arange(T)

    def block(args):
        qb, start = args
        s = jnp.einsum('bqhd,bkhd->bhqk', qb, k).astype(jnp.float32) * scale
        mask = kpos[None, :] <= (start + jnp.arange(QBLOCK))[:, None]
        pr = jax.nn.softmax(jnp.where(mask, s, -jnp.inf), axis=-1)
        return jnp.einsum('bhqk,bkhe->bqhe', pr.astype(v.dtype), v)

    return _sweep_query_blocks(block, q)

def causal_depthwise_conv(x, w):
    K, C = w.shape
    return lax.conv_general_dilated(
        x, w[:, None, :].astype(x.dtype), window_strides=(1,), padding=[(K - 1, 0)],
        dimension_numbers=('NWC', 'WIO', 'NWC'), feature_group_count=C)

def gated_delta_rule(q, k, v, g, beta):
    B, T, H, DK = q.shape
    DV = v.shape[-1]
    N = T // CHUNK
    f32 = jnp.float32

    def to_chunks(a):
        a = a.astype(f32).reshape((B, N, CHUNK, H) + a.shape[3:])
        return jnp.moveaxis(a, 3, 1)

    q, k, v, g, beta = (to_chunks(a) for a in (q, k, v, g, beta))
    gc = jnp.cumsum(g, axis=-1)
    i = jnp.arange(CHUNK)
    incl = i[:, None] >= i[None, :]
    strict = i[:, None] > i[None, :]
    gamma = jnp.exp(jnp.where(incl, gc[..., :, None] - gc[..., None, :], -jnp.inf))
    kk = jnp.einsum('bhncd,bhnsd->bhncs', k, k)
    a_mat = jnp.eye(CHUNK, dtype=f32) + jnp.where(strict, kk * gamma * beta[..., :, None], 0.0)
    rhs = jnp.concatenate([v * beta[..., None], k * (beta * jnp.exp(gc))[..., None]], axis=-1)
    sol = lax.linalg.triangular_solve(a_mat, rhs, left_side=True, lower=True, unit_diagonal=True)
    u, w = sol[..., :DV], sol[..., DV:]
    qk = jnp.einsum('bhncd,bhnsd->bhncs', q, k) * gamma
    q_dec = q * jnp.exp(gc)[..., None]
    k_dec = k * jnp.exp(gc[..., -1:] - gc)[..., None]
    g_last = jnp.exp(gc[..., -1])

    def step(S, inp):
        qk_c, qd_c, kd_c, u_c, w_c, gl_c = inp
        v_new = u_c - jnp.einsum('bhcd,bhde->bhce', w_c, S)
        o = jnp.einsum('bhcd,bhde->bhce', qd_c, S) + jnp.einsum('bhcs,bhse->bhce', qk_c, v_new)
        S = S * gl_c[..., None, None] + jnp.einsum('bhcd,bhce->bhde', kd_c, v_new)
        return S, o

    xs = tuple(jnp.moveaxis(a, 2, 0) for a in (qk, q_dec, k_dec, u, w, g_last))
    _, o = lax.scan(step, jnp.zeros((B, H, DK, DV), f32), xs)
    o = jnp.moveaxis(o, 0, 2)
    return jnp.moveaxis(o, 1, 3).reshape(B, T, H, DV)

def even_layer(h, layer_idx, positions, w_in, pool_w, pool_scale, q_norm, k_norm,
               lam_vec, subln, w_out):
    B, T, _ = h.shape
    z = h @ w_in
    a_in, a_gate, q, k, v, b_gate = _split(z, EVEN_WIDTHS)
    a = multiscale_pool(a_in)
    a = jnp.einsum('btgc,gce->btge', a, pool_w).reshape(B, T, W_A) * pool_scale
    a = a * jax.nn.silu(a_gate)
    q = q.reshape(B, T, H_B, 2, DK_B)
    k = k.reshape(B, T, H_B, 2, DK_B)
    v = v.reshape(B, T, H_B, DV_B)
    q = partial_rope(rmsnorm(q, q_norm), positions, B_ROT, ROPE_THETA)
    k = partial_rope(rmsnorm(k, k_norm), positions, B_ROT, ROPE_THETA)
    lam_init = 0.8 - 0.6 * math.exp(-0.3 * layer_idx)
    lv = lam_vec.astype(jnp.float32)
    lam = jnp.exp(jnp.sum(lv[0] * lv[1])) - jnp.exp(jnp.sum(lv[2] * lv[3])) + lam_init
    o = diff_attention(q, k, v, lam)
    o = rmsnorm(o, subln) * (1.0 - lam_init)
    o = o.reshape(B, T, W_B) * jax.nn.silu(b_gate)
    return jnp.concatenate([a, o], axis=-1) @ w_out

def odd_layer(h, positions, w_in, q_a_norm, w_uq, kv_a_norm, w_ukv, q_norm, k_norm,
              conv_w, a_log, dt_bias, o_norm, w_out):
    B, T, _ = h.shape
    z = h @ w_in
    cq, ckv, k_rope, c_gate, qkv, d_b, d_a, d_gate = _split(z, ODD_WIDTHS)
    q = (rmsnorm(cq, q_a_norm) @ w_uq).reshape(B, T, H_C, DQK_C)
    kv = (rmsnorm(ckv, kv_a_norm) @ w_ukv).reshape(B, T, H_C, D_NOPE + DV_C)
    k_nope, v_c = kv[..., :D_NOPE], kv[..., D_NOPE:]
    k = jnp.concatenate([k_nope, jnp.broadcast_to(k_rope[:, :, None, :], (B, T, H_C, D_ROPE))], axis=-1)
    q = rmsnorm(q, q_norm)
    k = rmsnorm(k, k_norm)
    q = jnp.concatenate([q[..., :D_NOPE], rope(q[..., D_NOPE:], positions, MLA_THETA)], axis=-1)
    k = jnp.concatenate([k[..., :D_NOPE], rope(k[..., D_NOPE:], positions, MLA_THETA)], axis=-1)
    oc = causal_attention(q, k, v_c).reshape(B, T, W_C) * jax.nn.silu(c_gate)
    qkv = jax.nn.silu(causal_depthwise_conv(qkv, conv_w))
    dq = qkv[..., :H_D * DK_D].reshape(B, T, H_D, DK_D)
    dk = qkv[..., H_D * DK_D:2 * H_D * DK_D].reshape(B, T, H_D, DK_D)
    dv = qkv[..., 2 * H_D * DK_D:].reshape(B, T, H_D, DV_D)
    dq = l2norm(dq) * (DK_D ** -0.5)
    dk = l2norm(dk)
    beta = jax.nn.sigmoid(d_b.astype(jnp.float32))
    g = -jnp.exp(a_log.astype(jnp.float32)) * jax.nn.softplus(
        d_a.astype(jnp.float32) + dt_bias.astype(jnp.float32))
    od = gated_delta_rule(dq, dk, dv, g, beta).astype(h.dtype)
    od = rmsnorm(od, o_norm).reshape(B, T, W_D) * jax.nn.silu(d_gate)
    return jnp.concatenate([oc, od], axis=-1) @ w_out

def first_inputs(seed: int = 0) -> dict:
    key = jax.random.key(seed)
    ks = jax.random.split(key, 32)
    f32 = jnp.float32
    n_even = (DEPTH + 1) // 2
    n_odd = DEPTH // 2

    def nrm(k, shape, fan_in):
        return jax.random.normal(k, shape, f32) * (fan_in ** -0.5)

    def gain(k, shape):
        return 1.0 + 0.02 * jax.random.normal(k, shape, f32)

    x = jax.random.normal(ks[0], (BATCH, SEQ, D_MODEL), f32)
    p = jax.random.normal(ks[1], (DEPTH, BATCH, SEQ, PLE_DIM), f32)
    positions = jnp.broadcast_to(jnp.arange(SEQ, dtype=jnp.int32), (BATCH, SEQ))
    dt = jnp.exp(jax.random.uniform(ks[24], (n_odd, H_D), f32, math.log(1e-3), math.log(1e-1)))
    return {
        "x": x,
        "p": p,
        "positions": positions,
        "norm_g": gain(ks[2], (DEPTH, D_MODEL)),
        "ple_w_gate": nrm(ks[3], (DEPTH, D_MODEL, D_MODEL), D_MODEL),
        "ple_w_proj": nrm(ks[4], (DEPTH, PLE_DIM, D_MODEL), PLE_DIM),
        "ev_w_in": nrm(ks[5], (n_even, D_MODEL, sum(EVEN_WIDTHS)), D_MODEL),
        "ev_pool_w": nrm(ks[6], (n_even, N_POOL_GROUPS, POOL_GC, POOL_GC), POOL_GC),
        "ev_pool_scale": gain(ks[7], (n_even, W_A)),
        "ev_q_norm": gain(ks[8], (n_even, DK_B)),
        "ev_k_norm": gain(ks[9], (n_even, DK_B)),
        "ev_lambda": 0.1 * jax.random.normal(ks[10], (n_even, 4, DK_B), f32),
        "ev_subln": gain(ks[11], (n_even, DV_B)),
        "ev_w_out": nrm(ks[12], (n_even, MIX_WIDTH, D_MODEL), MIX_WIDTH),
        "od_w_in": nrm(ks[13], (n_odd, D_MODEL, sum(ODD_WIDTHS)), D_MODEL),
        "od_q_a_norm": gain(ks[14], (n_odd, Q_LORA)),
        "od_w_uq": nrm(ks[15], (n_odd, Q_LORA, H_C * DQK_C), Q_LORA),
        "od_kv_a_norm": gain(ks[16], (n_odd, KV_LORA)),
        "od_w_ukv": nrm(ks[17], (n_odd, KV_LORA, H_C * (D_NOPE + DV_C)), KV_LORA),
        "od_q_norm": gain(ks[18], (n_odd, DQK_C)),
        "od_k_norm": gain(ks[19], (n_odd, DQK_C)),
        "od_conv_w": nrm(ks[20], (n_odd, CONV_K, CONV_CH), CONV_K),
        "od_a_log": jnp.log(jax.random.uniform(ks[21], (n_odd, H_D), f32, 1.0, 16.0)),
        "od_dt_bias": dt + jnp.log(-jnp.expm1(-dt)),
        "od_o_norm": gain(ks[22], (n_odd, DV_D)),
        "od_w_out": nrm(ks[23], (n_odd, MIX_WIDTH, D_MODEL), MIX_WIDTH),
    }

def first_block(x, p, positions, norm_g, ple_w_gate, ple_w_proj,
              ev_w_in, ev_pool_w, ev_pool_scale, ev_q_norm, ev_k_norm, ev_lambda, ev_subln, ev_w_out,
              od_w_in, od_q_a_norm, od_w_uq, od_kv_a_norm, od_w_ukv, od_q_norm, od_k_norm,
              od_conv_w, od_a_log, od_dt_bias, od_o_norm, od_w_out):
    h = x
    for i in range(DEPTH):
        hn = rmsnorm(h, norm_g[i])
        j = i // 2
        if i % 2 == 0:
            m = even_layer(hn, i, positions, ev_w_in[j], ev_pool_w[j], ev_pool_scale[j],
                           ev_q_norm[j], ev_k_norm[j], ev_lambda[j], ev_subln[j], ev_w_out[j])
        else:
            m = odd_layer(hn, positions, od_w_in[j], od_q_a_norm[j], od_w_uq[j], od_kv_a_norm[j],
                          od_w_ukv[j], od_q_norm[j], od_k_norm[j], od_conv_w[j], od_a_log[j],
                          od_dt_bias[j], od_o_norm[j], od_w_out[j])
        h = h + m
        h = h + jax.nn.sigmoid(h @ ple_w_gate[i]) * (p[i] @ ple_w_proj[i])
    return h


N_MIXERS = 2
N_META = 16
BLOCK = 128
NEG_INF = -1e30

FOX_HEADS = 16
FOX_HEAD_DIM = D_MODEL // FOX_HEADS
FOX_IN = 3 * D_MODEL + FOX_HEADS
FOX_FORGET_BIAS = 2.0

HG_HEADS = 8
HG_KEY_DIM = 128
HG_VAL_DIM = D_MODEL // HG_HEADS
HG_KEY_TOTAL = HG_HEADS * HG_KEY_DIM
HG_IN = 2 * HG_KEY_TOTAL + 2 * D_MODEL

N_GROUPS = 4
EXPERTS_PER_GROUP = 8
N_EXPERTS = N_GROUPS * EXPERTS_PER_GROUP
TOP_K = 2
D_EXPERT = D_MODEL // 2
EXPERT_ROW_BLOCK = 128


def rms_norm(x, gain):
    xf = x.astype(jnp.float32)
    y = xf * lax.rsqrt(jnp.mean(xf * xf, axis=-1, keepdims=True) + EPS)
    return (y * gain.astype(jnp.float32)).astype(x.dtype)

def front_pad(t, pad):
    widths = [(0, 0)] * t.ndim
    widths[1] = (pad, 0)
    return jnp.pad(t, widths)

def fox_attention(h, w_in, b_f, g_q, g_k, w_out):
    bsz, length, _ = h.shape
    q, k, v, f_logit = jnp.split(h @ w_in, [D_MODEL, 2 * D_MODEL, 3 * D_MODEL], axis=-1)
    q = rms_norm(q.reshape(bsz, length, FOX_HEADS, FOX_HEAD_DIM), g_q)
    k = rms_norm(k.reshape(bsz, length, FOX_HEADS, FOX_HEAD_DIM), g_k)
    v = v.reshape(bsz, length, FOX_HEADS, FOX_HEAD_DIM)
    log_f = jax.nn.log_sigmoid(f_logit.astype(jnp.float32) + b_f.astype(jnp.float32))
    pad = (-length) % BLOCK
    q, k, v, log_f = (front_pad(t, pad) for t in (q, k, v, log_f))
    lp = length + pad
    n_blk = lp // BLOCK
    cum = jnp.cumsum(log_f, axis=1).transpose(0, 2, 1)
    kh = k.transpose(0, 2, 1, 3)
    vh = v.transpose(0, 2, 1, 3)
    qb = q.reshape(bsz, n_blk, BLOCK, FOX_HEADS, FOX_HEAD_DIM).transpose(1, 0, 3, 2, 4)
    cb = cum.reshape(bsz, FOX_HEADS, n_blk, BLOCK).transpose(2, 0, 1, 3)
    key_pos = jnp.arange(lp)
    key_ok = key_pos >= pad
    scale = FOX_HEAD_DIM ** -0.5

    def attend(args):
        qi, ci, bi = args
        s = jnp.einsum('bhqd,bhkd->bhqk', qi, kh).astype(jnp.float32) * scale
        s = s + ci[..., :, None] - cum[:, :, None, :]
        q_pos = bi * BLOCK + jnp.arange(BLOCK)
        mask = (key_pos[None, :] <= q_pos[:, None]) & key_ok[None, :]
        p = jax.nn.softmax(jnp.where(mask, s, NEG_INF), axis=-1)
        return jnp.einsum('bhqk,bhkd->bhqd', p.astype(vh.dtype), vh)

    o = lax.map(attend, (qb, cb, jnp.arange(n_blk)))
    o = o.transpose(1, 0, 3, 2, 4).reshape(bsz, lp, D_MODEL)[:, pad:]
    return o @ w_out

def hgrn_lower_bounds(lb_logits):
    p = jax.nn.softmax(lb_logits.astype(jnp.float32), axis=0)
    cum = jnp.cumsum(p, axis=0)
    return cum - cum[:1]

def hgrn2_recurrence(h, w_in, b_f, lower_bound, g_o, w_out):
    bsz, length, _ = h.shape
    q, f_logit, v, g = jnp.split(
        h @ w_in, [HG_KEY_TOTAL, 2 * HG_KEY_TOTAL, 2 * HG_KEY_TOTAL + D_MODEL], axis=-1)
    f = lower_bound + (1.0 - lower_bound) * jax.nn.sigmoid(
        f_logit.astype(jnp.float32) + b_f.astype(jnp.float32))
    log_f = jnp.log(f)
    k = 1.0 - f
    q = jax.nn.silu(q.astype(jnp.float32))
    v = v.astype(jnp.float32)
    pad = (-length) % BLOCK
    lp = length + pad
    n_chk = lp // BLOCK

    def to_chunks(t, d):
        t = front_pad(t, pad).reshape(bsz, n_chk, BLOCK, HG_HEADS, d)
        return t.transpose(1, 0, 3, 2, 4)

    qc = to_chunks(q, HG_KEY_DIM)
    kc = to_chunks(k, HG_KEY_DIM)
    vc = to_chunks(v, HG_VAL_DIM)
    lc = to_chunks(log_f, HG_KEY_DIM)
    causal = jnp.tril(jnp.ones((BLOCK, BLOCK), dtype=bool))

    def step(state, args):
        qi, ki, vi, li = args
        b = jnp.cumsum(li, axis=2)
        o_inter = jnp.einsum('bhtk,bhkv->bhtv', qi * jnp.exp(b), state)
        diff = b[:, :, :, None, :] - b[:, :, None, :, :]
        decay = jnp.exp(jnp.where(causal[:, :, None], diff, -jnp.inf))
        scores = jnp.einsum('bhtk,bhsk,bhtsk->bhts', qi, ki, decay)
        o_intra = jnp.einsum('bhts,bhsv->bhtv', scores, vi)
        b_end = b[:, :, -1:, :]
        state = (jnp.exp(b_end[:, :, 0, :])[..., None] * state
                 + jnp.einsum('bhsk,bhsv->bhkv', ki * jnp.exp(b_end - b), vi))
        return state, o_inter + o_intra

    s0 = jnp.zeros((bsz, HG_HEADS, HG_KEY_DIM, HG_VAL_DIM), jnp.float32)
    _, o = lax.scan(step, s0, (qc, kc, vc, lc))
    o = o.transpose(1, 0, 3, 2, 4).reshape(bsz, lp, HG_HEADS, HG_VAL_DIM)[:, pad:]
    o = rms_norm(o, g_o).reshape(bsz, length, D_MODEL) * jax.nn.silu(g.astype(jnp.float32))
    return o.astype(h.dtype) @ w_out

def hier_moe(h, w_grp, b_grp, w_rt, b_rt, w_up, w_down):
    bsz, length, dm = h.shape
    n_tok = bsz * length
    n_asg = n_tok * TOP_K
    xt = h.reshape(n_tok, dm)
    g_prob = jax.nn.softmax((xt @ w_grp).astype(jnp.float32) + b_grp.astype(jnp.float32), axis=-1)
    g_gate, g_idx = lax.top_k(g_prob, 1)
    e_logit = ((xt @ w_rt).astype(jnp.float32) + b_rt.astype(jnp.float32)).reshape(
        n_tok, N_GROUPS, EXPERTS_PER_GROUP)
    e_logit = jnp.take_along_axis(e_logit, g_idx[:, :, None], axis=1)[:, 0]
    e_val, e_idx = lax.top_k(e_logit, TOP_K)
    gate = jax.nn.softmax(e_val, axis=-1) * g_gate
    expert = (g_idx * EXPERTS_PER_GROUP + e_idx).reshape(-1)
    order = jnp.argsort(expert)
    se = expert[order]
    tok = order // TOP_K
    w_sorted = gate.reshape(-1)[order]
    counts = jnp.bincount(expert, length=N_EXPERTS)
    padded = (counts + EXPERT_ROW_BLOCK - 1) // EXPERT_ROW_BLOCK * EXPERT_ROW_BLOCK
    start = jnp.cumsum(counts) - counts
    pend = jnp.cumsum(padded)
    pstart = pend - padded
    dest = pstart[se] + jnp.arange(n_asg) - start[se]
    n_blocks = (n_asg + N_EXPERTS * (EXPERT_ROW_BLOCK - 1) + EXPERT_ROW_BLOCK - 1) // EXPERT_ROW_BLOCK
    rows = n_blocks * EXPERT_ROW_BLOCK
    x_pad = jnp.zeros((rows, dm), h.dtype).at[dest].set(xt[tok])
    block_expert = jnp.minimum(
        jnp.searchsorted(pend, jnp.arange(n_blocks) * EXPERT_ROW_BLOCK, side='right'), N_EXPERTS - 1)

    def expert_block(args):
        xb, e = args
        gate_up = xb @ w_up[e]
        a, u = jnp.split(gate_up, 2, axis=-1)
        return (jax.nn.silu(a) * u) @ w_down[e]

    y_pad = lax.map(expert_block, (x_pad.reshape(n_blocks, EXPERT_ROW_BLOCK, dm), block_expert))
    y = y_pad.reshape(rows, dm)[dest] * w_sorted[:, None].astype(h.dtype)
    return jnp.zeros_like(xt).at[tok].add(y).reshape(bsz, length, dm)

def second_inputs(seed: int = 0) -> dict:
    key = jax.random.key(seed)
    ks = jax.random.split(key, 24)
    n_fox = (DEPTH + N_MIXERS - 1) // N_MIXERS
    n_hg = DEPTH // N_MIXERS
    out_scale = (2 * DEPTH) ** -0.5

    def nrm(k, shape, scale):
        return jax.random.normal(k, shape, jnp.float32) * scale

    def gain(k, shape):
        return 1.0 + nrm(k, shape, 0.02)

    return {
        'x': nrm(ks[0], (BATCH, SEQ, D_MODEL), 1.0),
        'meta_tokens': nrm(ks[1], (N_META, D_MODEL), 1.0),
        'fox_norm': gain(ks[2], (n_fox, D_MODEL)),
        'fox_w_in': nrm(ks[3], (n_fox, D_MODEL, FOX_IN), D_MODEL ** -0.5),
        'fox_b_f': FOX_FORGET_BIAS + nrm(ks[4], (n_fox, FOX_HEADS), 0.1),
        'fox_q_norm': gain(ks[5], (n_fox, FOX_HEAD_DIM)),
        'fox_k_norm': gain(ks[6], (n_fox, FOX_HEAD_DIM)),
        'fox_w_out': nrm(ks[7], (n_fox, D_MODEL, D_MODEL), D_MODEL ** -0.5 * out_scale),
        'hg_norm': gain(ks[8], (n_hg, D_MODEL)),
        'hg_w_in': nrm(ks[9], (n_hg, D_MODEL, HG_IN), D_MODEL ** -0.5),
        'hg_b_f': nrm(ks[10], (n_hg, HG_KEY_TOTAL), 0.02),
        'hg_lb_logits': nrm(ks[11], (DEPTH, HG_KEY_TOTAL), 0.5),
        'hg_o_norm': gain(ks[12], (n_hg, HG_VAL_DIM)),
        'hg_w_out': nrm(ks[13], (n_hg, D_MODEL, D_MODEL), D_MODEL ** -0.5 * out_scale),
        'moe_norm': gain(ks[14], (DEPTH, D_MODEL)),
        'moe_w_grp': nrm(ks[15], (DEPTH, D_MODEL, N_GROUPS), D_MODEL ** -0.5),
        'moe_b_grp': nrm(ks[16], (DEPTH, N_GROUPS), 0.01),
        'moe_w_rt': nrm(ks[17], (DEPTH, D_MODEL, N_EXPERTS), D_MODEL ** -0.5),
        'moe_b_rt': nrm(ks[18], (DEPTH, N_EXPERTS), 0.01),
        'moe_w_up': nrm(ks[19], (DEPTH, N_EXPERTS, D_MODEL, 2 * D_EXPERT), D_MODEL ** -0.5),
        'moe_w_down': nrm(ks[20], (DEPTH, N_EXPERTS, D_EXPERT, D_MODEL), D_EXPERT ** -0.5 * out_scale),
    }

def second_block(x, meta_tokens, fox_norm, fox_w_in, fox_b_f, fox_q_norm, fox_k_norm, fox_w_out,
              hg_norm, hg_w_in, hg_b_f, hg_lb_logits, hg_o_norm, hg_w_out,
              moe_norm, moe_w_grp, moe_b_grp, moe_w_rt, moe_b_rt, moe_w_up, moe_w_down):
    bsz = x.shape[0]
    meta = jnp.broadcast_to(meta_tokens[None].astype(x.dtype), (bsz, N_META, D_MODEL))
    h = jnp.concatenate([meta, x], axis=1)
    lower_bounds = hgrn_lower_bounds(hg_lb_logits)
    for i in range(DEPTH):
        j = i // N_MIXERS
        if i % N_MIXERS == 0:
            h = h + fox_attention(rms_norm(h, fox_norm[j]), fox_w_in[j], fox_b_f[j],
                                  fox_q_norm[j], fox_k_norm[j], fox_w_out[j])
        else:
            h = h + hgrn2_recurrence(rms_norm(h, hg_norm[j]), hg_w_in[j], hg_b_f[j],
                                     lower_bounds[i], hg_o_norm[j], hg_w_out[j])
        h = h + hier_moe(rms_norm(h, moe_norm[i]), moe_w_grp[i], moe_b_grp[i],
                         moe_w_rt[i], moe_b_rt[i], moe_w_up[i], moe_w_down[i])
    return h[:, N_META:]


def setup_inputs(seed=0):
    out = dict(first_inputs(seed))
    for name, value in second_inputs(seed + 1).items():
        if name != "x":
            out[name + "_2"] = value
    return out


def reference(
    x, p, positions, norm_g, ple_w_gate, ple_w_proj, ev_w_in, ev_pool_w, ev_pool_scale,
    ev_q_norm, ev_k_norm, ev_lambda, ev_subln, ev_w_out, od_w_in, od_q_a_norm, od_w_uq,
    od_kv_a_norm, od_w_ukv, od_q_norm, od_k_norm, od_conv_w, od_a_log, od_dt_bias, od_o_norm,
    od_w_out, meta_tokens_2, fox_norm_2, fox_w_in_2, fox_b_f_2, fox_q_norm_2, fox_k_norm_2,
    fox_w_out_2, hg_norm_2, hg_w_in_2, hg_b_f_2, hg_lb_logits_2, hg_o_norm_2, hg_w_out_2,
    moe_norm_2, moe_w_grp_2, moe_b_grp_2, moe_w_rt_2, moe_b_rt_2, moe_w_up_2, moe_w_down_2,
):
    x = first_block(
        x, p, positions, norm_g, ple_w_gate, ple_w_proj, ev_w_in, ev_pool_w, ev_pool_scale,
        ev_q_norm, ev_k_norm, ev_lambda, ev_subln, ev_w_out, od_w_in, od_q_a_norm, od_w_uq,
        od_kv_a_norm, od_w_ukv, od_q_norm, od_k_norm, od_conv_w, od_a_log, od_dt_bias,
        od_o_norm, od_w_out,
    )
    return second_block(
        x, meta_tokens_2, fox_norm_2, fox_w_in_2, fox_b_f_2, fox_q_norm_2, fox_k_norm_2,
        fox_w_out_2, hg_norm_2, hg_w_in_2, hg_b_f_2, hg_lb_logits_2, hg_o_norm_2, hg_w_out_2,
        moe_norm_2, moe_w_grp_2, moe_b_grp_2, moe_w_rt_2, moe_b_rt_2, moe_w_up_2, moe_w_down_2,
    )


_drawn_inputs = setup_inputs


def setup_inputs(seed=0):
    import zlib

    import numpy as np

    out = dict(_drawn_inputs(seed))
    spreads = {}
    factors = {'ev_pool_scale': 7.374,
     'ev_q_norm': 5.483,
     'ev_k_norm': 5.06,
     'ev_subln': 4.211,
     'od_q_a_norm': 8.0,
     'od_kv_a_norm': 8.0,
     'od_q_norm': 8.0,
     'od_k_norm': 8.0,
     'od_a_log': 2.766,
     'od_o_norm': 7.001,
     'meta_tokens_2': 3.446,
     'fox_norm_2': 6.846,
     'fox_b_f_2': 4.09,
     'fox_q_norm_2': 6.543,
     'fox_k_norm_2': 8.0,
     'hg_norm_2': 5.93,
     'hg_b_f_2': 29.049,
     'hg_lb_logits_2': 4.099,
     'hg_o_norm_2': 8.0,
     'moe_norm_2': 3.715,
     'moe_b_grp_2': 8.0,
     'moe_b_rt_2': 5.928}
    for name, (base, spread) in spreads.items():
        noise = np.random.default_rng([zlib.crc32(name.encode()), seed]).standard_normal(out[name].shape)
        drawn = base * np.exp(spread * noise) if base else spread * noise
        out[name] = jnp.asarray(drawn.astype(out[name].dtype))
    for name, factor in factors.items():
        out[name] = (out[name] * factor).astype(out[name].dtype)
    return out
```

```python
import math

import concourse.bass as bass
import numpy as np
from concourse import mybir
from contextlib import ExitStack

F32 = mybir.dt.float32
I32 = mybir.dt.int32
ALU = mybir.AluOpType
ACT = mybir.ActivationFunctionType
AX = mybir.AxisListType

P = 128
D = 1024
KD = D // P
SEQ, META = 512, 16
TOKENS = SEQ + META
EPS = 1e-6
TILES = [(0, META)] + [(META + P * i, P) for i in range(SEQ // P)]
XT = [1, 2, 3, 4]
ALLT = [0, 1, 2, 3, 4]
NEG = -1e30
TWO_PI = 2 * math.pi

HB, DKB, DVB, WA, WB = 6, 64, 128, 256, 768
HC, DNOPE, DROPE = 4, 128, 64
DQK = DNOPE + DROPE
HD = 4
FH, FD = 16, 64
HG = 8
NEXP, GROUPS, EPG, DFF = 32, 4, 8, 512
ROWS = 64
OVER = 16
SLOTS = (NEXP + OVER) * ROWS


def host_constants():
    i = np.arange(P)
    c = {}
    c["identity"] = np.eye(P)
    c["power"] = np.full((P, 1), -0.5)
    c["causal"] = np.where(i[None, :] <= i[:, None], 0.0, NEG)
    c["upto"] = (i[:, None] <= i[None, :])
    c["before"] = (i[:, None] < i[None, :])
    for n in range(7):
        b = 1 << n
        c[f"half{n}"] = (i[:, None] // (2 * b) == i[None, :] // (2 * b)) & (i[:, None] // b % 2 == 0) & (i[None, :] // b % 2 == 1)
    c["later"] = np.where(i[None, :] >= i[:, None], 0.0, NEG)
    c["freq"] = np.tile(np.concatenate([500000.0 ** (-np.arange(8) * 2.0 / 16), 10000.0 ** (-np.arange(32) * 2.0 / 64)]), (P, 1))
    t = np.arange(SEQ)
    c["pool"] = np.concatenate([np.repeat((1.0 / np.minimum(t + 1, w))[None], 64, 0) for w in (2, 4)] + [np.repeat((1.0 / np.minimum(t + 1, w))[None], 64, 0) for w in (8, 16)], 0).reshape(2, P, SEQ).transpose(1, 0, 2).reshape(P, 2 * SEQ)
    c["iota"] = np.tile(np.arange(NEXP, dtype=np.float64), (P, 1))
    c["steps"] = np.tile(ROWS * np.arange(1, 9, dtype=np.float64), (P, 1))
    c["overs"] = np.tile(np.arange(OVER, dtype=np.float64), (P, 1))
    start = np.ones(TOKENS); start[[a for a, _ in TILES]] = 0
    c["carry"] = np.tile(start, (P, 1))
    at, out = {}, []
    n = 0
    for k, v in c.items():
        at[k] = (n, v.shape[1])
        n += v.shape[1]
        out.append(v.astype(np.float32))
    return at, np.ascontiguousarray(np.concatenate(out, 1))


class Signal:

    def __init__(self, sem):
        self.sem, self.base, self.count = sem, 0, 0

    def up(self, step=1):
        self.count += step
        return self.sem, step

    def at(self, n):
        return self.sem, self.base + n

    def last(self):
        return self.at(self.count)


class Program:

    def __init__(self, nc, ctx, a, const_at):
        self.nc, self.ctx, self.a, self.const_at = nc, ctx, a, const_at
        self.signals = {}
        sb = lambda name, shape, dt=F32: ctx.enter_context(nc.sbuf_tensor(name, shape, dt))
        self.ring = sb("weight_ring", [P, 4, 4096])
        self.hT = sb("hidden_T", [P, KD, TOKENS])
        self.h = sb("hidden", [P, 5, D])
        self.const = sb("constants", [P, sum(w for _, w in const_at.values())])
        self.small = sb("small", [P, 1024])
        self.arena_cols = 23200
        self.arena = sb("arena", [P, self.arena_cols])
        self.psum = ctx.enter_context(nc.psum_tensor("psum", [P, 8, 512], F32))
        self.top = 0
        self.stop = 0
        self.chunks = []
        self.fed = 0
        self.ring_in = [self.sem(f"weights_in_{n}") for n in range(4)]
        self.used = {}
        self.over_sems, self.gather_sems, self.gathers = [], [], 0

    def sem(self, name):
        return self.ctx.enter_context(self.nc.semaphore(name))

    def sig(self, *names):
        out = []
        for n in names:
            if n not in self.signals:
                self.signals[n] = Signal(self.sem(n))
            s = self.signals[n]
            s.base += s.count
            s.count = 0
            out.append(s)
        return out if len(out) > 1 else out[0]

    def c(self, name):
        a, w = self.const_at[name]
        return self.const[:, a:a + w]

    def take(self, *shape):
        n = int(np.prod(shape))
        ap = self.arena[:, self.top:self.top + n]
        self.top += n
        assert self.top <= self.arena_cols, (self.top, self.arena_cols)
        if len(shape) == 2:
            ap = ap.rearrange("p (a b) -> p a b", a=shape[0])
        if len(shape) == 3:
            ap = ap.rearrange("p (a b c) -> p a b c", a=shape[0], b=shape[1])
        return ap

    def plan(self, src, kchunks, width):
        self.chunks.append((src, kchunks, width))
        return len(self.chunks) - 1

    def weights(self, n):
        _, k, w = self.chunks[n]
        return self.ring[:, n % 4, 0:k * w].rearrange("p (k w) -> p k w", k=k)

    def weights_wait(self, pe, n):
        pe.wait_ge(self.ring_in[n % 4], 16 * (n // 4 + 1))

    def chunk_used(self, n, signal):
        self.used[n] = (signal.sem, signal.base + signal.count)

    def feed(self, sp, upto):
        upto = min(upto, len(self.chunks))
        while self.fed < upto:
            n = self.fed
            src, k, w = self.chunks[n]
            if n >= 4:
                sp.wait_ge(*self.used[n - 4])
            sp.dma_start(self.weights(n), src.rearrange("(k p) w -> p k w", p=P)).then_inc(self.ring_in[n % 4], 16)
            self.fed += 1


def row_of_all(ap1d, n):
    return ap1d.rearrange("(a n) -> a n", a=1).to_broadcast([P, n])


def stage_load(g):
    nc, a = g.nc, g.a
    loaded, angled, sined, chain, zeroed = g.sig("inputs_loaded", "angles_ready", "sines_ready", "vector_step", "meta_rows_zeroed")
    g.x_rows_zeroed = g.sig("expert_rows_zeroed")
    g.sin = g.small[:, 0:160].rearrange("p (t f) -> p t f", t=4)
    g.cos = g.small[:, 160:320].rearrange("p (t f) -> p t f", t=4)
    mark = g.top
    pos_i = g.take(4).bitcast(I32)
    pos = g.take(4)
    ang, turns, red = g.take(4, 40), g.take(2, 160), g.take(2, 160)
    with nc.Block() as block:
        @block.sync
        def _(sp):
            sp.dma_start(g.const[:, :], a["constants"]).then_inc(*loaded.up(16))
            sp.dma_start(pos_i, a["positions"].rearrange("b (t p) -> p (b t)", p=P), allow_slow_non_contiguous=True).then_inc(*loaded.up(16))
            sp.dma_start(g.h[:, 1:5, :], a["x"].rearrange("b (t p) d -> p (b t) d", p=P)).then_inc(*loaded.up(16))
            sp.wait_ge(*zeroed.at(1))
            sp.dma_start(g.h[0:META, 0, :], a["meta_tokens_2"]).then_inc(*loaded.up(16))
            g.feed(sp, 3)
            sp.wait_ge(*loaded.at(64))

        @block.gpsimd
        def _(pool):
            nc.gpsimd.memset(g.h[:, 0, :], 0.0).then_inc(*zeroed.up())
            nc.gpsimd.memset(g.small[:, 512:1024], 0.0).then_inc(*zeroed.up())

        @block.vector
        def _(dve):
            dve.wait_ge(*loaded.at(64))
            nc.vector.tensor_copy(pos, pos_i).then_inc(*chain.up())
            dve.wait_ge(*chain.last())
            nc.vector.tensor_tensor(ang, pos.unsqueeze(2).to_broadcast([P, 4, 40]), g.c("freq").unsqueeze(1).to_broadcast([P, 4, 40]), ALU.mult).then_inc(*chain.up())
            dve.wait_ge(*chain.last())
            flat = ang.rearrange("p t f -> p (t f)")
            magic = 1.5 * 2.0 ** 23
            c1 = 6.28125
            c2 = float(np.float32(TWO_PI - c1))
            c3 = float(TWO_PI - c1 - c2)
            for n, quarter in enumerate((0.0, 0.25)):
                nc.vector.tensor_scalar(turns[:, n, :], flat, 1 / TWO_PI, quarter, ALU.mult, ALU.add).then_inc(*chain.up())
                dve.wait_ge(*chain.last())
                nc.vector.tensor_scalar(turns[:, n, :], turns[:, n, :], magic, magic, ALU.add, ALU.subtract).then_inc(*chain.up())
                dve.wait_ge(*chain.last())
                nc.vector.scalar_tensor_tensor(red[:, n, :], turns[:, n, :], -c1, flat, ALU.mult, ALU.add).then_inc(*chain.up())
                dve.wait_ge(*chain.last())
                nc.vector.scalar_tensor_tensor(red[:, n, :], turns[:, n, :], -c2, red[:, n, :], ALU.mult, ALU.add).then_inc(*chain.up())
                dve.wait_ge(*chain.last())
                nc.vector.scalar_tensor_tensor(red[:, n, :], turns[:, n, :], -c3, red[:, n, :], ALU.mult, ALU.add).then_inc(*chain.up())
                dve.wait_ge(*chain.last())
                nc.vector.tensor_scalar(red[:, n, :], red[:, n, :], quarter * TWO_PI, 3.1415925, ALU.add, ALU.min).then_inc(*chain.up())
                dve.wait_ge(*chain.last())
                nc.vector.tensor_scalar(red[:, n, :], red[:, n, :], -3.1415925, None, ALU.max).then_inc(*angled.up())

        @block.scalar
        def _(act):
            act.wait_ge(*zeroed.at(2))
            rows = a["x_rows"].rearrange("(p n) (two c) -> p (n two) c", p=P, c=512)
            act.dma_start(rows, g.small[:, 512:1024].unsqueeze(1).to_broadcast([P, SLOTS // P * 2, 512])).then_inc(*g.x_rows_zeroed.up(16))
            rows = a["y_rows"][NEXP * ROWS:].rearrange("(p n) (two c) -> p (n two) c", p=P, c=512)
            act.dma_start(rows, g.small[:, 512:1024].unsqueeze(1).to_broadcast([P, OVER * ROWS // P * 2, 512])).then_inc(*g.x_rows_zeroed.up(16))
            for n, dst in enumerate((g.sin, g.cos)):
                act.wait_ge(*angled.at(n + 1))
                nc.scalar.activation(dst.rearrange("p t f -> p (t f)"), red[:, n, :], ACT.Sin).then_inc(*sined.up())
            act.wait_ge(*sined.at(2))
    g.top = mark


def inverse_root(g, pool, out, sums, scale, chain, done, times=None):
    g.nc.gpsimd.tensor_scalar(out, sums, scale, EPS, ALU.mult, ALU.add).then_inc(*chain.up())
    pool.wait_ge(*chain.last())
    power = g.c("power")[0:out.shape[0], 0:1].to_broadcast(list(out.shape))
    if times is None:
        g.nc.gpsimd.tensor_tensor(out, out, power, ALU.pow).then_inc(*done.up())
    else:
        g.nc.gpsimd.tensor_tensor(out, out, power, ALU.pow).then_inc(*chain.up())
        pool.wait_ge(*chain.last())
        g.nc.gpsimd.tensor_scalar(out, out, times, None, ALU.mult).then_inc(*done.up())


def stage_norm(g, tiles, gain_dram, ring_upto, keep=None):
    nc = g.nc
    mark = g.top
    loaded, squared, rooted, scaled, transposed, moved, chain = g.sig("gain_loaded", "rows_squared", "norm_ready", "rows_scaled", "rows_transposed", "transposed_moved", "gpsimd_step")
    gain = g.take(KD)
    sq = g.take(2, D)
    rows = keep if keep is not None else g.take(2, D)
    nrows = 5 if keep is not None else 2
    ss, rs = g.take(5), g.take(5)
    normed = gain_dram is not None
    with nc.Block() as block:
        @block.sync
        def _(sp):
            if normed:
                sp.dma_start(gain, gain_dram.rearrange("(k p) -> p k", p=P), allow_slow_non_contiguous=True).then_inc(*loaded.up(16))
            g.feed(sp, ring_upto)
            if normed:
                sp.wait_ge(*loaded.at(16))

        @block.scalar
        def _(act):
            if normed:
                for i, t in enumerate(tiles):
                    n = TILES[t][1]
                    if i - 1 > 0:
                        act.wait_ge(*squared.at(i - 1))
                    nc.scalar.activation(sq[0:n, i % 2, :], g.h[0:n, t, :], ACT.Square, accum_out=ss[0:n, i:i + 1]).then_inc(*squared.up())
                for i, t in enumerate(tiles):
                    n = TILES[t][1]
                    act.wait_ge(*rooted.at(i + 1))
                    if nrows == 2:
                        if i - 1 > 0:
                            act.wait_ge(*transposed.at(i - 1))
                    nc.scalar.activation(rows[0:n, i % nrows, :], g.h[0:n, t, :], ACT.Copy, scale=rs[0:n, i:i + 1]).then_inc(*scaled.up())

        @block.vector
        def _(dve):
            if normed:
                dve.wait_ge(*loaded.at(16))
            for i, t in enumerate(tiles):
                a, n = TILES[t]
                for half in range(2):
                    dve.wait_ge(*transposed.at(i + 1))
                    src = g.psum[:, 2 * (i % 2) + half, :].rearrange("p (c n) -> p c n", c=4)[:, :, 0:n]
                    dst = g.hT[:, 4 * half:4 * half + 4, a:a + n]
                    if normed:
                        nc.vector.tensor_tensor(dst, src, gain[:, 4 * half:4 * half + 4].unsqueeze(2).to_broadcast([P, 4, n]), ALU.mult).then_inc(*moved.up())
                    else:
                        nc.vector.tensor_copy(dst, src).then_inc(*moved.up())

        @block.gpsimd
        def _(pool):
            if normed:
                for i, t in enumerate(tiles):
                    n = TILES[t][1]
                    pool.wait_ge(*squared.at(i + 1))
                    inverse_root(g, pool, rs[0:n, i:i + 1], ss[0:n, i:i + 1], 1.0 / D, chain, rooted)

        @block.tensor
        def _(pe):
            for i, t in enumerate(tiles):
                n = TILES[t][1]
                if normed:
                    pe.wait_ge(*scaled.at(i + 1))
                if 2 * (i - 1) > 0:
                    pe.wait_ge(*moved.at(2 * (i - 1)))
                for c in range(KD):
                    src = rows[0:n, i % nrows, c * P:(c + 1) * P] if normed else g.h[0:n, t, c * P:(c + 1) * P]
                    last = nc.tensor.transpose(g.psum[:, 2 * (i % 2) + c // 4, (c % 4) * P:(c % 4) * P + n], src, g.c("identity")[0:n, 0:n])
                last.then_inc(*transposed.up())
    g.top = mark


def products(nc, out, left, right):
    for i, (l, r) in enumerate(zip(left, right)):
        last = nc.tensor.matmul(out, l, r, start=i == 0, stop=i == len(left) - 1)
    return last


def rows_by_weights(g, pe, out, t, chunk, kchunks=KD, src=None):
    a, n = TILES[t]
    src = g.hT if src is None else src
    w = g.weights(chunk)
    return products(g.nc, out, [src[:, k, a:a + n] for k in range(kchunks)], [w[:, k, :] for k in range(kchunks)])


def stage_out(g, tiles, chunks, ring_upto):
    nc = g.nc
    ready, added = g.sig("product_ready", "residual_added")
    with nc.Block() as block:
        @block.tensor
        def _(pe):
            u = 0
            for half, chunk in enumerate(chunks):
                g.weights_wait(pe, chunk)
                for t in tiles:
                    n = TILES[t][1]
                    if u - 3 > 0:
                        pe.wait_ge(*added.at(u - 3))
                    last = rows_by_weights(g, pe, g.psum[0:n, u % 4, :], t, chunk)
                    last.then_inc(*ready.up())
                    u += 1
                g.chunk_used(chunk, ready)

        @block.sync
        def _(sp):
            g.feed(sp, ring_upto)

        @block.vector
        def _(dve):
            u = 0
            for half in range(2):
                for t in tiles:
                    n = TILES[t][1]
                    dve.wait_ge(*ready.at(u + 1))
                    dst = g.h[0:n, t, 512 * half:512 * half + 512]
                    nc.vector.tensor_tensor(dst, dst, g.psum[0:n, u % 4, :], ALU.add).then_inc(*added.up())
                    u += 1


def stage_ple(g, layer, chunks, proj_chunk, ring_upto):
    nc = g.nc
    mark = g.top
    p_in, ready, gated, multiplied, added, proj_ready = g.sig("ple_input_loaded", "product_ready", "gate_ready", "gate_applied", "residual_added", "ple_product_ready")
    pT = g.take(2, SEQ)
    gate = g.take(2, 512)
    gate2 = g.take(2, 512)
    with nc.Block() as block:
        @block.tensor
        def _(pe):
            u = 0
            pe.wait_ge(*p_in.at(16))
            g.weights_wait(pe, proj_chunk)
            for half, chunk in enumerate(chunks):
                g.weights_wait(pe, chunk)
                for t in XT:
                    a, n = TILES[t]
                    if u - 1 > 0:
                        pe.wait_ge(*gated.at(u - 1))
                    rows_by_weights(g, pe, g.psum[:, u % 2, :], t, chunk).then_inc(*ready.up())
                    if u - 1 > 0:
                        pe.wait_ge(*multiplied.at(u - 1))
                    w = g.weights(proj_chunk)
                    products(nc, g.psum[:, 2 + u % 2, :], [pT[:, k, a - META:a - META + n] for k in range(2)], [w[:, k, 512 * half:512 * half + 512] for k in range(2)]).then_inc(*proj_ready.up())
                    u += 1
                g.chunk_used(chunk, ready)
            g.chunk_used(proj_chunk, proj_ready)

        @block.sync
        def _(sp):
            sp.dma_start(pT, g.a["p_T"][layer].rearrange("(k p) t -> p k t", p=P)).then_inc(*p_in.up(16))
            g.feed(sp, ring_upto)

        @block.scalar
        def _(act):
            for u in range(8):
                act.wait_ge(*ready.at(u + 1))
                if u - 1 > 0:
                    act.wait_ge(*multiplied.at(u - 1))
                nc.scalar.activation(gate[:, u % 2, :], g.psum[:, u % 2, :], ACT.Sigmoid).then_inc(*gated.up())

        @block.vector
        def _(dve):
            for u in range(8):
                dve.wait_ge(*gated.at(u + 1))
                dve.wait_ge(*proj_ready.at(u + 1))
                if u - 1 > 0:
                    dve.wait_ge(*added.at(u - 1))
                nc.vector.tensor_tensor(gate2[:, u % 2, :], gate[:, u % 2, :], g.psum[:, 2 + u % 2, :], ALU.mult).then_inc(*multiplied.up())

        @block.gpsimd
        def _(pool):
            for u in range(8):
                half, t = u // 4, XT[u % 4]
                pool.wait_ge(*multiplied.at(u + 1))
                dst = g.h[:, t, 512 * half:512 * half + 512]
                nc.gpsimd.tensor_tensor(dst, dst, gate2[:, u % 2, :], ALU.add).then_inc(*added.up())
    g.top = mark


def stage_even_in(g, chunks, ring_upto):
    nc = g.nc
    ready, freed_a, freed_v, squared, summed, normed, rotated, transposed, placed, chain, gchain, gains_in, rooted = g.sig(
        "product_ready", "bank_read_by_scalar", "bank_read_by_vector", "heads_squared", "heads_summed", "heads_normed",
        "heads_rotated", "heads_transposed", "heads_placed", "vector_step", "gpsimd_step", "gains_loaded", "norm_ready")
    g.e_in = g.take(2, 16 + SEQ)
    g.e_gate = g.take(2, SEQ)
    g.e_qT, g.e_kT = g.take(HB, SEQ), g.take(HB, SEQ)
    g.e_v, g.e_bg = g.take(4, WB), g.take(4, WB)
    mark = g.top
    gain = g.take(2, 64)
    sq, qn = g.take(2, 384), g.take(2, 384)
    ss = g.take(2, 6)
    rope = g.take(4, 48)
    units = [("in" if f < 2 else "ingate", 0, f) for f in range(4)]
    for n, kind in enumerate(["q", "q", "k", "k", "v", "v", "b", "b"]):
        units += [(kind, n + 1, t) for t in XT]
    freed, na, nv = [], 0, 0
    for kind, *_ in units:
        if kind in ("in", "ingate", "b"):
            na += 1
            freed.append((freed_a, na))
        else:
            nv += 1
            freed.append((freed_v, nv))
    qk = [u for u in units if u[0] in "qk"]
    NB = 6
    heads = lambda ap: ap.rearrange("p (g d) -> p g d", d=64)
    with nc.Block() as block:
        @block.tensor
        def _(pe):
            def turn(i):
                pe.wait_ge(*rotated.at(i + 1))
                if i - 1 > 0:
                    pe.wait_ge(*placed.at(i - 1))
                for j in range(3):
                    last = nc.tensor.transpose(g.psum[:, 6 + i % 2, j * P:(j + 1) * P], qn[:, i % 2, j * P:(j + 1) * P], g.c("identity"))
                last.then_inc(*transposed.up())

            i = 0
            for u, (kind, c, x) in enumerate(units):
                if u == 0 or units[u - 1][1] != c:
                    g.weights_wait(pe, chunks[c])
                if u >= NB:
                    pe.wait_ge(*freed[u - NB][0].at(freed[u - NB][1]))
                w = g.weights(chunks[c])
                if c == 0:
                    products(nc, g.psum[:, u % NB, :], [w[:, k, x * P:(x + 1) * P] for k in range(KD)], [g.hT[:, k, META:] for k in range(KD)]).then_inc(*ready.up())
                else:
                    rows_by_weights(g, pe, g.psum[:, u % NB, 0:384], x, chunks[c]).then_inc(*ready.up())
                if u + 1 == len(units) or units[u + 1][1] != c:
                    g.chunk_used(chunks[c], ready)
                if kind in "qk":
                    if i >= 2:
                        turn(i - 2)
                    i += 1
                elif i < len(qk) + 2 and i >= len(qk):
                    turn(i - 2)
                    i += 1

        @block.sync
        def _(sp):
            sp.dma_start(gain[:, 0, :], g.a["ev_q_norm"].to_broadcast([P, 64])).then_inc(*gains_in.up(16))
            sp.dma_start(gain[:, 1, :], g.a["ev_k_norm"].to_broadcast([P, 64])).then_inc(*gains_in.up(16))
            g.feed(sp, ring_upto)

        @block.scalar
        def _(act):
            def place(i):
                kind, c, t = qk[i]
                dst = g.e_qT if kind == "q" else g.e_kT
                half = (c - 1) % 2
                act.wait_ge(*transposed.at(i + 1))
                nc.scalar.activation(dst[:, 3 * half:3 * half + 3, (t - 1) * P:t * P], g.psum[:, 6 + i % 2, 0:384].rearrange("p (h n) -> p h n", h=3), ACT.Copy).then_inc(*placed.up())

            i = 0
            for u, (kind, c, x) in enumerate(units):
                bank = g.psum[:, u % NB, :]
                if kind == "v":
                    if i < len(qk) + 2:
                        place(i - 2)
                        i += 1
                    continue
                act.wait_ge(*ready.at(u + 1))
                if kind == "in":
                    nc.scalar.activation(g.e_in[:, x, 16:], bank, ACT.Copy).then_inc(*freed_a.up())
                elif kind == "ingate":
                    nc.scalar.activation(g.e_gate[:, x - 2, :], bank, ACT.Silu).then_inc(*freed_a.up())
                elif kind == "b":
                    nc.scalar.activation(g.e_bg[:, x - 1, 384 * (c - 7):384 * (c - 6)], bank[:, 0:384], ACT.Silu).then_inc(*freed_a.up())
                else:
                    if i - 1 > 0:
                        act.wait_ge(*summed.at(i - 1))
                    nc.scalar.activation(sq[:, i % 2, :], bank[:, 0:384], ACT.Square).then_inc(*squared.up())
                    if i >= 2:
                        place(i - 2)
                    i += 1

        @block.vector
        def _(dve):
            nc_v = nc.vector
            nc_v.memset(g.e_in[:, :, 0:16], 0.0).then_inc(*chain.up())
            dve.wait_ge(*chain.last())
            dve.wait_ge(*gains_in.at(32))
            i = 0
            for u, (kind, c, x) in enumerate(units):
                bank = g.psum[:, u % NB, 0:384]
                if kind == "v":
                    dve.wait_ge(*ready.at(u + 1))
                    nc_v.tensor_copy(g.e_v[:, x - 1, 384 * (c - 5):384 * (c - 4)], bank).then_inc(*freed_v.up())
                elif kind in "qk":
                    s = ss[:, i % 2, :]
                    dve.wait_ge(*squared.at(i + 1))
                    nc_v.tensor_reduce(s, heads(sq[:, i % 2, :]), AX.X, ALU.add).then_inc(*summed.up())
                    dve.wait_ge(*summed.last())
                    dve.wait_ge(*rooted.at(i + 1))
                    if i - 1 > 0:
                        dve.wait_ge(*transposed.at(i - 1))
                    nc_v.tensor_tensor(heads(qn[:, i % 2, :]), heads(bank), s.unsqueeze(2).to_broadcast([P, 6, 64]), ALU.mult).then_inc(*freed_v.up())
                    dve.wait_ge(*freed_v.last())
                    gn = gain[:, 0 if kind == "q" else 1, :].unsqueeze(1).to_broadcast([P, 6, 64])
                    nc_v.tensor_tensor(heads(qn[:, i % 2, :]), heads(qn[:, i % 2, :]), gn, ALU.mult).then_inc(*normed.up())
                    i += 1

        @block.gpsimd
        def _(pool):
            for i in range(len(qk) + 1):
                if i < len(qk):
                    pool.wait_ge(*summed.at(i + 1))
                    inverse_root(g, pool, ss[:, i % 2, :], ss[:, i % 2, :], 1.0 / 64, gchain, rooted)
                if i == 0:
                    continue
                kind, c, t = qk[i - 1]
                if i > 0:
                    pool.wait_ge(*normed.at(i))
                v = heads(qn[:, (i - 1) % 2, :])
                rotate(g, pool, v[:, :, 0:8], v[:, :, 8:16], g.cos[:, t - 1, 0:8], g.sin[:, t - 1, 0:8], [rope[:, j, :] for j in range(4)], 6, 8, gchain, rotated)
    g.top = mark


def rotate(g, pool, x1, x2, cos, sin, tmp, groups, half, gchain, done):
    op = g.nc.gpsimd.tensor_tensor
    c = cos.unsqueeze(1).to_broadcast([P, groups, half])
    s = sin.unsqueeze(1).to_broadcast([P, groups, half])
    t = [a.rearrange("p (g d) -> p g d", g=groups) for a in tmp]
    if done.count:
        pool.wait_ge(*done.last())
    op(t[0], x1, c, ALU.mult).then_inc(*gchain.up())
    op(t[1], x2, s, ALU.mult).then_inc(*gchain.up())
    op(t[2], x2, c, ALU.mult).then_inc(*gchain.up())
    op(t[3], x1, s, ALU.mult).then_inc(*gchain.up())
    pool.wait_ge(*gchain.last())
    op(x1, t[0], t[1], ALU.subtract).then_inc(*gchain.up())
    pool.wait_ge(*gchain.last())
    op(x2, t[2], t[3], ALU.add).then_inc(*done.up())


def stage_pool(g, ring_upto):
    nc = g.nc
    mark = g.top
    loaded, zeroed, pooled, mixed, chain, done = g.sig("pool_weights_loaded", "pool_weights_zeroed", "pooled", "pool_product_ready", "gpsimd_step", "pool_gated")
    wp = g.take(2, P)
    scale = g.take(2)
    s = g.take(2, 2, 16 + SEQ)
    with nc.Block() as block:
        @block.tensor
        def _(pe):
            pe.wait_ge(*loaded.at(80))
            for n in range(2):
                pe.wait_ge(*pooled.at(n + 1))
                products(nc, g.psum[:, n, :], [wp[:, n, :]], [s[:, n, 0, 16:]]).then_inc(*mixed.up())

        @block.sync
        def _(sp):
            sp.wait_ge(*zeroed.at(1))
            for n in range(2):
                for m in range(2):
                    sp.dma_start(wp[64 * m:64 * m + 64, n, 64 * m:64 * m + 64], g.a["ev_pool_w"][2 * n + m]).then_inc(*loaded.up(16))
            sp.dma_start(scale, g.a["ev_pool_scale"].rearrange("a (n p) -> p (a n)", p=P), allow_slow_non_contiguous=True).then_inc(*loaded.up(16))
            g.feed(sp, ring_upto)

        @block.gpsimd
        def _(pool):
            op = nc.gpsimd.tensor_tensor
            nc.gpsimd.memset(wp, 0.0).then_inc(*zeroed.up())
            nc.gpsimd.memset(s[:, :, :, 0:16], 0.0).then_inc(*chain.up())
            pool.wait_ge(*chain.last())
            for n in range(2):
                src, dst = g.e_in[:, n, :], s[:, n, 0, :]
                op(dst[:, 16:], src[:, 16:], src[:, 15:-1], ALU.add).then_inc(*chain.up())
                pool.wait_ge(*chain.last())
                for m, shift in enumerate((2, 4, 8)):
                    if n == 0 and shift > 2:
                        break
                    lo = 0 if shift == 4 or (shift == 2 and n == 1) else 64
                    a, b = s[:, n, m % 2, :], s[:, n, (m + 1) % 2, :]
                    op(b[lo:, 16:], a[lo:, 16:], a[lo:, 16 - shift:SEQ + 16 - shift], ALU.add).then_inc(*chain.up())
                    pool.wait_ge(*chain.last())
                halves = [(0, 0), (64, 1)] if n == 0 else [(0, 0), (64, 1)]
                for lo, m in halves:
                    r = g.c("pool").rearrange("p (n t) -> p n t", n=2)
                    op(s[lo:lo + 64, n, 0, 16:], s[lo:lo + 64, n, m, 16:], r[lo:lo + 64, n, :], ALU.mult).then_inc(*chain.up())
                    pool.wait_ge(*chain.last())
                op(s[:, n, 0, 16:], s[:, n, 0, 16:], src[:, 16:], ALU.subtract).then_inc(*pooled.up())
                pool.wait_ge(*pooled.last())

        @block.vector
        def _(dve):
            dve.wait_ge(*loaded.at(80))
            for n in range(2):
                dve.wait_ge(*mixed.at(n + 1))
                nc.vector.scalar_tensor_tensor(g.hT[:, n, META:], g.psum[:, n, :], scale[:, n:n + 1], g.e_gate[:, n, :], ALU.mult, ALU.mult).then_inc(*done.up())
    g.top = mark


def stage_even_attention(g, ring_upto):
    nc = g.nc
    mark = g.top
    lam_init = 0.8 - 0.6 * math.exp(-0.3 * 0)
    lam_in, exp_in, exp_out, scored, peaked, expd, combined, turned, placed, mixed, rows_ready, rows_turned, rows_placed, chain, taken, summed, rooted, gchain = g.sig(
        "lambda_loaded", "lambda_sums", "lambda_exps", "scores_ready", "row_peaks", "probabilities", "maps_combined", "heads_transposed", "heads_placed",
        "mixed_ready", "rows_scaled", "rows_transposed", "rows_placed", "vector_step", "mixed_taken", "heads_summed", "norm_ready", "gpsimd_step")
    lv = g.take(4, 64)
    pair = g.take(2, 64)
    lam = g.take(4)
    subln = g.take(DVB)
    peak, total = g.take(4), g.take(2, 2)
    pr = g.take(2, 2, 512)
    am = g.take(2, 512)
    aT = g.take(2, 512)
    o, osq = g.take(2, WB), g.take(WB)
    so = g.take(HB)
    jobs = [(t, h) for t in range(4) for h in range(HB)]
    cw = lambda t: P * (t + 1)
    with nc.Block() as block:
        @block.tensor
        def _(pe):
            def scores(j):
                t, h = jobs[j]
                if j >= 2:
                    if 2 * (j - 1) > 0:
                        pe.wait_ge(*expd.at(2 * (j - 1)))
                for m in range(2):
                    r = slice(64 * m, 64 * m + 64)
                    bank = g.psum[:, 2 * (j % 2) + m, :]
                    nc.tensor.matmul(bank[:, 0:cw(t)], g.e_qT[r, h, t * P:(t + 1) * P], g.e_kT[r, h, 0:cw(t)], start=True, stop=False)
                    nc.tensor.matmul(bank[:, t * P:cw(t)], g.c("identity"), g.c("causal"), start=False, stop=True).then_inc(*scored.up())

            def mix(j):
                t, h = jobs[j]
                pe.wait_ge(*combined.at(j + 1))
                if j - 1 > 0:
                    pe.wait_ge(*placed.at(j - 1))
                for k in range(t + 1):
                    last = nc.tensor.transpose(g.psum[:, 4 + j % 2, k * P:(k + 1) * P], am[:, j % 2, k * P:(k + 1) * P], g.c("identity"))
                last.then_inc(*turned.up())

            def values(j):
                t, h = jobs[j]
                pe.wait_ge(*placed.at(j + 1))
                if j > 0:
                    pe.wait_ge(*taken.at(j))
                products(nc, g.psum[:, 6, (j % 2) * P:(j % 2) * P + P], [aT[:, j % 2, k * P:(k + 1) * P] for k in range(t + 1)], [g.e_v[:, k, h * DVB:(h + 1) * DVB] for k in range(t + 1)]).then_inc(*mixed.up())

            def turn_rows(t):
                pe.wait_ge(*rows_ready.at(t + 1))
                for half in range(2):
                    if 2 * t + half > 0:
                        pe.wait_ge(*rows_placed.at(2 * t + half))
                    for c in range(3):
                        last = nc.tensor.transpose(g.psum[:, 7, c * P:(c + 1) * P], o[:, t % 2, (3 * half + c) * P:(3 * half + c + 1) * P], g.c("identity"))
                    last.then_inc(*rows_turned.up())

            scores(0)
            for j in range(len(jobs)):
                if j + 1 < len(jobs):
                    scores(j + 1)
                mix(j)
                if j >= 1:
                    values(j - 1)
                if j % HB == 3 and j > HB:
                    turn_rows(j // HB - 1)
            values(len(jobs) - 1)
            turn_rows(3)

        @block.sync
        def _(sp):
            sp.dma_start(lv, g.a["ev_lambda"].rearrange("a b c -> a (b c)").to_broadcast([P, 256])).then_inc(*lam_in.up(16))
            sp.dma_start(subln, g.a["ev_subln"].to_broadcast([P, DVB])).then_inc(*lam_in.up(16))
            g.feed(sp, ring_upto)

        @block.scalar
        def _(act):
            def copy_maps(j):
                t, h = jobs[j]
                act.wait_ge(*turned.at(j + 1))
                if j - 1 > 0:
                    act.wait_ge(*mixed.at(j - 1))
                nc.scalar.activation(aT[:, j % 2, 0:cw(t)], g.psum[:, 4 + j % 2, 0:cw(t)], ACT.Copy).then_inc(*placed.up())

            act.wait_ge(*exp_in.at(1))
            nc.scalar.activation(lam[:, 2:4], lam[:, 0:2], ACT.Exp).then_inc(*exp_out.up())
            for j, (t, h) in enumerate(jobs):
                for m in range(2):
                    act.wait_ge(*peaked.at(2 * j + m + 1))
                    if j - 1 > 0:
                        act.wait_ge(*combined.at(j - 1))
                    nc.scalar.activation(pr[:, j % 2, m, 0:cw(t)], g.psum[:, 2 * (j % 2) + m, 0:cw(t)], ACT.Exp, bias=peak[:, 2 * (j % 2) + m:2 * (j % 2) + m + 1],
                                                 scale=DKB ** -0.5, accum_out=total[:, j % 2, m:m + 1]).then_inc(*expd.up())
                if j:
                    copy_maps(j - 1)
            copy_maps(len(jobs) - 1)

        @block.gpsimd
        def _(pool):
            for t in range(4):
                pool.wait_ge(*summed.at(t + 1))
                inverse_root(g, pool, so, so, 1.0 / DVB, gchain, rooted, 1.0 - lam_init)

        @block.vector
        def _(dve):
            v = nc.vector
            dve.wait_ge(*lam_in.at(32))
            v.tensor_tensor(pair[:, 0, :], lv[:, 0, :], lv[:, 1, :], ALU.mult).then_inc(*chain.up())
            dve.wait_ge(*chain.last())
            v.tensor_tensor(pair[:, 1, :], lv[:, 2, :], lv[:, 3, :], ALU.mult).then_inc(*chain.up())
            dve.wait_ge(*chain.last())
            v.tensor_reduce(lam[:, 0:2], pair, AX.X, ALU.add).then_inc(*exp_in.up())
            dve.wait_ge(*exp_out.at(1))
            v.tensor_tensor(lam[:, 0:1], lam[:, 2:3], lam[:, 3:4], ALU.subtract).then_inc(*chain.up())
            dve.wait_ge(*chain.last())
            v.tensor_scalar(lam[:, 0:1], lam[:, 0:1], -1.0, -lam_init, ALU.mult, ALU.add).then_inc(*chain.up())
            dve.wait_ge(*chain.last())

            def peaks(j):
                t, h = jobs[j]
                for m in range(2):
                    q = peak[:, 2 * (j % 2) + m:2 * (j % 2) + m + 1]
                    dve.wait_ge(*scored.at(2 * j + m + 1))
                    if 2 * (j - 1) > 0:
                        dve.wait_ge(*expd.at(2 * (j - 1)))
                    v.tensor_reduce(q, g.psum[:, 2 * (j % 2) + m, 0:cw(t)], AX.X, ALU.max).then_inc(*chain.up())
                    dve.wait_ge(*chain.last())
                    v.tensor_scalar(q, q, -DKB ** -0.5, None, ALU.mult).then_inc(*peaked.up())

            def combine(j):
                t, h = jobs[j]
                dve.wait_ge(*expd.at(2 * j + 2))
                v.reciprocal(total[:, j % 2, :], total[:, j % 2, :]).then_inc(*chain.up())
                dve.wait_ge(*chain.last())
                v.tensor_tensor(total[:, j % 2, 1:2], total[:, j % 2, 1:2], lam[:, 0:1], ALU.mult).then_inc(*chain.up())
                dve.wait_ge(*chain.last())
                if j - 1 > 0:
                    dve.wait_ge(*turned.at(j - 1))
                v.tensor_scalar(pr[:, j % 2, 0, 0:cw(t)], pr[:, j % 2, 0, 0:cw(t)], total[:, j % 2, 0:1], None, ALU.mult).then_inc(*chain.up())
                dve.wait_ge(*chain.last())
                v.scalar_tensor_tensor(am[:, j % 2, 0:cw(t)], pr[:, j % 2, 1, 0:cw(t)], total[:, j % 2, 1:2], pr[:, j % 2, 0, 0:cw(t)], ALU.mult, ALU.add).then_inc(*combined.up())

            def take(j):
                t, h = jobs[j]
                dve.wait_ge(*mixed.at(j + 1))
                if h == 0 and t >= 2:
                    if 2 * (t - 1) > 0:
                        dve.wait_ge(*rows_turned.at(2 * (t - 1)))
                v.tensor_copy(o[:, t % 2, h * DVB:(h + 1) * DVB], g.psum[:, 6, (j % 2) * P:(j % 2) * P + P]).then_inc(*taken.up())
                if h == HB - 1:
                    dve.wait_ge(*taken.at(j + 1))
                    hv = lambda a: a.rearrange("p (h d) -> p h d", h=HB)
                    r = o[:, t % 2, :]
                    v.tensor_tensor(osq, r, r, ALU.mult).then_inc(*chain.up())
                    dve.wait_ge(*chain.last())
                    v.tensor_reduce(so, hv(osq), AX.X, ALU.add).then_inc(*summed.up())
                    dve.wait_ge(*rooted.at(t + 1))
                    v.tensor_tensor(hv(r), hv(r), so.unsqueeze(2).to_broadcast([P, HB, DVB]), ALU.mult).then_inc(*chain.up())
                    dve.wait_ge(*chain.last())
                    v.tensor_tensor(hv(r), hv(r), subln.unsqueeze(1).to_broadcast([P, HB, DVB]), ALU.mult).then_inc(*chain.up())
                    dve.wait_ge(*chain.last())
                    v.tensor_tensor(r, r, g.e_bg[:, t, :], ALU.mult).then_inc(*rows_ready.up())

            def place_rows(t):
                for half in range(2):
                    dve.wait_ge(*rows_turned.at(2 * t + half + 1))
                    v.tensor_copy(g.hT[:, 2 + 3 * half:5 + 3 * half, META + t * P:META + (t + 1) * P], g.psum[:, 7, 0:384].rearrange("p (c n) -> p c n", c=3)).then_inc(*rows_placed.up())

            peaks(0)
            for j in range(len(jobs)):
                if j % HB == 4 and j > HB:
                    place_rows(j // HB - 1)
                if j + 1 < len(jobs):
                    peaks(j + 1)
                combine(j)
                if j >= 2:
                    take(j - 2)
            take(len(jobs) - 2)
            take(len(jobs) - 1)
            place_rows(3)
    g.top = mark


def plan_odd(g):
    w = g.a["od_w_in"][0]
    chunks = [g.plan(w[:, 0:448], KD, 448), g.plan(w[:, 448:960], KD, 512)]
    chunks += [g.plan(w[:, 960 + 512 * n:1472 + 512 * n], KD, 512) for n in range(3)]
    chunks += [g.plan(w[:, 2496:2504], KD, 8), g.plan(w[:, 2504:3016], KD, 512)]
    up = [g.plan(g.a["od_w_uq"][0], 2, HC * DQK), g.plan(g.a["od_w_ukv"][0], 1, 1024)]
    out = [g.plan(g.a["od_w_out"][0][:, 512 * n:512 * n + 512], KD, 512) for n in range(2)]
    return chunks, up, out


def odd_layer(g, plans):
    chunks, up, out = plans
    g.top = 0
    g.o_conv = g.take(12, 4 + SEQ)
    g.o_dgate = g.take(4, 512)
    g.o_small = g.take(4, 8)
    keep = g.top
    g.o_cgate = g.take(4, 512)
    g.o_low = g.take(4, 448)
    stage_norm(g, XT, g.a["norm_g"][1], chunks[0] + 4)
    stage_odd_in(g, chunks, up[0] + 2)
    stage_mla_low(g, up[0] + 4)
    stage_mla_up(g, up, out[0] + 4)
    stage_mla_attention(g, out[0] + 4)
    g.top = keep
    stage_delta(g, out[0] + 4)
    stage_out(g, XT, out, out[1] + 4)
    g.top = 0


def stage_odd_in(g, chunks, ring_upto):
    nc = g.nc
    ready, freed_a, freed_v, zeroed = g.sig("product_ready", "bank_read_by_scalar", "bank_read_by_vector", "history_zeroed")
    units = [("low", 0, t) for t in XT] + [("cgate", 1, t) for t in XT]
    units += [("conv", 2 + f // 4, f) for f in range(12)]
    units += [("small", 5, t) for t in XT] + [("dgate", 6, t) for t in XT]
    width = {"low": 448, "cgate": 512, "conv": 512, "small": 8, "dgate": 512}
    scalar = lambda kind, x: kind in ("cgate", "dgate") or (kind == "conv" and x % 2 == 1)
    freed, na, nv = [], 0, 0
    for kind, c, x in units:
        if scalar(kind, x):
            na += 1
            freed.append((freed_a, na))
        else:
            nv += 1
            freed.append((freed_v, nv))
    NB = 8
    with nc.Block() as block:
        @block.tensor
        def _(pe):
            for u, (kind, c, x) in enumerate(units):
                if u == 0 or units[u - 1][1] != c:
                    g.weights_wait(pe, chunks[c])
                if u >= NB:
                    pe.wait_ge(*freed[u - NB][0].at(freed[u - NB][1]))
                bank = g.psum[:, u % NB, 0:width[kind]]
                if kind == "conv":
                    w = g.weights(chunks[c])
                    f = x % 4
                    products(nc, bank, [w[:, k, f * P:(f + 1) * P] for k in range(KD)], [g.hT[:, k, META:] for k in range(KD)]).then_inc(*ready.up())
                else:
                    rows_by_weights(g, pe, bank, x, chunks[c]).then_inc(*ready.up())
                if u + 1 == len(units) or units[u + 1][1] != c:
                    g.chunk_used(chunks[c], ready)

        @block.sync
        def _(sp):
            g.feed(sp, ring_upto)

        @block.scalar
        def _(act):
            for u, (kind, c, x) in enumerate(units):
                if not scalar(kind, x):
                    continue
                act.wait_ge(*ready.at(u + 1))
                bank = g.psum[:, u % NB, :]
                if kind == "conv":
                    nc.scalar.activation(g.o_conv[:, x, 4:], bank, ACT.Copy).then_inc(*freed_a.up())
                else:
                    dst = g.o_cgate if kind == "cgate" else g.o_dgate
                    nc.scalar.activation(dst[:, x - 1, :], bank, ACT.Silu).then_inc(*freed_a.up())

        @block.vector
        def _(dve):
            nc.vector.memset(g.o_conv[:, :, 0:4], 0.0).then_inc(*zeroed.up())
            for u, (kind, c, x) in enumerate(units):
                if scalar(kind, x):
                    continue
                dve.wait_ge(*ready.at(u + 1))
                bank = g.psum[:, u % NB, 0:width[kind]]
                dst = g.o_conv[:, x, 4:] if kind == "conv" else g.o_low[:, x - 1, :] if kind == "low" else g.o_small[:, x - 1, :]
                nc.vector.tensor_copy(dst, bank).then_inc(*freed_v.up())


def stage_mla_low(g, ring_upto):
    nc = g.nc
    g.m_low = g.take(3, SEQ)
    mark = g.top
    loaded, squared, rooted, scaled, transposed, moved, gchain = g.sig("gain_loaded", "rows_squared", "norm_ready", "rows_scaled", "rows_transposed", "transposed_moved", "gpsimd_step")
    gain = g.take(3)
    junk, rows = g.take(4, 384), g.take(4, 384)
    ss = g.take(8)
    with nc.Block() as block:
        @block.tensor
        def _(pe):
            for t in range(4):
                pe.wait_ge(*scaled.at(2 * t + 2))
                if t - 1 > 0:
                    pe.wait_ge(*moved.at(t - 1))
                for c in range(3):
                    last = nc.tensor.transpose(g.psum[:, t % 2, c * P:(c + 1) * P], rows[:, t, c * P:(c + 1) * P], g.c("identity"))
                last.then_inc(*transposed.up())

        @block.sync
        def _(sp):
            sp.dma_start(gain[:, 0:2], g.a["od_q_a_norm"].rearrange("a (k p) -> p (a k)", p=P), allow_slow_non_contiguous=True).then_inc(*loaded.up(16))
            sp.dma_start(gain[:, 2:3], g.a["od_kv_a_norm"].rearrange("a (k p) -> p (a k)", p=P), allow_slow_non_contiguous=True).then_inc(*loaded.up(16))
            g.feed(sp, ring_upto)

        @block.scalar
        def _(act):
            parts = [(t, part) for t in range(4) for part in (slice(0, 256), slice(256, 384))]
            for n, (t, part) in enumerate(parts):
                nc.scalar.activation(junk[:, t, part], g.o_low[:, t, part], ACT.Square, accum_out=ss[:, n:n + 1]).then_inc(*squared.up())
            for n, (t, part) in enumerate(parts):
                act.wait_ge(*rooted.at(2))
                nc.scalar.activation(rows[:, t, part], g.o_low[:, t, part], ACT.Copy, scale=ss[:, n:n + 1]).then_inc(*scaled.up())

        @block.gpsimd
        def _(pool):
            pool.wait_ge(*squared.at(8))
            pairs = ss.rearrange("p (t n) -> p n t", n=2)
            for n, width in enumerate((256, 128)):
                inverse_root(g, pool, pairs[:, n, :], pairs[:, n, :], 1.0 / width, gchain, rooted)

        @block.vector
        def _(dve):
            dve.wait_ge(*loaded.at(32))
            for t in range(4):
                dve.wait_ge(*transposed.at(t + 1))
                nc.vector.tensor_tensor(g.m_low[:, :, t * P:(t + 1) * P], g.psum[:, t % 2, 0:384].rearrange("p (c n) -> p c n", c=3), gain.unsqueeze(2).to_broadcast([P, 3, P]), ALU.mult).then_inc(*moved.up())
    g.top = mark


def stage_mla_up(g, up, ring_upto):
    nc = g.nc
    g.m_qn, g.m_kn = g.take(HC, SEQ), g.take(HC, SEQ)
    g.m_qr, g.m_kr = g.take(HC, SEQ), g.take(HC, SEQ)
    g.m_v = g.hT[:, 4:8, 0:HC * 128]
    mark = g.top
    ready, copied, values_out, squared, summed, rooted, normed, rotated, transposed, placed, chain, gchain, gains_in = g.sig(
        "product_ready", "heads_copied", "values_copied", "heads_squared", "heads_summed", "norm_ready", "heads_normed",
        "heads_rotated", "heads_transposed", "heads_placed", "vector_step", "gpsimd_step", "gains_loaded")
    gain = g.take(2, DQK)
    b = g.hT[:, 0:2, 0:2 * DQK].rearrange("p a (h d) -> p a h d", h=2)
    sq = g.hT[:, 2:4, 0:2 * DQK].rearrange("p a (h d) -> p a h d", h=2)
    ss = g.take(2, 2)
    rope = g.take(4, 64)
    units = [("q", t, half) for t in range(4) for half in range(2)] + [("k", t, half) for t in range(4) for half in range(2)]
    with nc.Block() as block:
        @block.tensor
        def _(pe):
            def turn(i):
                pe.wait_ge(*rotated.at(i + 1))
                if 2 * (i - 1) > 0:
                    pe.wait_ge(*placed.at(2 * (i - 1)))
                for j in range(2):
                    nc.tensor.transpose(g.psum[:, 4 + i % 2, j * P:(j + 1) * P], b[:, i % 2, j, 0:128], g.c("identity"))
                    last = nc.tensor.transpose(g.psum[0:64, 4 + i % 2, 256 + j * P:256 + (j + 1) * P], b[:, i % 2, j, 128:DQK], g.c("identity"))
                last.then_inc(*transposed.up())

            for i, (kind, t, half) in enumerate(units):
                if i in (0, 8):
                    g.weights_wait(pe, up[i // 8])
                if i - 1 > 0:
                    pe.wait_ge(*copied.at(i - 1))
                if kind == "q":
                    w = g.weights(up[0])
                    products(nc, g.psum[:, i % 2, 0:384], [g.m_low[:, k, t * P:(t + 1) * P] for k in range(2)], [w[:, k, 384 * half:384 * half + 384] for k in range(2)]).then_inc(*ready.up())
                else:
                    if i - 8 - 1 > 0:
                        pe.wait_ge(*values_out.at(i - 8 - 1))
                    w = g.weights(up[1])
                    products(nc, g.psum[:, i % 2, :], [g.m_low[:, 2, t * P:(t + 1) * P]], [w[:, 0, 512 * half:512 * half + 512]]).then_inc(*ready.up())
                if i in (7, 15):
                    g.chunk_used(up[i // 8], ready)
                if i:
                    turn(i - 1)
            turn(len(units) - 1)

        @block.sync
        def _(sp):
            sp.dma_start(gain[:, 0, :], g.a["od_q_norm"].to_broadcast([P, DQK])).then_inc(*gains_in.up(16))
            sp.dma_start(gain[:, 1, :], g.a["od_k_norm"].to_broadcast([P, DQK])).then_inc(*gains_in.up(16))
            g.feed(sp, ring_upto)

        @block.scalar
        def _(act):
            def place(i):
                kind, t, half = units[i]
                cols = slice(t * P, (t + 1) * P)
                n_, r_ = (g.m_qn, g.m_qr) if kind == "q" else (g.m_kn, g.m_kr)
                act.wait_ge(*transposed.at(i + 1))
                nc.scalar.activation(n_[:, 2 * half:2 * half + 2, cols], g.psum[:, 4 + i % 2, 0:256].rearrange("p (h n) -> p h n", h=2), ACT.Copy).then_inc(*placed.up())
                nc.scalar.activation(r_[0:64, 2 * half:2 * half + 2, cols], g.psum[0:64, 4 + i % 2, 256:512].rearrange("p (h n) -> p h n", h=2), ACT.Copy).then_inc(*placed.up())

            for i, (kind, t, half) in enumerate(units):
                act.wait_ge(*copied.at(i + 1))
                if i - 1 > 0:
                    act.wait_ge(*summed.at(i - 1))
                nc.scalar.activation(sq[:, i % 2, :, :], b[:, i % 2, :, :], ACT.Square).then_inc(*squared.up())
                if i:
                    place(i - 1)
            place(len(units) - 1)

        @block.vector
        def _(dve):
            v = nc.vector
            dve.wait_ge(*gains_in.at(32))
            for i, (kind, t, half) in enumerate(units):
                buf, bank = b[:, i % 2, :, :], g.psum[:, i % 2, :]
                dve.wait_ge(*ready.at(i + 1))
                if i - 1 > 0:
                    dve.wait_ge(*transposed.at(i - 1))
                if kind == "q":
                    v.tensor_copy(buf, bank[:, 0:384].rearrange("p (h d) -> p h d", h=2)).then_inc(*copied.up())
                    dve.wait_ge(*copied.last())
                else:
                    kv = bank.rearrange("p (h d) -> p h d", h=2)
                    v.tensor_copy(g.m_v[:, t, 256 * half:256 * half + 256].rearrange("p (h d) -> p h d", h=2), kv[:, :, 128:256]).then_inc(*values_out.up())
                    v.tensor_copy(buf[:, :, 128:DQK], g.o_low[:, t, 384:448].unsqueeze(1).to_broadcast([P, 2, 64])).then_inc(*chain.up())
                    dve.wait_ge(*chain.last())
                    v.tensor_copy(buf[:, :, 0:128], kv[:, :, 0:128]).then_inc(*copied.up())
                    dve.wait_ge(*copied.last())
                dve.wait_ge(*squared.at(i + 1))
                v.tensor_reduce(ss[:, i % 2, :], sq[:, i % 2, :, :], AX.X, ALU.add).then_inc(*summed.up())
                dve.wait_ge(*rooted.at(i + 1))
                v.tensor_tensor(buf, buf, ss[:, i % 2, :].unsqueeze(2).to_broadcast([P, 2, DQK]), ALU.mult).then_inc(*chain.up())
                dve.wait_ge(*chain.last())
                v.tensor_tensor(buf, buf, gain[:, 0 if kind == "q" else 1, :].unsqueeze(1).to_broadcast([P, 2, DQK]), ALU.mult).then_inc(*normed.up())

        @block.gpsimd
        def _(pool):
            for i in range(len(units) + 1):
                if i < len(units):
                    pool.wait_ge(*summed.at(i + 1))
                    inverse_root(g, pool, ss[:, i % 2, :], ss[:, i % 2, :], 1.0 / DQK, gchain, rooted)
                if i == 0:
                    continue
                kind, t, half = units[i - 1]
                if i > 0:
                    pool.wait_ge(*normed.at(i))
                v = b[:, (i - 1) % 2, :, :]
                rotate(g, pool, v[:, :, 128:160], v[:, :, 160:192], g.cos[:, t, 8:40], g.sin[:, t, 8:40], [rope[:, j, :] for j in range(4)], 2, 32, gchain, rotated)
    g.top = mark


def stage_mla_attention(g, ring_upto):
    nc = g.nc
    mark = g.top
    scored, peaked, expd, turned, placed, mixed, rows_turned, rows_placed, chain, taken = g.sig(
        "scores_ready", "row_peaks", "probabilities", "heads_transposed", "heads_placed",
        "mixed_ready", "rows_transposed", "rows_placed", "vector_step", "mixed_taken")
    peak, total = g.take(2), g.take(2)
    pr = g.m_low[:, 0:2, :]
    pT = g.o_low.rearrange("p t n -> p (t n)")[:, 0:1024].rearrange("p (a n) -> p a n", a=2)
    o = g.take(2, 512)
    jobs = [(t, h) for t in range(4) for h in range(HC)]
    cw = lambda t: P * (t + 1)
    N = len(jobs)
    with nc.Block() as block:
        @block.tensor
        def _(pe):
            def scores(j):
                t, h = jobs[j]
                if j - 1 > 0:
                    pe.wait_ge(*expd.at(j - 1))
                bank = g.psum[:, j % 2, :]
                q = slice(t * P, (t + 1) * P)
                nc.tensor.matmul(bank[:, 0:cw(t)], g.m_qn[:, h, q], g.m_kn[:, h, 0:cw(t)], start=True, stop=False)
                nc.tensor.matmul(bank[:, 0:cw(t)], g.m_qr[0:64, h, q], g.m_kr[0:64, h, 0:cw(t)], start=False, stop=False)
                nc.tensor.matmul(bank[:, t * P:cw(t)], g.c("identity"), g.c("causal"), start=False, stop=True).then_inc(*scored.up())

            def turn(j):
                t, h = jobs[j]
                pe.wait_ge(*expd.at(j + 1))
                if j - 1 > 0:
                    pe.wait_ge(*placed.at(j - 1))
                for k in range(t + 1):
                    last = nc.tensor.transpose(g.psum[:, 2 + j % 2, k * P:(k + 1) * P], pr[:, j % 2, k * P:(k + 1) * P], g.c("identity"))
                last.then_inc(*turned.up())

            def values(j):
                t, h = jobs[j]
                pe.wait_ge(*placed.at(j + 1))
                if j - 1 > 0:
                    pe.wait_ge(*taken.at(j - 1))
                products(nc, g.psum[:, 4 + j % 2, 0:P], [pT[:, j % 2, k * P:(k + 1) * P] for k in range(t + 1)], [g.m_v[:, k, h * P:(h + 1) * P] for k in range(t + 1)]).then_inc(*mixed.up())

            def turn_rows(t):
                if True:
                    pe.wait_ge(*taken.at(HC * (t + 1)))
                if t - 1 > 0:
                    pe.wait_ge(*rows_placed.at(t - 1))
                for c in range(4):
                    last = nc.tensor.transpose(g.psum[:, 6 + t % 2, c * P:(c + 1) * P], o[:, t % 2, c * P:(c + 1) * P], g.c("identity"))
                last.then_inc(*rows_turned.up())

            scores(0)
            for j in range(N):
                if j + 1 < N:
                    scores(j + 1)
                turn(j)
                if j:
                    values(j - 1)
                if j % HC == 2 and j > HC:
                    turn_rows(j // HC - 1)
            values(N - 1)
            turn_rows(3)

        @block.sync
        def _(sp):
            g.feed(sp, ring_upto)

        @block.scalar
        def _(act):
            def copy_map(j):
                t, h = jobs[j]
                act.wait_ge(*turned.at(j + 1))
                if j - 1 > 0:
                    act.wait_ge(*mixed.at(j - 1))
                nc.scalar.activation(pT[:, j % 2, 0:cw(t)], g.psum[:, 2 + j % 2, 0:cw(t)], ACT.Copy).then_inc(*placed.up())

            for j, (t, h) in enumerate(jobs):
                act.wait_ge(*peaked.at(j + 1))
                if j - 1 > 0:
                    act.wait_ge(*turned.at(j - 1))
                if j - 1 > 0:
                    act.wait_ge(*taken.at(j - 1))
                nc.scalar.activation(pr[:, j % 2, 0:cw(t)], g.psum[:, j % 2, 0:cw(t)], ACT.Exp, bias=peak[:, j % 2:j % 2 + 1], scale=DQK ** -0.5, accum_out=total[:, j % 2:j % 2 + 1]).then_inc(*expd.up())
                if j:
                    copy_map(j - 1)
            copy_map(N - 1)

        @block.vector
        def _(dve):
            v = nc.vector

            def peaks(j):
                t, h = jobs[j]
                q = peak[:, j % 2:j % 2 + 1]
                dve.wait_ge(*scored.at(j + 1))
                if j - 1 > 0:
                    dve.wait_ge(*expd.at(j - 1))
                v.tensor_reduce(q, g.psum[:, j % 2, 0:cw(t)], AX.X, ALU.max).then_inc(*chain.up())
                dve.wait_ge(*chain.last())
                v.tensor_scalar(q, q, -DQK ** -0.5, None, ALU.mult).then_inc(*peaked.up())

            def take(j):
                t, h = jobs[j]
                dve.wait_ge(*mixed.at(j + 1))
                if h == 0 and t >= 2:
                    if t - 1 > 0:
                        dve.wait_ge(*rows_turned.at(t - 1))
                s = total[:, j % 2:j % 2 + 1]
                v.reciprocal(s, s).then_inc(*chain.up())
                dve.wait_ge(*chain.last())
                v.scalar_tensor_tensor(o[:, t % 2, h * P:(h + 1) * P], g.psum[:, 4 + j % 2, 0:P], s, g.o_cgate[:, t, h * P:(h + 1) * P], ALU.mult, ALU.mult).then_inc(*taken.up())

            def place_rows(t):
                dve.wait_ge(*rows_turned.at(t + 1))
                v.tensor_copy(g.hT[:, 0:4, META + t * P:META + (t + 1) * P], g.psum[:, 6 + t % 2, :].rearrange("p (c n) -> p c n", c=4)).then_inc(*rows_placed.up())

            for j in range(N + 2):
                if j % HC == 3 and j > HC:
                    place_rows(j // HC - 1)
                if j < N:
                    peaks(j)
                if j >= 2:
                    take(j - 2)
            place_rows(3)
    g.top = mark


def stage_delta(g, ring_upto):
    nc = g.nc
    NCH = 4
    tok = g.take(4, 8, P)
    vt = g.take(4, 4, P)
    qkT = g.take(8, SEQ)
    beta, gl = g.take(4, HD), g.take(4, HD)
    mark = g.top
    loaded, convd, silud, turned, copied, chain, achain, gchain, betas, decays, squared, rooted, scaled, back, backed = g.sig(
        "delta_weights_loaded", "channels_convolved", "channels_activated", "channels_transposed", "channels_placed", "vector_step", "scalar_step", "gpsimd_step",
        "betas_ready", "decays_ready", "heads_summed", "norm_ready", "heads_scaled", "heads_transposed", "heads_placed")
    cwt = g.take(12, 4)
    gate_in = g.take(2, HD)
    acc, sil = g.take(2, SEQ), g.take(2, SEQ)
    tmp = g.take(4, 16)
    sq = g.take(8, P)
    ss = g.take(4, 8)
    with nc.Block() as block:
        @block.tensor
        def _(pe):
            for f in range(12):
                pe.wait_ge(*silud.at(f + 1))
                if f - 1 > 0:
                    pe.wait_ge(*copied.at(f - 1))
                for t in range(4):
                    last = nc.tensor.transpose(g.psum[:, f % 2, t * P:(t + 1) * P], sil[:, f % 2, t * P:(t + 1) * P], g.c("identity"))
                last.then_inc(*turned.up())
            for t in range(4):
                pe.wait_ge(*scaled.at(t + 1))
                for half in range(2):
                    u = 2 * t + half
                    if u - 1 > 0:
                        pe.wait_ge(*backed.at(u - 1))
                    for c in range(4):
                        last = nc.tensor.transpose(g.psum[:, 2 + u % 2, c * P:(c + 1) * P], tok[:, t, 4 * half + c, :], g.c("identity"))
                    last.then_inc(*back.up())

        @block.sync
        def _(sp):
            sp.dma_start(cwt, g.a["od_conv_T"].rearrange("(f p) k -> p f k", p=P)).then_inc(*loaded.up(16))
            sp.dma_start(gate_in[:, 0, :], g.a["od_a_log"].to_broadcast([P, HD])).then_inc(*loaded.up(16))
            sp.dma_start(gate_in[:, 1, :], g.a["od_dt_bias"].to_broadcast([P, HD])).then_inc(*loaded.up(16))
            g.feed(sp, ring_upto)

        @block.scalar
        def _(act):
            for f in range(12):
                act.wait_ge(*convd.at(f + 1))
                if f - 1 > 0:
                    act.wait_ge(*turned.at(f - 1))
                nc.scalar.activation(sil[:, f % 2, :], acc[:, f % 2, :], ACT.Silu).then_inc(*silud.up())
            act.wait_ge(*loaded.at(48))
            nc.scalar.activation(beta, g.o_small[:, :, 0:4], ACT.Sigmoid).then_inc(*betas.up())
            act.wait_ge(*decays.at(1))
            nc.scalar.activation(tmp[:, 1, :], tmp[:, 1, :], ACT.Exp, scale=-1.0).then_inc(*achain.up())
            act.wait_ge(*achain.last())
            nc.scalar.activation(tmp[:, 2, 0:4], gate_in[:, 0, :], ACT.Exp).then_inc(*achain.up())
            act.wait_ge(*achain.last())
            act.wait_ge(*decays.at(2))
            nc.scalar.activation(tmp[:, 1, :], tmp[:, 1, :], ACT.Ln).then_inc(*achain.up())

        @block.gpsimd
        def _(pool):
            for t in range(4):
                pool.wait_ge(*squared.at(t + 1))
                for n, factor in enumerate((128 ** -0.5, None)):
                    s = ss[:, t, 4 * n:4 * n + 4]
                    inverse_root(g, pool, s, s, 1.0, gchain, rooted, factor)

        @block.vector
        def _(dve):
            v = nc.vector
            def place(t):
                for half in range(2):
                    u = 2 * t + half
                    dve.wait_ge(*back.at(u + 1))
                    v.tensor_copy(qkT[:, 4 * half:4 * half + 4, t * P:(t + 1) * P], g.psum[:, 2 + u % 2, :].rearrange("p (c n) -> p c n", c=4)).then_inc(*backed.up())

            dve.wait_ge(*loaded.at(48))
            for f in range(14):
                if f < 12:
                    x = g.o_conv[:, f, :]
                    if f - 1 > 0:
                        dve.wait_ge(*silud.at(f - 1))
                    a = acc[:, f % 2, :]
                    v.tensor_scalar(a, x[:, 1:1 + SEQ], cwt[:, f, 0:1], None, ALU.mult).then_inc(*chain.up())
                    dve.wait_ge(*chain.last())
                    for k in range(1, 3):
                        v.scalar_tensor_tensor(a, x[:, 1 + k:1 + k + SEQ], cwt[:, f, k:k + 1], a, ALU.mult, ALU.add).then_inc(*chain.up())
                        dve.wait_ge(*chain.last())
                    v.scalar_tensor_tensor(a, x[:, 4:4 + SEQ], cwt[:, f, 3:4], a, ALU.mult, ALU.add).then_inc(*convd.up())
                if f >= 2:
                    if f - 1 > 0:
                        dve.wait_ge(*turned.at(f - 1))
                    n = f - 2
                    dst = tok[:, :, n, :] if n < 8 else vt[:, :, n - 8, :]
                    v.tensor_copy(dst, g.psum[:, n % 2, :].rearrange("p (t d) -> p t d", t=4)).then_inc(*copied.up())
            dve.wait_ge(*copied.at(12))
            for t in range(4):
                v.tensor_tensor(sq, tok[:, t, :, :], tok[:, t, :, :], ALU.mult).then_inc(*chain.up())
                dve.wait_ge(*chain.last())
                v.tensor_reduce(ss[:, t, :], sq, AX.X, ALU.add).then_inc(*squared.up())
                dve.wait_ge(*rooted.at(2 * t + 2))
                v.tensor_tensor(tok[:, t, :, :], tok[:, t, :, :], ss[:, t, :].unsqueeze(2).to_broadcast([P, 8, P]), ALU.mult).then_inc(*scaled.up())
                if t:
                    place(t - 1)
            place(3)
            fl = lambda n: tmp[:, n, :].rearrange("p (t h) -> p t h", t=4)
            v.tensor_tensor(fl(0), g.o_small[:, :, 4:8], gate_in[:, 1, :].unsqueeze(1).to_broadcast([P, 4, HD]), ALU.add).then_inc(*chain.up())
            dve.wait_ge(*chain.last())
            v.tensor_scalar(tmp[:, 1, :], tmp[:, 0, :], -1.0, None, ALU.mult).then_inc(*chain.up())
            dve.wait_ge(*chain.last())
            v.tensor_tensor(tmp[:, 1, :], tmp[:, 0, :], tmp[:, 1, :], ALU.max).then_inc(*decays.up())
            dve.wait_ge(*achain.at(2))
            v.tensor_scalar(tmp[:, 1, :], tmp[:, 1, :], 1.0, None, ALU.add).then_inc(*decays.up())
            dve.wait_ge(*achain.at(3))
            v.scalar_tensor_tensor(tmp[:, 0, :], tmp[:, 0, :], 0.0, tmp[:, 1, :], ALU.max, ALU.add).then_inc(*chain.up())
            dve.wait_ge(*chain.last())
            v.tensor_scalar(tmp[:, 2, 0:4], tmp[:, 2, 0:4], -1.0, None, ALU.mult).then_inc(*chain.up())
            dve.wait_ge(*chain.last())
            v.tensor_tensor(gl, fl(0), tmp[:, 2, 0:4].unsqueeze(1).to_broadcast([P, 4, HD]), ALU.mult).then_inc(*chain.up())
            dve.wait_ge(*chain.last())
    g.top = mark
    cum_ready, cols, expd, kq, ut, tt, prod, red, scanned, done, rows_turned, rows_placed, rooted, gains_in, summed = g.sig(
        "cumulated", "exponents_ready", "decays_exped", "key_products", "inverse_T", "inverse", "product_ready", "reduced", "scan_product", "scan_step",
        "rows_transposed", "rows_placed", "norm_ready", "gains_loaded", "heads_summed")
    H4 = lambda ap: ap.rearrange("p (h d) -> p h d", h=HD)
    col, nlast, egc, dlast, elast = (g.take(HD) for _ in range(5))
    spare = g.o_conv.rearrange("p f n -> p (f n)")[:, 0:12 * HD * P].rearrange("p (n h d) -> p n h d", n=12, h=HD)
    rowc, gamT, LT = (spare[:, n, :, :] for n in (0, 1, 2))
    U, T, Lv, X = (spare[:, n, :, :] for n in (3, 4, 5, 6))
    qkg, kb, vb, kd = (spare[:, n, :, :] for n in (7, 8, 9, 10))
    uu = spare[:, 11, :, :]
    wT, vn = g.take(HD, P), g.take(HD, P)
    S = g.take(HD, P)
    o, og = g.take(HD, P), g.take(HD, P)
    so = g.take(HD)
    onorm = g.take(P)
    bc = lambda ap: ap.unsqueeze(2).to_broadcast([P, HD, P])
    mid = lambda name: g.c(name).unsqueeze(1).to_broadcast([P, HD, P])
    pq = lambda n: H4(g.psum[:, n, :])
    with nc.Block() as block:
        @block.tensor
        def _(pe):
            mm, tr = nc.tensor.matmul, nc.tensor.transpose
            for n in range(NCH):
                q = slice(n * P, (n + 1) * P)
                if n:
                    if n > 0:
                        pe.wait_ge(*done.at(n))
                mm(g.psum[:, 0, 0:HD], g.c("upto"), gl[:, n, :], start=True, stop=True)
                for h in range(HD):
                    last = mm(pq(1)[:, h, :], gl[:, n, h:h + 1].to_broadcast([P, P]), g.c("upto"), start=True, stop=True)
                last.then_inc(*cum_ready.up())
                for h in range(HD):
                    mm(pq(2)[:, h, :], qkT[:, 4 + h, q], qkT[:, 4 + h, q], start=True, stop=True)
                    last = mm(pq(3)[:, h, :], qkT[:, 4 + h, q], qkT[:, h, q], start=True, stop=True)
                for h in range(HD):
                    last = mm(pq(4)[:, h, :], beta[:, n, h:h + 1].to_broadcast([P, P]), g.c("identity"), start=True, stop=True)
                last.then_inc(*kq.up())
                pe.wait_ge(*ut.at(7 * n + 1))
                for h in range(HD):
                    last = tr(pq(5)[:, h, :], U[:, h, :], g.c("identity"))
                last.then_inc(*prod.up())
                for level in range(1, 7):
                    if 6 * n + level > 0:
                        pe.wait_ge(*tt.at(6 * n + level))
                    for h in range(HD):
                        last = mm(pq(2)[:, h, :], Lv[:, h, :], T[:, h, :], start=True, stop=True)
                    last.then_inc(*prod.up())
                    if 6 * n + level > 0:
                        pe.wait_ge(*red.at(6 * n + level))
                    for h in range(HD):
                        last = mm(pq(3)[:, h, :], X[:, h, :], U[:, h, :], start=True, stop=True)
                    if level < 6:
                        for h in range(HD):
                            last = mm(pq(4)[:, h, :], U[:, h, :], X[:, h, :], start=True, stop=True)
                    last.then_inc(*prod.up())
                pe.wait_ge(*ut.at(7 * n + 7))
                for h in range(HD):
                    mm(pq(0)[:, h, :], U[:, h, :], vb[:, h, :], start=True, stop=True)
                    last = mm(pq(1)[:, h, :], kb[:, h, :], U[:, h, :], start=True, stop=True)
                last.then_inc(*prod.up())
                pe.wait_ge(*scanned.at(3 * n + 1))
                for h in range(HD):
                    mm(pq(5)[:, h, :], wT[:, h, :], S[:, h, :], start=True, stop=True)
                    last = mm(pq(6)[:, h, :], qkT[:, h, q], S[:, h, :], start=True, stop=True)
                last.then_inc(*prod.up())
                pe.wait_ge(*scanned.at(3 * n + 2))
                for h in range(HD):
                    mm(pq(7)[:, h, :], qkg[:, h, :], vn[:, h, :], start=True, stop=True)
                    last = mm(pq(0)[:, h, :], kd[:, h, :], vn[:, h, :], start=True, stop=True)
                last.then_inc(*prod.up())
                pe.wait_ge(*scanned.at(3 * n + 3))
                for h in range(HD):
                    last = tr(pq(1)[:, h, :], og[:, h, :], g.c("identity"))
                last.then_inc(*rows_turned.up())

        @block.sync
        def _(sp):
            sp.dma_start(onorm, g.a["od_o_norm"].to_broadcast([P, P])).then_inc(*gains_in.up(16))
            g.feed(sp, ring_upto)

        @block.scalar
        def _(act):
            for n in range(NCH):
                act.wait_ge(*cols.at(n + 1))
                nc.scalar.activation(gamT, gamT, ACT.Exp).then_inc(*expd.up())
                nc.scalar.activation(egc, col, ACT.Exp).then_inc(*expd.up())
                nc.scalar.activation(dlast, dlast, ACT.Exp).then_inc(*expd.up())
                nc.scalar.activation(elast, nlast, ACT.Exp).then_inc(*expd.up())

        @block.gpsimd
        def _(pool):
            for n in range(NCH):
                pool.wait_ge(*summed.at(n + 1))
                inverse_root(g, pool, so, so, 1.0 / P, gchain, rooted)

        @block.vector
        def _(dve):
            v = nc.vector
            dve.wait_ge(*gains_in.at(16))
            v.memset(S, 0.0).then_inc(*chain.up())
            dve.wait_ge(*chain.last())
            per = 16
            for n in range(NCH):
                p0 = per * n
                dve.wait_ge(*cum_ready.at(n + 1))
                v.tensor_copy(col, g.psum[:, 0, 0:HD]).then_inc(*chain.up())
                dve.wait_ge(*chain.last())
                v.tensor_copy(rowc, pq(1)).then_inc(*chain.up())
                dve.wait_ge(*chain.last())
                v.tensor_copy(nlast, rowc[:, :, P - 1]).then_inc(*chain.up())
                dve.wait_ge(*chain.last())
                v.tensor_tensor(dlast, nlast, col, ALU.subtract).then_inc(*chain.up())
                dve.wait_ge(*chain.last())
                v.tensor_tensor(gamT, rowc, bc(col), ALU.subtract).then_inc(*chain.up())
                dve.wait_ge(*chain.last())
                v.tensor_tensor(gamT, gamT, mid("upto"), ALU.mult).then_inc(*chain.up())
                dve.wait_ge(*chain.last())
                v.tensor_tensor(gamT, gamT, mid("later"), ALU.add).then_inc(*cols.up())
                dve.wait_ge(*expd.at(4 * n + 4))
                dve.wait_ge(*kq.at(n + 1))
                v.tensor_tensor(LT, gamT, pq(2), ALU.mult).then_inc(*chain.up())
                dve.wait_ge(*chain.last())
                v.tensor_tensor(LT, LT, pq(4), ALU.mult).then_inc(*chain.up())
                dve.wait_ge(*chain.last())
                v.tensor_tensor(qkg, gamT, pq(3), ALU.mult).then_inc(*chain.up())
                dve.wait_ge(*chain.last())
                v.tensor_tensor(Lv, LT, mid("half0"), ALU.mult).then_inc(*chain.up())
                dve.wait_ge(*chain.last())
                v.scalar_tensor_tensor(U, Lv, -1.0, mid("identity"), ALU.mult, ALU.add).then_inc(*ut.up())
                b = bc(beta[:, n, :])
                v.tensor_tensor(vb, vt[:, n, :, :], b, ALU.mult).then_inc(*chain.up())
                v.tensor_tensor(kb, tok[:, n, 4:8, :], b, ALU.mult).then_inc(*chain.up())
                dve.wait_ge(*chain.last())
                v.tensor_tensor(kb, kb, bc(egc), ALU.mult).then_inc(*chain.up())
                dve.wait_ge(*chain.last())
                v.tensor_tensor(kd, tok[:, n, 4:8, :], bc(dlast), ALU.mult).then_inc(*chain.up())
                dve.wait_ge(*chain.last())
                dve.wait_ge(*prod.at(p0 + 1))
                v.tensor_copy(T, pq(5)).then_inc(*chain.up())
                dve.wait_ge(*chain.last())
                for level in range(1, 7):
                    v.tensor_tensor(Lv, LT, mid(f"half{level}"), ALU.mult).then_inc(*tt.up())
                    if p0 + 2 * level > 0:
                        dve.wait_ge(*prod.at(p0 + 2 * level))
                    v.tensor_copy(X, pq(2)).then_inc(*red.up())
                    dve.wait_ge(*prod.at(p0 + 2 * level + 1))
                    if level < 6:
                        v.tensor_tensor(T, T, pq(4), ALU.subtract).then_inc(*chain.up())
                        dve.wait_ge(*chain.last())
                    v.tensor_tensor(U, U, pq(3), ALU.subtract).then_inc(*ut.up())
                    dve.wait_ge(*ut.last())
                if p0 + 14 + 0 > 0:
                    dve.wait_ge(*prod.at(p0 + 14 + 0))
                v.tensor_copy(uu, pq(0)).then_inc(*chain.up())
                dve.wait_ge(*chain.last())
                v.tensor_copy(wT, pq(1)).then_inc(*scanned.up())
                dve.wait_ge(*prod.at(p0 + 15))
                v.tensor_tensor(vn, uu, pq(5), ALU.subtract).then_inc(*chain.up())
                dve.wait_ge(*chain.last())
                v.tensor_tensor(o, pq(6), bc(egc), ALU.mult).then_inc(*scanned.up())
                dve.wait_ge(*prod.at(p0 + 16))
                dve.wait_ge(*scanned.at(3 * n + 2))
                v.tensor_tensor(o, o, pq(7), ALU.add).then_inc(*chain.up())
                dve.wait_ge(*chain.last())
                v.tensor_tensor(S, S, bc(elast), ALU.mult).then_inc(*chain.up())
                dve.wait_ge(*chain.last())
                v.tensor_tensor(S, S, pq(0), ALU.add).then_inc(*chain.up())
                dve.wait_ge(*chain.last())
                v.tensor_tensor(X, o, o, ALU.mult).then_inc(*chain.up())
                dve.wait_ge(*chain.last())
                v.tensor_reduce(so, X, AX.X, ALU.add).then_inc(*summed.up())
                dve.wait_ge(*rooted.at(n + 1))
                v.tensor_tensor(o, o, bc(so), ALU.mult).then_inc(*chain.up())
                dve.wait_ge(*chain.last())
                v.tensor_tensor(o, o, onorm.unsqueeze(1).to_broadcast([P, HD, P]), ALU.mult).then_inc(*chain.up())
                dve.wait_ge(*chain.last())
                v.tensor_tensor(og, o, H4(g.o_dgate[:, n, :]), ALU.mult).then_inc(*scanned.up())
                dve.wait_ge(*rows_turned.at(n + 1))
                v.tensor_copy(g.hT[:, 4:8, META + n * P:META + (n + 1) * P], pq(1)).then_inc(*done.up())
    g.top = mark


def plan_fox(g):
    w = g.a["fox_w_in_2"][0]
    chunks = [g.plan(w[:, 512 * n:512 * n + 512], KD, 512) for n in range(6)] + [g.plan(w[:, 3072:3088], KD, 16)]
    out = [g.plan(g.a["fox_w_out_2"][0][:, 512 * n:512 * n + 512], KD, 512) for n in range(2)]
    return chunks, out


def fox_layer(g, plans):
    chunks, out = plans
    g.top = 0
    stage_norm(g, ALLT, g.a["fox_norm_2"][0], chunks[0] + 4)
    stage_fox_in(g, chunks, out[0] + 2)
    stage_fox_attention(g, out[0] + 2)
    stage_out(g, ALLT, out, out[0] + 2)
    g.top = 0


def stage_fox_in(g, chunks, ring_upto):
    nc = g.nc
    ready, freed_a, freed_v, squared, summed, rooted, normed, transposed, placed, chain, gchain, gains_in = g.sig(
        "product_ready", "bank_read_by_scalar", "bank_read_by_vector", "heads_squared", "heads_summed", "norm_ready", "heads_normed",
        "heads_transposed", "heads_placed", "vector_step", "gpsimd_step", "gains_loaded")
    g.f_qT, g.f_kT = g.take(8, TOKENS), g.take(8, TOKENS)
    g.f_v = g.take(5, D)
    g.f_logit = g.take(5, FH)
    mark = g.top
    gain = g.take(2, FD)
    sq, qn = g.take(2, 512), g.take(2, 512)
    ss = g.take(2, 8)
    units = [(kind, 2 * "qkv".index(kind) + half, t) for kind in "qkv" for half in range(2) for t in ALLT] + [("f", 6, t) for t in ALLT]
    freed, na, nv = [], 0, 0
    for kind, *_ in units:
        if kind in "vf":
            na += 1
            freed.append((freed_a, na))
        else:
            nv += 1
            freed.append((freed_v, nv))
    qk = [u for u in units if u[0] in "qk"]
    NB = 6
    heads = lambda ap: ap.rearrange("p (g d) -> p g d", d=FD)
    with nc.Block() as block:
        @block.tensor
        def _(pe):
            def turn(i):
                n = TILES[qk[i][2]][1]
                pe.wait_ge(*normed.at(i + 1))
                if i - 1 > 0:
                    pe.wait_ge(*placed.at(i - 1))
                for j in range(4):
                    last = nc.tensor.transpose(g.psum[:, 6 + i % 2, j * P:j * P + n], qn[0:n, i % 2, j * P:(j + 1) * P], g.c("identity")[0:n, 0:n])
                last.then_inc(*transposed.up())

            i = 0
            for u, (kind, c, t) in enumerate(units):
                n = TILES[t][1]
                if u == 0 or units[u - 1][1] != c:
                    g.weights_wait(pe, chunks[c])
                if u >= NB:
                    pe.wait_ge(*freed[u - NB][0].at(freed[u - NB][1]))
                rows_by_weights(g, pe, g.psum[0:n, u % NB, 0:FH if kind == "f" else 512], t, chunks[c]).then_inc(*ready.up())
                if u + 1 == len(units) or units[u + 1][1] != c:
                    g.chunk_used(chunks[c], ready)
                if 2 <= i + (kind in "qk") and i < len(qk) + 2:
                    if i >= 2:
                        turn(i - 2)
                i += 1

        @block.sync
        def _(sp):
            sp.dma_start(gain[:, 0, :], g.a["fox_q_norm_2"].to_broadcast([P, FD])).then_inc(*gains_in.up(16))
            sp.dma_start(gain[:, 1, :], g.a["fox_k_norm_2"].to_broadcast([P, FD])).then_inc(*gains_in.up(16))
            g.feed(sp, ring_upto)

        @block.scalar
        def _(act):
            def place(i):
                kind, c, t = qk[i]
                a, n = TILES[t]
                dst = g.f_qT if kind == "q" else g.f_kT
                act.wait_ge(*transposed.at(i + 1))
                nc.scalar.activation(dst[:, 4 * (c % 2):4 * (c % 2) + 4, a:a + n], g.psum[:, 6 + i % 2, :].rearrange("p (h n) -> p h n", h=4)[:, :, 0:n], ACT.Copy).then_inc(*placed.up())

            for u, (kind, c, t) in enumerate(units):
                n = TILES[t][1]
                act.wait_ge(*ready.at(u + 1))
                bank = g.psum[0:n, u % NB, :]
                if kind in "qk":
                    if u - 1 > 0:
                        act.wait_ge(*summed.at(u - 1))
                    nc.scalar.activation(sq[0:n, u % 2, :], bank, ACT.Square).then_inc(*squared.up())
                elif kind == "v":
                    nc.scalar.activation(g.f_v[0:n, t, 512 * (c - 4):512 * (c - 3)], bank, ACT.Copy).then_inc(*freed_a.up())
                else:
                    nc.scalar.activation(g.f_logit[0:n, t, :], bank[:, 0:FH], ACT.Copy).then_inc(*freed_a.up())
                if 2 <= u < len(qk) + 2:
                    place(u - 2)

        @block.gpsimd
        def _(pool):
            for i, (kind, c, t) in enumerate(qk):
                n = TILES[t][1]
                pool.wait_ge(*summed.at(i + 1))
                inverse_root(g, pool, ss[0:n, i % 2, :], ss[0:n, i % 2, :], 1.0 / FD, gchain, rooted)

        @block.vector
        def _(dve):
            v = nc.vector
            dve.wait_ge(*gains_in.at(32))
            for i, (kind, c, t) in enumerate(qk):
                n = TILES[t][1]
                dve.wait_ge(*squared.at(i + 1))
                v.tensor_reduce(ss[0:n, i % 2, :], heads(sq[0:n, i % 2, :]), AX.X, ALU.add).then_inc(*summed.up())
                dve.wait_ge(*rooted.at(i + 1))
                if i - 1 > 0:
                    dve.wait_ge(*transposed.at(i - 1))
                buf = heads(qn[0:n, i % 2, :])
                v.tensor_tensor(buf, heads(g.psum[0:n, i % NB, :]), ss[0:n, i % 2, :].unsqueeze(2).to_broadcast([n, 8, FD]), ALU.mult).then_inc(*freed_v.up())
                dve.wait_ge(*freed_v.last())
                v.tensor_tensor(buf, buf, gain[0:n, 0 if kind == "q" else 1, :].unsqueeze(1).to_broadcast([n, 8, FD]), ALU.mult).then_inc(*normed.up())
    g.top = mark


def stage_fox_attention(g, ring_upto):
    nc = g.nc
    mark = g.top
    bias_in, gate, cums, rows, rows_out, scored, peaked, expd, turned, placed, mixed, o_turned, o_placed, chain, achain, taken = g.sig(
        "forget_bias_loaded", "forget_exponents", "cumulated", "gate_row_ready", "gate_row_placed", "scores_ready", "row_peaks", "probabilities",
        "heads_transposed", "heads_placed", "mixed_ready", "rows_transposed", "rows_placed", "vector_step", "scalar_step", "mixed_taken")
    bf = g.take(FH)
    lf = g.take(2, 5 * FH)
    cum = g.take(TOKENS)
    ones = g.take(TOKENS)
    row = g.take(2, TOKENS)
    sc = g.take(2, TOKENS)
    pT = g.take(1, 5 * P)
    peak, total = g.take(2), g.take(2)
    jobs = [(h, t) for h in range(FH) for t in reversed(ALLT)]
    N = len(jobs)
    keys = lambda t: TILES[t][0] + TILES[t][1]
    window = lambda j: g.psum[:, 2 * (j % 2):2 * (j % 2) + 2, :].rearrange("p b n -> p (b n)")
    flat = lambda n: lf[:, n, :]
    with nc.Block() as block:
        @block.tensor
        def _(pe):
            mm, tr = nc.tensor.matmul, nc.tensor.transpose
            pe.wait_ge(*gate.at(3))
            for t in ALLT:
                a, n = TILES[t]
                dst = g.psum[0:FH, 4, 0:n] if t == 0 else g.psum[0:FH, 5, a - META:a - META + n]
                last = tr(dst, flat(0)[0:n, t * FH:(t + 1) * FH], g.c("identity")[0:n, 0:n])
            last.then_inc(*cums.up())

            def gate_row(h):
                if h >= 1:
                    if 2 * h > 0:
                        pe.wait_ge(*rows_out.at(2 * h))
                pick = g.c("identity")[0:FH, h:h + 1].to_broadcast([FH, P])
                mm(g.psum[:, 7, :], pick, cum[0:FH, META:], start=True, stop=True).then_inc(*rows.up())
                pe.wait_ge(*rows_out.at(2 * h + 1))
                mm(g.psum[:, 7, 0:META], pick, cum[0:FH, 0:META], start=True, stop=True).then_inc(*rows.up())

            def scores(j):
                h, t = jobs[j]
                a, n = TILES[t]
                if j - 1 > 0:
                    pe.wait_ge(*peaked.at(j - 1))
                r = slice(64 * (h % 2), 64 * (h % 2) + 64)
                w, q, c = window(j), g.f_qT[r, h // 2, a:a + n], h // 2
                if t == 0:
                    mm(w[0:n, 496:512], q, g.f_kT[r, c, 0:META], start=True, stop=False)
                    mm(w[0:n, 496:512], g.c("identity")[0:n, 0:n], g.c("causal")[0:n, 0:n], start=False, stop=True).then_inc(*scored.up())
                else:
                    mm(w[:, 496:512], q, g.f_kT[r, c, 0:META], start=True, stop=True)
                    mm(w[:, 512:512 + t * P], q, g.f_kT[r, c, META:keys(t)], start=True, stop=False)
                    mm(w[:, 512 + (t - 1) * P:512 + t * P], g.c("identity"), g.c("causal"), start=False, stop=True).then_inc(*scored.up())

            def turn(j):
                h, t = jobs[j]
                n = TILES[t][1]
                pe.wait_ge(*expd.at(j + 1))
                if j > 0:
                    pe.wait_ge(*placed.at(j))
                for k in range(t + 1):
                    a, m = TILES[k]
                    dst = g.psum[0:META, 5, 0:n] if k == 0 else g.psum[:, 4, (k - 1) * P:(k - 1) * P + n]
                    last = tr(dst, sc[0:n, j % 2, a:a + m], g.c("identity")[0:n, 0:n])
                last.then_inc(*turned.up())

            def values(j):
                h, t = jobs[j]
                n = TILES[t][1]
                pe.wait_ge(*placed.at(j + 1))
                if j > 0:
                    pe.wait_ge(*taken.at(j))
                left = [pT[0:META, 0, 4 * P:4 * P + n]] + [pT[:, 0, (k - 1) * P:k * P] for k in range(1, t + 1)]
                right = [g.f_v[0:TILES[k][1], k, h * FD:(h + 1) * FD] for k in range(t + 1)]
                products(nc, g.psum[0:n, 6, 0:FD], left, right).then_inc(*mixed.up())

            pe.wait_ge(*cums.at(2))
            gate_row(0)
            scores(0)
            for j in range(N):
                h, t = jobs[j]
                if t == 2 and h + 1 < FH:
                    gate_row(h + 1)
                if j + 1 < N:
                    scores(j + 1)
                if j:
                    values(j - 1)
                turn(j)
            values(N - 1)
            if N > 0:
                pe.wait_ge(*taken.at(N))
            for i, t in enumerate(ALLT):
                n = TILES[t][1]
                if 2 * (i - 1) > 0:
                    pe.wait_ge(*o_placed.at(2 * (i - 1)))
                for c in range(KD):
                    last = tr(g.psum[:, 2 * (i % 2) + c // 4, (c % 4) * P:(c % 4) * P + n], g.f_v[0:n, t, c * P:(c + 1) * P], g.c("identity")[0:n, 0:n])
                last.then_inc(*o_turned.up())

        @block.sync
        def _(sp):
            sp.dma_start(bf, g.a["fox_b_f_2"].to_broadcast([P, FH])).then_inc(*bias_in.up(16))
            g.feed(sp, ring_upto)

        @block.scalar
        def _(act):
            act.wait_ge(*gate.at(1))
            nc.scalar.activation(flat(1), flat(1), ACT.Exp, scale=-1.0).then_inc(*achain.up())
            act.wait_ge(*achain.last())
            act.wait_ge(*gate.at(2))
            nc.scalar.activation(flat(1), flat(1), ACT.Ln).then_inc(*achain.up())

            def place_row(h):
                if h >= 2:
                    if 5 * (h - 1) > 0:
                        act.wait_ge(*peaked.at(5 * (h - 1)))
                act.wait_ge(*rows.at(2 * h + 1))
                nc.scalar.activation(row[:, h % 2, META:], g.psum[:, 7, :], ACT.Copy).then_inc(*rows_out.up())
                act.wait_ge(*rows.at(2 * h + 2))
                nc.scalar.activation(row[:, h % 2, 0:META], g.psum[:, 7, 0:META], ACT.Copy).then_inc(*rows_out.up())

            def place(j):
                h, t = jobs[j]
                n = TILES[t][1]
                act.wait_ge(*turned.at(j + 1))
                if j > 0:
                    act.wait_ge(*mixed.at(j))
                first = nc.scalar.activation(pT[0:META, 0, 4 * P:4 * P + n], g.psum[0:META, 5, 0:n], ACT.Copy)
                if t:
                    nc.scalar.activation(pT[:, 0, 0:t * P], g.psum[:, 4, 0:t * P], ACT.Copy).then_inc(*placed.up())
                else:
                    first.then_inc(*placed.up())

            place_row(0)
            for j, (h, t) in enumerate(jobs):
                n, w = TILES[t][1], keys(t)
                act.wait_ge(*peaked.at(j + 1))
                if j - 1 > 0:
                    act.wait_ge(*taken.at(j - 1))
                nc.scalar.activation(sc[0:n, j % 2, 0:w], sc[0:n, j % 2, 0:w], ACT.Exp, bias=peak[0:n, j % 2:j % 2 + 1], accum_out=total[0:n, j % 2:j % 2 + 1]).then_inc(*expd.up())
                if t == 2 and h + 1 < FH:
                    place_row(h + 1)
                place(j)

        @block.vector
        def _(dve):
            v = nc.vector
            dve.wait_ge(*bias_in.at(16))
            v.memset(lf, 0.0).then_inc(*chain.up())
            dve.wait_ge(*chain.last())
            for t in ALLT:
                n = TILES[t][1]
                v.tensor_tensor(flat(0)[0:n, t * FH:(t + 1) * FH], g.f_logit[0:n, t, :], bf[0:n, :], ALU.add).then_inc(*chain.up())
                dve.wait_ge(*chain.last())
            v.tensor_scalar(flat(1), flat(0), -1.0, None, ALU.mult).then_inc(*chain.up())
            dve.wait_ge(*chain.last())
            v.tensor_tensor(flat(1), flat(0), flat(1), ALU.max).then_inc(*gate.up())
            v.memset(ones, 1.0).then_inc(*chain.up())
            v.tensor_scalar(g.f_qT, g.f_qT, FD ** -0.5, None, ALU.mult).then_inc(*chain.up())
            dve.wait_ge(*chain.last())
            dve.wait_ge(*achain.at(1))
            v.tensor_scalar(flat(1), flat(1), 1.0, None, ALU.add).then_inc(*gate.up())
            dve.wait_ge(*achain.at(2))
            v.scalar_tensor_tensor(flat(0), flat(0), 0.0, flat(1), ALU.min, ALU.subtract).then_inc(*gate.up())
            dve.wait_ge(*cums.at(1))
            v.tensor_tensor_scan(cum[0:FH, 0:META], ones[0:FH, 0:META], g.psum[0:FH, 4, 0:META], 0.0, ALU.mult, ALU.add).then_inc(*chain.up())
            dve.wait_ge(*chain.last())
            v.tensor_tensor_scan(cum[0:FH, META:], ones[0:FH, META:], g.psum[0:FH, 5, :], cum[0:FH, META - 1:META], ALU.mult, ALU.add).then_inc(*cums.up())

            def peaks(j):
                h, t = jobs[j]
                n, w = TILES[t][1], keys(t)
                q = peak[0:n, j % 2:j % 2 + 1]
                dve.wait_ge(*scored.at(j + 1))
                dve.wait_ge(*rows_out.at(2 * h + 2))
                if j - 1 > 0:
                    dve.wait_ge(*turned.at(j - 1))
                v.tensor_tensor_reduce(out=sc[0:n, j % 2, 0:w], in0=window(j)[0:n, 496:496 + w], in1=row[0:n, h % 2, 0:w], scale=1.0, scalar=-3e38,
                                            op0=ALU.subtract, op1=ALU.max, accum_out=q).then_inc(*chain.up())
                dve.wait_ge(*chain.last())
                v.tensor_scalar(q, q, -1.0, None, ALU.mult).then_inc(*peaked.up())

            def take(j):
                h, t = jobs[j]
                n = TILES[t][1]
                dve.wait_ge(*mixed.at(j + 1))
                s = total[0:n, j % 2:j % 2 + 1]
                v.reciprocal(s, s).then_inc(*chain.up())
                dve.wait_ge(*chain.last())
                v.tensor_scalar(g.f_v[0:n, t, h * FD:(h + 1) * FD], g.psum[0:n, 6, 0:FD], s, None, ALU.mult).then_inc(*taken.up())

            for j in range(N + 1):
                if j < N:
                    peaks(j)
                if j >= 1:
                    take(j - 1)
            for i, t in enumerate(ALLT):
                a, n = TILES[t]
                for half in range(2):
                    dve.wait_ge(*o_turned.at(i + 1))
                    v.tensor_copy(g.hT[:, 4 * half:4 * half + 4, a:a + n], g.psum[:, 2 * (i % 2) + half, :].rearrange("p (c n) -> p c n", c=4)[:, :, 0:n]).then_inc(*o_placed.up())
    g.top = mark



def moe_layer(g, layer):
    g.top = 0
    keep = g.take(5, D)
    gw = g.take(2, 5)
    dest = g.take(2, 5).bitcast(I32)
    over = g.take(OVER + 1).bitcast(I32)
    stage_norm(g, ALLT, g.a["moe_norm_2"][layer], g.fed, keep)
    stage_route(g, layer, gw, dest, over)
    stage_dispatch(g, keep, dest)
    g.top = keep_top = 5 * D + 10 + 10 + OVER + 1
    g.top += (-g.top) % 8
    stage_experts(g, layer, over)
    g.top = 5 * D + 64
    stage_combine(g, gw, dest)
    g.top = 0


def stage_route(g, layer, gw, dest, over):
    nc = g.nc
    mark = g.top
    loaded, ready, chain, gated, gate_exp, counted, counts_ready, placed = g.sig(
        "router_loaded", "product_ready", "vector_step", "group_shifts", "gate_exps", "assignments_ready", "counts_ready", "logits_placed")
    NL = GROUPS + NEXP
    w = g.take(KD, NL)
    bias = g.take(NL)
    L = g.take(5, NL)
    one = g.take(P)
    gs, ge = g.take(5, GROUPS), g.take(5, GROUPS)
    goh = g.take(5, GROUPS)
    gm, gsum = g.take(5), g.take(5)
    pick = g.take(5, NEXP)
    el, e2 = g.take(5, EPG), g.take(5, EPG)
    oh = g.take(2, 5 * EPG)
    m1, m2, ex, den, idx = (g.take(5) for _ in range(5))
    OH = g.take(2, 5 * NEXP)
    both = g.take(5, NEXP)
    C = g.take(5, NEXP)
    cnt, ovb, inc, base, obase = (g.take(NEXP) for _ in range(5))
    big = g.take(OVER * NEXP)
    t1, t2 = g.take(5, NEXP), g.take(5, NEXP)
    rank, lo, hi, past = (g.take(5) for _ in range(4))
    ovf = g.take(OVER + 1)
    bc = lambda ap, n: ap.unsqueeze(2).to_broadcast([P, 5, n])
    row = lambda ap, n: ap.unsqueeze(1).to_broadcast([P, 5, n])
    with nc.Block() as block:
        @block.tensor
        def _(pe):
            pe.wait_ge(*loaded.at(64))
            for i, t in enumerate(ALLT):
                a, n = TILES[t]
                last = products(nc, g.psum[0:n, i, 0:NL], [g.hT[:, k, a:a + n] for k in range(KD)], [w[:, k, :] for k in range(KD)])
                last.then_inc(*ready.up())
            pe.wait_ge(*counted.at(1))
            for i, t in enumerate(ALLT):
                n = TILES[t][1]
                left = [one[0:TILES[k][1], 0:n] for k in range(t)] + [g.c("before")[0:n, 0:n]]
                products(nc, g.psum[0:n, 5, i * NEXP:(i + 1) * NEXP], left, [both[0:TILES[k][1], k, :] for k in range(t + 1)])
            products(nc, g.psum[:, 6, 0:NEXP], [one[0:TILES[k][1], :] for k in ALLT], [both[0:TILES[k][1], k, :] for k in ALLT]).then_inc(*counts_ready.up())

        @block.sync
        def _(sp):
            sp.dma_start(w[:, :, 0:GROUPS], g.a["moe_w_grp_2"][layer].rearrange("(k p) n -> p k n", p=P), allow_slow_non_contiguous=True).then_inc(*loaded.up(16))
            sp.dma_start(w[:, :, GROUPS:], g.a["moe_w_rt_2"][layer].rearrange("(k p) n -> p k n", p=P)).then_inc(*loaded.up(16))
            sp.dma_start(bias[:, 0:GROUPS], g.a["moe_b_grp_2"][layer:layer + 1].to_broadcast([P, GROUPS])).then_inc(*loaded.up(16))
            sp.dma_start(bias[:, GROUPS:], g.a["moe_b_rt_2"][layer:layer + 1].to_broadcast([P, NEXP])).then_inc(*loaded.up(16))

        @block.scalar
        def _(act):
            act.wait_ge(*gated.at(1))
            nc.scalar.activation(ge, gs, ACT.Exp).then_inc(*gate_exp.up())
            act.wait_ge(*gated.at(2))
            nc.scalar.activation(ex, ex, ACT.Exp).then_inc(*gate_exp.up())

        @block.vector
        def _(dve):
            v = nc.vector
            TT, TS = v.tensor_tensor, v.tensor_scalar

            def first(onehot, values, peak, index, n):
                it = row(g.c("iota")[:, 0:n], n)
                TT(onehot, values, bc(peak, n), ALU.is_equal).then_inc(*chain.up())
                dve.wait_ge(*chain.last())
                TS(onehot, onehot, -1000.0, 1000.0, ALU.mult, ALU.add).then_inc(*chain.up())
                dve.wait_ge(*chain.last())
                TT(onehot, onehot, it, ALU.add).then_inc(*chain.up())
                dve.wait_ge(*chain.last())
                v.tensor_reduce(index, onehot, AX.X, ALU.min).then_inc(*chain.up())
                dve.wait_ge(*chain.last())
                TT(onehot, it, bc(index, n), ALU.is_equal).then_inc(*chain.up())
                dve.wait_ge(*chain.last())

            v.memset(L, 0.0).then_inc(*chain.up())
            dve.wait_ge(*chain.last())
            v.memset(one, 1.0).then_inc(*chain.up())
            dve.wait_ge(*chain.last())
            v.memset(C, 0.0).then_inc(*chain.up())
            dve.wait_ge(*chain.last())
            dve.wait_ge(*loaded.at(64))
            for i, t in enumerate(ALLT):
                n = TILES[t][1]
                dve.wait_ge(*ready.at(i + 1))
                TT(L[0:n, t, :], g.psum[0:n, i, 0:NL], bias[0:n, :], ALU.add).then_inc(*chain.up())
                dve.wait_ge(*chain.last())
            G = L[:, :, 0:GROUPS]
            v.tensor_reduce(gm, G, AX.X, ALU.max).then_inc(*chain.up())
            dve.wait_ge(*chain.last())
            TT(gs, G, bc(gm, GROUPS), ALU.subtract).then_inc(*gated.up())
            first(goh, G, gm, idx, GROUPS)
            E = L[:, :, GROUPS:].rearrange("p t (g e) -> p t g e", g=GROUPS)
            pk = pick.rearrange("p t (g e) -> p t g e", g=GROUPS)
            for t in ALLT:
                TT(pk[:, t, :, :], E[:, t, :, :], goh[:, t, :].unsqueeze(2).to_broadcast([P, GROUPS, EPG]), ALU.mult).then_inc(*chain.up())
                dve.wait_ge(*chain.last())
            v.tensor_reduce(el, pick.rearrange("p t (g e) -> p t e g", g=GROUPS), AX.X, ALU.add).then_inc(*chain.up())
            dve.wait_ge(*chain.last())
            o1 = oh[:, 0, :].rearrange("p (t e) -> p t e", t=5)
            o2 = oh[:, 1, :].rearrange("p (t e) -> p t e", t=5)
            v.tensor_reduce(m1, el, AX.X, ALU.max).then_inc(*chain.up())
            dve.wait_ge(*chain.last())
            first(o1, el, m1, idx, EPG)
            TS(e2, o1, -3e38, None, ALU.mult).then_inc(*chain.up())
            dve.wait_ge(*chain.last())
            TT(e2, e2, el, ALU.add).then_inc(*chain.up())
            dve.wait_ge(*chain.last())
            v.tensor_reduce(m2, e2, AX.X, ALU.max).then_inc(*chain.up())
            dve.wait_ge(*chain.last())
            first(o2, e2, m2, idx, EPG)
            TT(ex, m2, m1, ALU.subtract).then_inc(*gated.up())
            for k, o in enumerate((o1, o2)):
                for t in ALLT:
                    dst = OH[:, k, t * NEXP:(t + 1) * NEXP].rearrange("p (g e) -> p g e", g=GROUPS)
                    TT(dst, goh[:, t, :].unsqueeze(2).to_broadcast([P, GROUPS, EPG]), o[:, t, :].unsqueeze(1).to_broadcast([P, GROUPS, EPG]), ALU.mult).then_inc(*chain.up())
                    dve.wait_ge(*chain.last())
            TT(both.rearrange("p t e -> p (t e)"), OH[:, 0, :], OH[:, 1, :], ALU.add).then_inc(*counted.up())
            dve.wait_ge(*gate_exp.at(2))
            v.tensor_reduce(gsum, ge, AX.X, ALU.add).then_inc(*chain.up())
            dve.wait_ge(*chain.last())
            TS(den, ex, 1.0, None, ALU.add).then_inc(*chain.up())
            dve.wait_ge(*chain.last())
            TT(den, den, gsum, ALU.mult).then_inc(*chain.up())
            dve.wait_ge(*chain.last())
            v.reciprocal(gw[:, 0, :], den).then_inc(*chain.up())
            dve.wait_ge(*chain.last())
            TT(gw[:, 1, :], gw[:, 0, :], ex, ALU.mult).then_inc(*chain.up())
            dve.wait_ge(*chain.last())
            dve.wait_ge(*counts_ready.at(1))
            for i, t in enumerate(ALLT):
                n = TILES[t][1]
                v.tensor_copy(C[0:n, t, :], g.psum[0:n, 5, i * NEXP:(i + 1) * NEXP]).then_inc(*chain.up())
                dve.wait_ge(*chain.last())
            v.tensor_copy(cnt, g.psum[:, 6, 0:NEXP]).then_inc(*chain.up())
            dve.wait_ge(*chain.last())
            bg = big[:, 0:NEXP * 8].rearrange("p (e j) -> p e j", e=NEXP)
            TT(bg, cnt.unsqueeze(2).to_broadcast([P, NEXP, 8]), g.c("steps").unsqueeze(1).to_broadcast([P, NEXP, 8]), ALU.is_gt).then_inc(*chain.up())
            dve.wait_ge(*chain.last())
            v.tensor_reduce(ovb, bg, AX.X, ALU.add).then_inc(*chain.up())
            dve.wait_ge(*chain.last())
            v.tensor_tensor_scan(inc, one[:, 0:NEXP], ovb, 0.0, ALU.mult, ALU.add).then_inc(*chain.up())
            dve.wait_ge(*chain.last())
            TS(base, g.c("iota"), float(ROWS), None, ALU.mult).then_inc(*chain.up())
            dve.wait_ge(*chain.last())
            TT(obase, inc, ovb, ALU.subtract).then_inc(*chain.up())
            dve.wait_ge(*chain.last())
            TS(obase, obase, float(ROWS), float(NEXP * ROWS - ROWS), ALU.mult, ALU.add).then_inc(*chain.up())
            dve.wait_ge(*chain.last())
            for k in range(2):
                oh_k = OH[:, k, :].rearrange("p (t e) -> p t e", t=5)
                for dst, src in ((rank, C), (lo, row(base, NEXP)), (hi, row(obase, NEXP))):
                    TT(t1, oh_k, src, ALU.mult).then_inc(*chain.up())
                    dve.wait_ge(*chain.last())
                    v.tensor_reduce(dst, t1, AX.X, ALU.add).then_inc(*chain.up())
                    dve.wait_ge(*chain.last())
                TS(past, rank, float(ROWS), None, ALU.is_ge).then_inc(*chain.up())
                dve.wait_ge(*chain.last())
                TT(hi, hi, lo, ALU.subtract).then_inc(*chain.up())
                dve.wait_ge(*chain.last())
                TT(hi, hi, past, ALU.mult).then_inc(*chain.up())
                dve.wait_ge(*chain.last())
                TT(lo, lo, hi, ALU.add).then_inc(*chain.up())
                dve.wait_ge(*chain.last())
                TT(lo, lo, rank, ALU.add).then_inc(*chain.up())
                dve.wait_ge(*chain.last())
                v.tensor_copy(dest[:, k, :], lo).then_inc(*chain.up())
                dve.wait_ge(*chain.last())
            bo = big.rearrange("p (j e) -> p j e", j=OVER)
            TT(bo, inc.unsqueeze(1).to_broadcast([P, OVER, NEXP]), g.c("overs").unsqueeze(2).to_broadcast([P, OVER, NEXP]), ALU.is_le).then_inc(*chain.up())
            dve.wait_ge(*chain.last())
            v.tensor_reduce(ovf[:, 0:OVER], bo, AX.X, ALU.add).then_inc(*chain.up())
            dve.wait_ge(*chain.last())
            TS(ovf[:, 0:OVER], ovf[:, 0:OVER], float(NEXP - 1), None, ALU.min).then_inc(*chain.up())
            dve.wait_ge(*chain.last())
            v.tensor_copy(ovf[:, OVER:], inc[:, NEXP - 1:]).then_inc(*chain.up())
            dve.wait_ge(*chain.last())
            v.tensor_copy(over, ovf).then_inc(*placed.up())
    g.top = mark


def stage_dispatch(g, keep, dest):
    nc = g.nc
    sent = g.sig("rows_sent")
    with nc.Block() as block:
        @block.gpsimd
        def _(pool):
            pool.wait_ge(*g.x_rows_zeroed.at(32))
            for k in range(2):
                for t in ALLT:
                    n = TILES[t][1]
                    nc.gpsimd.indirect_dma_start(out=g.a["x_rows"], out_offset=bass.IndirectOffsetOnAxis(ap=dest[0:n, k, t:t + 1], axis=0),
                                                         in_=keep[0:n, t, :], in_offset=None).then_inc(*sent.up(16))
            pool.wait_ge(*sent.last())


def stage_experts(g, layer, over):
    nc = g.nc
    mark = g.top
    names = ["gain_loaded", "rows_loaded", "up_loaded_0", "up_loaded_1", "down_loaded_0", "down_loaded_1", "rows_transposed", "rows_placed", "up_ready",
             "gated", "gate_silu", "hidden_transposed", "hidden_placed", "down_ready", "result_placed", "result_free_0", "result_free_1"]
    gain_in, x_in, up_in0, up_in1, dn_in0, dn_in1, x_turned, x_placed, up_ready, hid, silu, h_turned, h_placed, dn_ready, y_placed, y_free0, y_free1 = g.sig(*names)
    up_in, dn_in, y_free = (up_in0, up_in1), (dn_in0, dn_in1), (y_free0, y_free1)
    gain = g.take(KD)
    up = [g.ring[:, 0:2, :].rearrange("p a (k n) -> p (a k) n", k=4), g.take(KD, D)]
    down = [g.ring[:, 2 + n, :].rearrange("p (k n) -> p k n", k=4) for n in range(2)]
    x = g.hT[:, 0:2, 0:512]
    xT = g.hT[:, 2:4, 0:512].rearrange("p a (k r) -> p a k r", k=4)
    s = g.hT[:, 6, 0:256]
    act_ = g.hT[:, 6, 256:512]
    aT = g.hT[:, 7, 0:256].rearrange("p (j r) -> p j r", j=2)
    y = [g.take(512), g.take(512)]
    wu, wd = g.a["moe_w_up_2"], g.a["moe_w_down_2"]
    xr, yr = g.a["x_rows"], g.a["y_rows"]
    PAIRS = NEXP // 2

    def load_rows(sp, blk, rows):
        return sp.dma_start(x[0:rows, :, :], xr[bass.ds(blk * ROWS, rows)].rearrange("r (a c) -> r a c", a=2))

    def load_up(sp, e, n):
        return sp.dma_start(up[n], wu[layer][bass.ds(e, 1)].rearrange("a (k p) f -> p (a k) f", p=P))

    def load_down(sp, e, n):
        return sp.dma_start(down[n], wd[layer][bass.ds(e, 1)].rearrange("a (k p) f -> p (a k) f", p=P))

    def tensor_rows():
        for c in range(KD):
            last = nc.tensor.transpose(g.psum[:, c // 4, (c % 4) * P:(c % 4 + 1) * P], x[:, c // 4, (c % 4) * P:(c % 4 + 1) * P], g.c("identity"))
        return last

    def place_rows():
        for a in range(2):
            last = nc.vector.tensor_tensor(xT[:, a, :, :], g.psum[:, a, :].rearrange("p (k r) -> p k r", k=4), gain[:, 4 * a:4 * a + 4].unsqueeze(2).to_broadcast([P, 4, P]), ALU.mult)
        return last

    def tensor_up(n):
        wv = up[n].rearrange("p k (s q c) -> p k q s c", s=2, q=2)
        for k in range(KD):
            for q in range(2):
                last = nc.tensor.matmul(g.psum[64 * q:64 * q + 64, 2 + n, :].rearrange("p (s c) -> p s c", s=2), xT[:, k // 4, k % 4, ROWS * n:ROWS * n + ROWS], wv[:, k, q, :, :], start=k == 0, stop=k == KD - 1)
        return last

    def tensor_hidden():
        for j in range(2):
            last = nc.tensor.transpose(g.psum[:, 4, j * P:(j + 1) * P], act_[:, j * P:(j + 1) * P], g.c("identity"))
        return last

    def tensor_down(n):
        for k in range(4):
            for q in range(2):
                last = nc.tensor.matmul(g.psum[64 * q:64 * q + 64, 6 + n, :], aT[:, k % 2, 64 * (k // 2):64 * (k // 2) + 64], down[n][:, k, 512 * q:512 * q + 512], start=k == 0, stop=k == 3)
        return last

    def store(eng, blk, n):
        rows = yr[bass.ds(blk * ROWS, ROWS)]
        a = eng.dma_start(rows[:, 0:512], y[n][0:64, :])
        b = eng.dma_start(rows[:, 512:], y[n][64:128, :])
        return a, b

    with nc.Block() as block:
        @block.sync
        def _(sp):
            sp.dma_start(gain, g.a["moe_norm_2"][layer].rearrange("(k p) -> p k", p=P), allow_slow_non_contiguous=True).then_inc(*gain_in.up(16))
            load_rows(sp, 0, P).then_inc(x_in.sem, 16)
            for n in range(2):
                load_up(sp, n, n).then_inc(up_in[n].sem, 16)
                load_down(sp, n, n).then_inc(dn_in[n].sem, 16)
            with sp.Fori(1, PAIRS) as i:
                sp.wait_ge(x_turned.sem, i + x_turned.base)
                load_rows(sp, 2 * i, P).then_inc(x_in.sem, 16)
                for n in range(2):
                    sp.wait_ge(up_ready.sem, 2 * i + (up_ready.base + n - 1))
                    load_up(sp, 2 * i + n, n).then_inc(up_in[n].sem, 16)
                    sp.wait_ge(dn_ready.sem, 2 * i + (dn_ready.base + n - 1))
                    load_down(sp, 2 * i + n, n).then_inc(dn_in[n].sem, 16)

        @block.tensor
        def _(pe):
            with pe.Fori(0, PAIRS) as i:
                pe.wait_ge(x_in.sem, 16 * i + (x_in.base + 16))
                tensor_rows().then_inc(x_turned.sem, 1)
                pe.wait_ge(x_placed.sem, i + (x_placed.base + 1))
                for n in range(2):
                    pe.wait_ge(up_in[n].sem, 16 * i + (up_in[n].base + 16))
                    tensor_up(n).then_inc(up_ready.sem, 1)
                    pe.wait_ge(hid.sem, 2 * i + (hid.base + n + 1))
                    tensor_hidden().then_inc(h_turned.sem, 1)
                    pe.wait_ge(h_placed.sem, 2 * i + (h_placed.base + n + 1))
                    pe.wait_ge(dn_in[n].sem, 16 * i + (dn_in[n].base + 16))
                    tensor_down(n).then_inc(dn_ready.sem, 1)

        @block.scalar
        def _(act):
            with act.Fori(0, PAIRS) as i:
                for n in range(2):
                    act.wait_ge(up_ready.sem, 2 * i + (up_ready.base + n + 1))
                    nc.scalar.activation(s, g.psum[:, 2 + n, 0:256], ACT.Silu).then_inc(silu.sem, 1)
                    act.wait_ge(h_turned.sem, 2 * i + (h_turned.base + n + 1))
                    nc.scalar.activation(aT.rearrange("p j r -> p (j r)"), g.psum[:, 4, 0:256], ACT.Copy).then_inc(h_placed.sem, 1)
                    act.wait_ge(y_placed.sem, 2 * i + (y_placed.base + n + 1))
                    for ins in store(act, 2 * i + n, n):
                        ins.then_inc(y_free[n].sem, 16)
            for n in range(2):
                act.wait_ge(y_free[n].sem, y_free[n].base + 1 + 32 * PAIRS)

        @block.vector
        def _(dve):
            dve.wait_ge(*gain_in.at(16))
            for n in range(2):
                nc.vector.memset(y[n], 0.0).then_inc(y_free[n].sem, 1)
            with dve.Fori(0, PAIRS) as i:
                dve.wait_ge(x_turned.sem, i + (x_turned.base + 1))
                place_rows().then_inc(x_placed.sem, 1)
                for n in range(2):
                    dve.wait_ge(silu.sem, 2 * i + (silu.base + n + 1))
                    nc.vector.tensor_tensor(act_, s, g.psum[:, 2 + n, 256:512], ALU.mult).then_inc(hid.sem, 1)
                    dve.wait_ge(dn_ready.sem, 2 * i + (dn_ready.base + n + 1))
                    dve.wait_ge(y_free[n].sem, 32 * i + (y_free[n].base + 1))
                    nc.vector.tensor_copy(y[n], g.psum[:, 6 + n, :]).then_inc(y_placed.sem, 1)
    for sig in (x_in, up_in0, up_in1, dn_in0, dn_in1):
        sig.count = 16 * PAIRS
    x_turned.count = x_placed.count = PAIRS
    for sig in (up_ready, hid, silu, h_turned, h_placed, dn_ready, y_placed):
        sig.count = NEXP
    for sig in y_free:
        sig.count = 1 + 32 * PAIRS

    if not g.over_sems:
        g.over_sems = [g.sem("over_" + n) for n in ("done", "rows", "up", "down", "rows_T", "rows_placed", "up_ready", "silu", "gated", "hidden_T", "hidden_placed", "down_ready", "placed", "stored")]
    done, rows_l, up_l, down_l, rT, rp, ur, si, ga, hT_, hp, dr, pl, st = g.over_sems
    with nc.Block() as block:
        def each(eng, body):
            count = eng.value_load(over[0:1, OVER:OVER + 1], min_val=0, max_val=OVER)
            with eng.Fori(0, OVER) as j:
                with eng.If(j < count):
                    body(j)

        @block.sync
        def _(sp):
            def body(j):
                e = sp.value_load(over[0:1, bass.ds(j, 1)], min_val=0, max_val=NEXP - 1)
                sp.wait_ge(done, j + 1)
                load_rows(sp, j + NEXP, ROWS).then_inc(rows_l, 16)
                load_up(sp, e, 0).then_inc(up_l, 16)
                load_down(sp, e, 0).then_inc(down_l, 16)
            each(sp, body)

        @block.tensor
        def _(pe):
            def body(j):
                pe.wait_ge(rows_l, 16 * j + 16)
                tensor_rows().then_inc(rT, 1)
                pe.wait_ge(rp, j + 1)
                pe.wait_ge(up_l, 16 * j + 16)
                tensor_up(0).then_inc(ur, 1)
                pe.wait_ge(ga, j + 1)
                tensor_hidden().then_inc(hT_, 1)
                pe.wait_ge(hp, j + 1)
                pe.wait_ge(down_l, 16 * j + 16)
                tensor_down(0).then_inc(dr, 1)
            each(pe, body)

        @block.scalar
        def _(act):
            def body(j):
                act.wait_ge(ur, j + 1)
                nc.scalar.activation(s, g.psum[:, 2, 0:256], ACT.Silu).then_inc(si, 1)
                act.wait_ge(hT_, j + 1)
                nc.scalar.activation(aT.rearrange("p j r -> p (j r)"), g.psum[:, 4, 0:256], ACT.Copy).then_inc(hp, 1)
                act.wait_ge(pl, j + 1)
                for ins in store(act, j + NEXP, 0):
                    ins.then_inc(st, 16)
                act.wait_ge(st, 32 * j + 32)
                act.sem_inc(done, 1)
            each(act, body)

        @block.vector
        def _(dve):
            nc.vector.memset(y[0], 0.0).then_inc(done, 1)

            def body(j):
                dve.wait_ge(rT, j + 1)
                place_rows().then_inc(rp, 1)
                dve.wait_ge(si, j + 1)
                nc.vector.tensor_tensor(act_, s, g.psum[:, 2, 256:512], ALU.mult).then_inc(ga, 1)
                dve.wait_ge(dr, j + 1)
                nc.vector.tensor_copy(y[0], g.psum[:, 6, :]).then_inc(pl, 1)
            each(dve, body)

    with nc.Block() as block:
        @block.sync
        def _(sp):
            for sem in g.over_sems:
                sp.sem_clear(sem)
    g.top = mark


def stage_combine(g, gw, dest):
    nc = g.nc
    added = g.sig("results_added")
    yb = g.take(10, D)
    jobs = [(t, k) for t in ALLT for k in range(2)]
    if not g.gather_sems:
        g.gather_sems = [g.sem(f"gathered_{n}") for n in range(10)]
    g.gathers += 1
    with nc.Block() as block:
        @block.gpsimd
        def _(pool):
            for n, (t, k) in enumerate(jobs):
                r = TILES[t][1]
                nc.gpsimd.indirect_dma_start(out=yb[0:r, n, :], out_offset=None, in_=g.a["y_rows"],
                                             in_offset=bass.IndirectOffsetOnAxis(ap=dest[0:r, k, t:t + 1], axis=0)).then_inc(g.gather_sems[n], 16)

        @block.vector
        def _(dve):
            for n, (t, k) in enumerate(jobs):
                r = TILES[t][1]
                dve.wait_ge(g.gather_sems[n], 16 * g.gathers)
                if n > 0:
                    dve.wait_ge(*added.at(n))
                nc.vector.scalar_tensor_tensor(g.h[0:r, t, :], yb[0:r, n, :], gw[0:r, k, t:t + 1], g.h[0:r, t, :], ALU.mult, ALU.add).then_inc(*added.up())


def plan_hg(g):
    w = g.a["hg_w_in_2"][0]
    chunks = [g.plan(w[:, 512 * n:512 * n + 512], KD, 512) for n in range(8)]
    out = [g.plan(g.a["hg_w_out_2"][0][:, 512 * n:512 * n + 512], KD, 512) for n in range(2)]
    return chunks, out


def hg_layer(g, plans):
    chunks, out = plans
    g.top = 0
    stage_norm(g, ALLT, g.a["hg_norm_2"][0], chunks[0] + 4)
    stage_hg_in(g, chunks, out[0] + 1)
    stage_hg_scores(g, out)
    stage_hg_scan(g, out)
    stage_out(g, ALLT, out, out[0] + 2)
    g.top = 0


def stage_hg_in(g, chunks, ring_upto):
    nc = g.nc
    ready, freed, loaded, bound, exps, sig, kept, logs, chain, vfreed = g.sig("product_ready", "bank_read_by_scalar", "gate_weights_loaded", "bound_steps", "bound_exps", "forget_sigmoids", "keys_ready",
                                                                              "log_gates", "vector_step", "bank_read_by_vector")
    g.g_q, g.g_k, g.g_b = g.take(HG, TOKENS), g.take(HG, TOKENS), g.take(HG, TOKENS)
    g.g_v, g.g_g = g.take(5, D), g.take(5, D)
    bf = g.small[:, 400:408]
    lbl = g.small[:, 408:424].rearrange("p (l k) -> p l k", l=2)
    lb, oml = g.small[:, 424:432], g.small[:, 432:440]
    mx = g.small[:, 440:448]
    units = [("q", f // 4, f) for f in range(8)] + [("f", 2 + f // 4, f) for f in range(8)]
    units += [(kind, c, t) for kind, c in (("v", 4), ("v", 5), ("g", 6), ("g", 7)) for t in ALLT]
    window = lambda u: g.psum[:, 2 * (u % 4):2 * (u % 4) + 2, :].rearrange("p b n -> p (b n)")
    order, na, nv = [], 0, 0
    for kind, *_ in units:
        if kind == "v":
            nv += 1
            order.append((vfreed, nv))
        else:
            na += 1
            order.append((freed, na))
    with nc.Block() as block:
        @block.tensor
        def _(pe):
            for u, (kind, c, x) in enumerate(units):
                if u == 0 or units[u - 1][1] != c:
                    g.weights_wait(pe, chunks[c])
                if u >= 4:
                    pe.wait_ge(*order[u - 4][0].at(order[u - 4][1]))
                if kind in "qf":
                    w = g.weights(chunks[c])
                    left = [w[:, k, (x % 4) * P:(x % 4 + 1) * P] for k in range(KD)]
                    products(nc, window(u)[:, 496:512], left, [g.hT[:, k, 0:META] for k in range(KD)])
                    products(nc, window(u)[:, 512:1024], left, [g.hT[:, k, META:] for k in range(KD)]).then_inc(*ready.up())
                else:
                    n = TILES[x][1]
                    rows_by_weights(g, pe, window(u)[0:n, 0:512], x, chunks[c]).then_inc(*ready.up())
                if u + 1 == len(units) or units[u + 1][1] != c:
                    g.chunk_used(chunks[c], ready)

        @block.sync
        def _(sp):
            sp.dma_start(bf, g.a["hg_b_f_2"].rearrange("a (k p) -> p (a k)", p=P), allow_slow_non_contiguous=True).then_inc(*loaded.up(16))
            for n in range(2):
                sp.dma_start(lbl[:, n, :], g.a["hg_lb_logits_2"][n].rearrange("(k p) -> p k", p=P), allow_slow_non_contiguous=True).then_inc(*loaded.up(16))
            g.feed(sp, ring_upto)

        @block.scalar
        def _(act):
            act.wait_ge(*bound.at(1))
            nc.scalar.activation(lbl, lbl, ACT.Exp).then_inc(*exps.up())
            for u, (kind, c, x) in enumerate(units):
                if kind == "v":
                    continue
                act.wait_ge(*ready.at(u + 1))
                if kind == "q":
                    nc.scalar.activation(g.g_q[:, x, :], window(u)[:, 496:1024], ACT.Silu).then_inc(*freed.up())
                elif kind == "f":
                    nc.scalar.activation(g.g_k[:, x, :], window(u)[:, 496:1024], ACT.Sigmoid, bias=bf[:, x:x + 1]).then_inc(*sig.up())
                    nc.scalar.activation(g.g_b[:, x, 0:1], window(u)[:, 496:497], ACT.Copy).then_inc(*freed.up())
                else:
                    n = TILES[x][1]
                    nc.scalar.activation(g.g_g[0:n, x, 512 * (c - 6):512 * (c - 5)], window(u)[0:n, 0:512], ACT.Silu).then_inc(*freed.up())
            act.wait_ge(*kept.at(8))
            nc.scalar.activation(g.g_b, g.g_b, ACT.Ln).then_inc(*logs.up())

        @block.vector
        def _(dve):
            v = nc.vector
            dve.wait_ge(*loaded.at(48))
            v.tensor_tensor(mx, lbl[:, 0, :], lbl[:, 1, :], ALU.max).then_inc(*chain.up())
            dve.wait_ge(*chain.last())
            v.tensor_tensor(lbl, lbl, mx.unsqueeze(1).to_broadcast([P, 2, KD]), ALU.subtract).then_inc(*bound.up())
            dve.wait_ge(*exps.at(1))
            v.tensor_tensor(mx, lbl[:, 0, :], lbl[:, 1, :], ALU.add).then_inc(*chain.up())
            dve.wait_ge(*chain.last())
            v.reciprocal(mx, mx).then_inc(*chain.up())
            dve.wait_ge(*chain.last())
            v.tensor_tensor(lb, lbl[:, 1, :], mx, ALU.mult).then_inc(*chain.up())
            dve.wait_ge(*chain.last())
            v.tensor_scalar(oml, lb, -1.0, 1.0, ALU.mult, ALU.add).then_inc(*chain.up())
            dve.wait_ge(*chain.last())
            for x in range(8):
                dve.wait_ge(*sig.at(x + 1))
                dve.wait_ge(*freed.at(8 + x + 1))
                v.tensor_scalar(g.g_b[:, x, :], g.g_k[:, x, :], oml[:, x:x + 1], lb[:, x:x + 1], ALU.mult, ALU.add).then_inc(*chain.up())
                dve.wait_ge(*chain.last())
                v.tensor_scalar(g.g_k[:, x, :], g.g_b[:, x, :], -1.0, 1.0, ALU.mult, ALU.add).then_inc(*kept.up())
            for u, (kind, c, x) in enumerate(units):
                if kind == "v":
                    n = TILES[x][1]
                    dve.wait_ge(*ready.at(u + 1))
                    v.tensor_copy(g.g_v[0:n, x, 512 * (c - 4):512 * (c - 3)], window(u)[0:n, 0:512]).then_inc(*vfreed.up())
            dve.wait_ge(*logs.at(1))
            for x in range(8):
                v.tensor_tensor_scan(g.g_b[:, x, :], g.c("carry"), g.g_b[:, x, :], 0.0, ALU.mult, ALU.add).then_inc(*chain.up())
            dve.wait_ge(*chain.last())


def stage_hg_scores(g, out):
    nc = g.nc
    spare = g.ring[:, (out[0] + 2) % 4, :]
    cut = lambda n: spare[:, n * TOKENS:(n + 1) * TOKENS]
    diff, xx, masked = [cut(0), cut(1)], [cut(2), cut(3)], [cut(4), cut(5)]
    subbed, exped, built, producted, maskd, added, applied = g.sig("exponents_ready", "decays_exped", "operands_ready", "product_ready", "scores_masked", "scores_added", "decays_applied")
    A = g.hT
    DIAG, QE, KE = 7, 8, 9
    jobs = [(h, n) for h in range(HG) for n in range(10)]
    N = len(jobs)
    lev = [j for j, (h, n) in enumerate(jobs) if n < 7]
    prod = [j for j, (h, n) in enumerate(jobs) if n <= DIAG]
    subs = [j for j, (h, n) in enumerate(jobs) if n < 7 or n == KE]
    exps = [j for j, (h, n) in enumerate(jobs) if n != DIAG]
    rank = lambda seq, j: sum(1 for x in seq if x < j)
    window = lambda i: g.psum[:, 2 * (i % 2):2 * (i % 2) + 2, :].rearrange("p b n -> p (b n)")

    def halves(ap, n):
        lo = 0 if n < 4 else META
        return ap[:, lo:].rearrange("p (g two b) -> p g two b", two=2, b=1 << n)

    def built_wait(eng, j):
        if j < 0 or jobs[j][1] == DIAG:
            return
        if jobs[j][1] < 7:
            eng.wait_ge(*built.at(2 * rank(lev, j) + 2))
        else:
            if 2 * jobs[j][0] + jobs[j][1] - QE + 1 > 0:
                eng.wait_ge(*applied.at(2 * jobs[j][0] + jobs[j][1] - QE + 1))

    def added_wait(eng, i):
        if i < 0:
            return
        n = 0
        for j in prod[:i + 1]:
            level = jobs[j][1]
            n += 0 if level == 0 else 2 if level < 4 or level == DIAG else 1
        if n > 0:
            eng.wait_ge(*added.at(n))

    with nc.Block() as block:
        @block.gpsimd
        def _(pool):
            op = nc.gpsimd.tensor_tensor

            def add(i):
                h, n = jobs[prod[i]]
                pool.wait_ge(*maskd.at(i + 1))
                m = masked[i % 2]
                lo = 0 if n < 4 or n == DIAG else META
                if n == 0:
                    return
                pool.wait_ge(*added.last())
                if lo == 0:
                    op(A[0:META, h, 0:META], A[0:META, h, 0:META], m[0:META, 0:META], ALU.add).then_inc(*added.up())
                    op(A[:, h, META:], A[:, h, META:], m[:, META:], ALU.add).then_inc(*added.up())
                else:
                    op(A[:, h, META:], A[:, h, META:], m[:, META:], ALU.add).then_inc(*added.up())

            done = 0
            for j, (h, n) in enumerate(jobs):
                d, b = diff[j % 2], g.g_b[:, h, :]
                if n < 7 or n == KE:
                    if j >= 2:
                        built_wait(pool, j - 2)
                    if n < 7:
                        dv, bv = halves(d, n), halves(b, n)
                        mid = bv[:, :, 0, (1 << n) - 1:1 << n].to_broadcast(list(bv[:, :, 0, :].shape))
                        op(dv[:, :, 0, :], mid, bv[:, :, 0, :], ALU.subtract).then_inc(*subbed.up())
                        op(dv[:, :, 1, :], bv[:, :, 1, :], mid, ALU.subtract).then_inc(*subbed.up())
                    else:
                        op(d[:, 0:META], b[:, META - 1:META].to_broadcast([P, META]), b[:, 0:META], ALU.subtract).then_inc(*subbed.up())
                        bm = b[:, META:].rearrange("p (t n) -> p t n", t=4)
                        op(d[:, META:].rearrange("p (t n) -> p t n", t=4), bm[:, :, P - 1:P].to_broadcast([P, 4, P]), bm, ALU.subtract).then_inc(*subbed.up())
                while done < len(prod) and prod[done] <= j - 3:
                    add(done)
                    done += 1
            while done < len(prod):
                add(done)
                done += 1
            if added.count:
                pool.wait_ge(*added.last())

        @block.scalar
        def _(act):
            for j, (h, n) in enumerate(jobs):
                if n == DIAG:
                    continue
                d = diff[j % 2]
                if n == QE:
                    built_wait(act, j - 2)
                    nc.scalar.activation(d, g.g_b[:, h, :], ACT.Exp).then_inc(*exped.up())
                else:
                    lo = 0 if n < 4 or n == KE else META
                    act.wait_ge(*subbed.at(2 * rank(subs, j) + 2))
                    nc.scalar.activation(d[:, lo:], d[:, lo:], ACT.Exp).then_inc(*exped.up())

        @block.vector
        def _(dve):
            v = nc.vector

            def mask(i):
                h, n = jobs[prod[i]]
                name = "identity" if n == DIAG else f"half{n}"
                dve.wait_ge(*producted.at(i + 1))
                added_wait(dve, i - 2)
                dst = A[:, h, :] if n == 0 else masked[i % 2]
                main = lambda ap: ap[:, META:].rearrange("p (t n) -> p t n", t=4)
                if n < 4 or n == DIAG:
                    v.tensor_tensor(dst[0:META, 0:META], window(i)[0:META, 496:512], g.c(name)[0:META, 0:META], ALU.mult)
                v.tensor_tensor(main(dst), window(i)[:, 512:].rearrange("p (t n) -> p t n", t=4), g.c(name).unsqueeze(1).to_broadcast([P, 4, P]), ALU.mult).then_inc(*maskd.up())

            done = 0
            for j, (h, n) in enumerate(jobs):
                d = diff[j % 2]
                if n < 7:
                    dve.wait_ge(*exped.at(rank(exps, j) + 1))
                    i = rank(lev, j)
                    if i >= 2:
                        if rank(prod, lev[i - 2]) + 1 > 0:
                            dve.wait_ge(*producted.at(rank(prod, lev[i - 2]) + 1))
                    dv, xv = halves(d, n), halves(xx[i % 2], n)
                    v.tensor_tensor(xv[:, :, 0, :], dv[:, :, 0, :], halves(g.g_k[:, h, :], n)[:, :, 0, :], ALU.mult).then_inc(*built.up())
                    v.tensor_tensor(xv[:, :, 1, :], dv[:, :, 1, :], halves(g.g_q[:, h, :], n)[:, :, 1, :], ALU.mult).then_inc(*built.up())
                elif n == QE or n == KE:
                    dve.wait_ge(*exped.at(rank(exps, j) + 1))
                    if rank(prod, j) > 0:
                        dve.wait_ge(*producted.at(rank(prod, j)))
                    x = g.g_q if n == QE else g.g_k
                    v.tensor_tensor(x[:, h, :], x[:, h, :], d, ALU.mult).then_inc(*applied.up())
                while done < len(prod) and prod[done] <= j - 1:
                    mask(done)
                    done += 1
            while done < len(prod):
                mask(done)
                done += 1

        @block.tensor
        def _(pe):
            for i, j in enumerate(prod):
                h, n = jobs[j]
                if i - 1 > 0:
                    pe.wait_ge(*maskd.at(i - 1))
                if n == DIAG:
                    left, right, tiles = g.g_k[:, h, :], g.g_q[:, h, :], ALLT
                else:
                    pe.wait_ge(*built.at(2 * rank(lev, j) + 2))
                    left = right = xx[rank(lev, j) % 2]
                    tiles = ALLT if n < 4 else XT
                for t in tiles:
                    a, m = TILES[t]
                    out_ = window(i)[0:META, 496:512] if t == 0 else window(i)[:, 512 + (t - 1) * P:512 + t * P]
                    last = nc.tensor.matmul(out_, left[:, a:a + m], right[:, a:a + m], start=True, stop=True)
                last.then_inc(*producted.up())

        @block.sync
        def _(sp):
            g.feed(sp, out[0] + 2)


def stage_hg_scan(g, out):
    nc = g.nc
    spare = g.ring[:, (out[0] + 3) % 4, :]
    cut = lambda n: spare[:, n * D:(n + 1) * D].rearrange("p (h d) -> p h d", h=HG)
    S, kT, o, osq = (cut(n) for n in range(4))
    eb = g.small[:, 450:490].rearrange("p (h t) -> p h t", h=HG)
    so = g.small[:, 490:498]
    gain = g.ring[:, (out[0] + 2) % 4, 0:P]
    chain, exped, kturned, kplaced, outs, upds, state, summed, gchain, rooted, normed, turned, moved, gained = g.sig(
        "vector_step", "decays_exped", "keys_transposed", "keys_placed", "outputs_ready", "updates_ready", "state_ready", "heads_summed",
        "gpsimd_step", "norm_ready", "rows_normed", "rows_transposed", "transposed_moved", "gains_loaded")
    pair = lambda n, m: g.psum[0:m, n:n + 2, :].rearrange("p b (h d) -> p (b h) d", d=P)
    with nc.Block() as block:
        @block.tensor
        def _(pe):
            mm, tr = nc.tensor.matmul, nc.tensor.transpose

            def finish(t):
                a, n = TILES[t]
                pe.wait_ge(*normed.at(t + 1))
                for c in range(KD):
                    last = tr(g.psum[:, 6 + c // 4, (c % 4) * P:(c % 4) * P + n], o[0:n, c, :], g.c("identity")[0:n, 0:n])
                last.then_inc(*turned.up())

            for t in ALLT:
                a, n = TILES[t]
                if t:
                    if 2 * t > 0:
                        pe.wait_ge(*kplaced.at(2 * t))
                    pe.wait_ge(*state.at(t + 1))
                else:
                    pe.wait_ge(*state.at(1))
                for h in range(HG):
                    last = tr(pair(0, n)[:, h, :], g.g_k[:, h, a:a + n], g.c("identity"))
                last.then_inc(*kturned.up())
                for h in range(HG):
                    mm(pair(2, n)[:, h, :], g.hT[0:n, h, a:a + n], g.g_v[0:n, t, h * P:(h + 1) * P], start=True, stop=False)
                    last = mm(pair(2, n)[:, h, :], g.g_q[:, h, a:a + n], S[:, h, :], start=False, stop=True)
                last.then_inc(*outs.up())
                pe.wait_ge(*kplaced.at(2 * t + 2))
                for h in range(HG):
                    last = mm(pair(4, P)[:, h, :], kT[0:n, h, :], g.g_v[0:n, t, h * P:(h + 1) * P], start=True, stop=True)
                last.then_inc(*upds.up())
                finish(t)

        @block.sync
        def _(sp):
            sp.dma_start(gain, g.a["hg_o_norm_2"].to_broadcast([P, P])).then_inc(*gained.up(16))

        @block.scalar
        def _(act):
            b = g.g_b
            nc.scalar.activation(eb[:, :, 0], b[:, :, META - 1], ACT.Exp).then_inc(*exped.up())
            nc.scalar.activation(eb[:, :, 1:5], b[:, :, META + P - 1::P], ACT.Exp).then_inc(*exped.up())
            for t in ALLT:
                a, n = TILES[t]
                act.wait_ge(*kturned.at(t + 1))
                if t:
                    if t > 0:
                        act.wait_ge(*upds.at(t))
                for half in range(2):
                    nc.scalar.activation(kT[0:n, 4 * half:4 * half + 4, :], pair(0, n)[:, 4 * half:4 * half + 4, :], ACT.Copy).then_inc(*kplaced.up())

        @block.gpsimd
        def _(pool):
            for t in ALLT:
                n = TILES[t][1]
                pool.wait_ge(*summed.at(t + 1))
                inverse_root(g, pool, so[0:n, :], so[0:n, :], 1.0 / P, gchain, rooted)

        @block.vector
        def _(dve):
            v = nc.vector
            v.memset(S, 0.0).then_inc(*state.up())
            dve.wait_ge(*state.at(1))
            dve.wait_ge(*exped.at(2))
            dve.wait_ge(*gained.at(16))
            for t in ALLT:
                a, n = TILES[t]
                dve.wait_ge(*outs.at(t + 1))
                if t:
                    if t > 0:
                        dve.wait_ge(*turned.at(t))
                for half in range(2):
                    v.tensor_copy(o[0:n, 4 * half:4 * half + 4, :], pair(2, n)[:, 4 * half:4 * half + 4, :]).then_inc(*chain.up())
                v.tensor_tensor(S, S, eb[:, :, t:t + 1].to_broadcast([P, HG, P]), ALU.mult).then_inc(*chain.up())
                dve.wait_ge(*chain.last())
                dve.wait_ge(*upds.at(t + 1))
                v.tensor_tensor(S[:, 0:4, :], S[:, 0:4, :], pair(4, P)[:, 0:4, :], ALU.add).then_inc(*chain.up())
                dve.wait_ge(*chain.last())
                v.tensor_tensor(S[:, 4:8, :], S[:, 4:8, :], pair(4, P)[:, 4:8, :], ALU.add).then_inc(*state.up())
                on = o[0:n, :, :]
                v.tensor_tensor(osq[0:n, :, :], on, on, ALU.mult).then_inc(*chain.up())
                dve.wait_ge(*chain.last())
                v.tensor_reduce(so[0:n, :], osq[0:n, :, :], AX.X, ALU.add).then_inc(*summed.up())
                dve.wait_ge(*rooted.at(t + 1))
                v.tensor_tensor(on, on, so[0:n, :].unsqueeze(2).to_broadcast([n, HG, P]), ALU.mult).then_inc(*chain.up())
                dve.wait_ge(*chain.last())
                v.tensor_tensor(on, on, gain[0:n, :].unsqueeze(1).to_broadcast([n, HG, P]), ALU.mult).then_inc(*chain.up())
                dve.wait_ge(*chain.last())
                v.tensor_tensor(on, on, g.g_g[0:n, t, :].rearrange("p (h d) -> p h d", h=HG), ALU.mult).then_inc(*normed.up())
                dve.wait_ge(*turned.at(t + 1))
                for half in range(2):
                    v.tensor_copy(g.hT[:, 4 * half:4 * half + 4, a:a + n], g.psum[:, 6 + half, :].rearrange("p (c m) -> p c m", c=4)[:, :, 0:n]).then_inc(*chain.up())
                dve.wait_ge(*chain.last())


def plan_first_half(g):
    a = g.a
    even = [g.plan(a["ev_w_in"][0][:, 0:512], KD, 512)] + [g.plan(a["ev_w_in"][0][:, 512 + 384 * n:896 + 384 * n], KD, 384) for n in range(8)]
    even_out = [g.plan(a["ev_w_out"][0][:, 512 * n:512 * n + 512], KD, 512) for n in range(2)]
    return even, even_out


def plan_ple(g, layer):
    proj = g.plan(g.a["ple_w_proj"][layer], 2, D)
    return [g.plan(g.a["ple_w_gate"][layer][:, 512 * n:512 * n + 512], KD, 512) for n in range(2)], proj


def build(nc, a, const_at):
    with ExitStack() as ctx:
        g = Program(nc, ctx, a, const_at)
        plans = {}
        plans["even"] = plan_first_half(g)
        plans["ple0"] = plan_ple(g, 0)
        plans["odd"] = plan_odd(g)
        plans["ple1"] = plan_ple(g, 1)
        plans["fox"] = plan_fox(g)
        plans["hg"] = plan_hg(g)
        stage_load(g)
        even, even_out = plans["even"]
        stage_norm(g, XT, a["norm_g"][0], even[3])
        stage_even_in(g, even, even_out[0] + 2)
        stage_pool(g, even_out[0] + 3)
        stage_even_attention(g, even_out[0] + 4)
        stage_out(g, XT, even_out, even_out[1] + 4)
        g.top = 0
        gate, proj = plans["ple0"]
        stage_norm(g, XT, None, g.fed)
        stage_ple(g, 0, gate, proj, gate[1] + 4)
        odd_layer(g, plans["odd"])
        gate, proj = plans["ple1"]
        stage_norm(g, XT, None, g.fed)
        stage_ple(g, 1, gate, proj, gate[1] + 4)
        fox_layer(g, plans["fox"])
        moe_layer(g, 0)
        hg_layer(g, plans["hg"])
        moe_layer(g, 1)
        stage_store(g)


def stage_store(g):
    stored = g.sig("output_stored")
    with g.nc.Block() as block:
        @block.sync
        def _(sp):
            sp.dma_start(g.a["out"].rearrange("b (t p) d -> p (b t) d", p=P), g.h[:, 1:5, :]).then_inc(*stored.up(16))
            sp.wait_ge(*stored.last())
            sp.wait_ge(*g.x_rows_zeroed.at(32))


_INS = ["x", "positions", "norm_g", "ple_w_gate", "ple_w_proj", "ev_w_in", "ev_pool_w", "ev_pool_scale",
        "ev_q_norm", "ev_k_norm", "ev_lambda", "ev_subln", "ev_w_out", "od_w_in", "od_q_a_norm", "od_w_uq",
        "od_kv_a_norm", "od_w_ukv", "od_q_norm", "od_k_norm", "od_a_log", "od_dt_bias", "od_o_norm",
        "od_w_out", "meta_tokens_2", "fox_norm_2", "fox_w_in_2", "fox_b_f_2", "fox_q_norm_2", "fox_k_norm_2",
        "fox_w_out_2", "hg_norm_2", "hg_w_in_2", "hg_b_f_2", "hg_lb_logits_2", "hg_o_norm_2", "hg_w_out_2",
        "moe_norm_2", "moe_w_grp_2", "moe_b_grp_2", "moe_w_rt_2", "moe_b_rt_2", "moe_w_up_2", "moe_w_down_2"]


def kernel(**inputs):
    import numpy as _np
    import concourse.bacc as _bacc
    from concourse import mybir as _mybir

    nc = _bacc.Bacc("TRN2", target_bir_lowering=False, num_devices=1)
    arrays, args = {}, {}
    at, constants = host_constants()
    laid = {name: _np.ascontiguousarray(inputs[name]) for name in _INS}
    laid["p_T"] = _np.ascontiguousarray(_np.transpose(_np.asarray(inputs["p"])[:, 0], (0, 2, 1)))
    laid["od_conv_T"] = _np.ascontiguousarray(_np.transpose(_np.asarray(inputs["od_conv_w"])[0], (1, 0)))
    laid["ev_pool_w"] = _np.ascontiguousarray(_np.asarray(inputs["ev_pool_w"])[0])
    laid["constants"] = constants
    for name, v in laid.items():
        arrays[f"in_{name}"] = v
        args[name] = nc.dram_tensor(f"in_{name}", v.shape, _mybir.dt.from_np(v.dtype), kind="ExternalInput").ap()
    args["out"] = nc.dram_tensor("out_0", (1, SEQ, D), F32, kind="ExternalOutput").ap()
    args["x_rows"] = nc.dram_tensor("expert_rows_in", (SLOTS, D), F32).ap()
    args["y_rows"] = nc.dram_tensor("expert_rows_out", (SLOTS, D), F32).ap()
    build(nc, args, at)
    from concourse.bass_utils import run_bass_kernel_spmd as _run
    r = _run(nc, [arrays], core_ids=[0])
    return r.results[0]["out_0"]
```

```python
import math

import concourse.bass as bass
import numpy as np
from concourse import mybir
from contextlib import ExitStack

F32 = mybir.dt.float32
I32 = mybir.dt.int32
ALU = mybir.AluOpType
ACT = mybir.ActivationFunctionType
AX = mybir.AxisListType

P = 128
D = 1024
KD = D // P
SEQ, META = 512, 16
TOKENS = SEQ + META
EPS = 1e-6
TILES = [(0, META)] + [(META + P * i, P) for i in range(SEQ // P)]
XT = [1, 2, 3, 4]
ALLT = [0, 1, 2, 3, 4]
NEG = -1e30
TWO_PI = 2 * math.pi

HB, DKB, DVB, WA, WB = 6, 64, 128, 256, 768
HC, DNOPE, DROPE = 4, 128, 64
DQK = DNOPE + DROPE
HD = 4
FH, FD = 16, 64
HG = 8
NEXP, GROUPS, EPG, DFF = 32, 4, 8, 512
ROWS = 64
OVER = 16
SLOTS = (NEXP + OVER) * ROWS


def host_constants():
    i = np.arange(P)
    c = {}
    c["identity"] = np.eye(P)
    c["power"] = np.full((P, 1), -0.5)
    c["causal"] = np.where(i[None, :] <= i[:, None], 0.0, NEG)
    c["upto"] = (i[:, None] <= i[None, :])
    c["before"] = (i[:, None] < i[None, :])
    for n in range(7):
        b = 1 << n
        c[f"half{n}"] = (i[:, None] // (2 * b) == i[None, :] // (2 * b)) & (i[:, None] // b % 2 == 0) & (i[None, :] // b % 2 == 1)
    c["later"] = np.where(i[None, :] >= i[:, None], 0.0, NEG)
    c["freq"] = np.tile(np.concatenate([500000.0 ** (-np.arange(8) * 2.0 / 16), 10000.0 ** (-np.arange(32) * 2.0 / 64)]), (P, 1))
    t = np.arange(SEQ)
    c["pool"] = np.concatenate([np.repeat((1.0 / np.minimum(t + 1, w))[None], 64, 0) for w in (2, 4)] + [np.repeat((1.0 / np.minimum(t + 1, w))[None], 64, 0) for w in (8, 16)], 0).reshape(2, P, SEQ).transpose(1, 0, 2).reshape(P, 2 * SEQ)
    c["iota"] = np.tile(np.arange(NEXP, dtype=np.float64), (P, 1))
    c["steps"] = np.tile(ROWS * np.arange(1, 9, dtype=np.float64), (P, 1))
    c["overs"] = np.tile(np.arange(OVER, dtype=np.float64), (P, 1))
    start = np.ones(TOKENS); start[[a for a, _ in TILES]] = 0
    c["carry"] = np.tile(start, (P, 1))
    at, out = {}, []
    n = 0
    for k, v in c.items():
        at[k] = (n, v.shape[1])
        n += v.shape[1]
        out.append(v.astype(np.float32))
    return at, np.ascontiguousarray(np.concatenate(out, 1))


class Signal:

    def __init__(self, sem):
        self.sem, self.base, self.count = sem, 0, 0

    def up(self, step=1):
        self.count += step
        return self.sem, step

    def at(self, n):
        return self.sem, self.base + n

    def last(self):
        return self.at(self.count)


class Program:

    def __init__(self, nc, ctx, a, const_at):
        self.nc, self.ctx, self.a, self.const_at = nc, ctx, a, const_at
        self.signals = {}
        sb = lambda name, shape, dt=F32: ctx.enter_context(nc.sbuf_tensor(name, shape, dt))
        self.ring = sb("weight_ring", [P, 4, 4096])
        self.hT = sb("hidden_T", [P, KD, TOKENS])
        self.h = sb("hidden", [P, 5, D])
        self.const = sb("constants", [P, sum(w for _, w in const_at.values())])
        self.small = sb("small", [P, 1024])
        self.gains = sb("norm_gains", [P, 6 * KD])
        self.arena_cols = 23200
        self.arena = sb("arena", [P, self.arena_cols])
        self.psum = ctx.enter_context(nc.psum_tensor("psum", [P, 8, 512], F32))
        self.top = 0
        self.stop = 0
        self.chunks = []
        self.fed = 0
        self.ring_in = [self.sem(f"weights_in_{n}") for n in range(4)]
        self.used = {}
        self.over_sems, self.gather_sems, self.gathers = [], [], 0

    def sem(self, name):
        return self.ctx.enter_context(self.nc.semaphore(name))

    def sig(self, *names):
        out = []
        for n in names:
            if n not in self.signals:
                self.signals[n] = Signal(self.sem(n))
            s = self.signals[n]
            s.base += s.count
            s.count = 0
            out.append(s)
        return out if len(out) > 1 else out[0]

    def c(self, name):
        a, w = self.const_at[name]
        return self.const[:, a:a + w]

    def gain(self, n):
        return self.gains[:, n * KD:(n + 1) * KD]

    def take(self, *shape):
        n = int(np.prod(shape))
        ap = self.arena[:, self.top:self.top + n]
        self.top += n
        assert self.top <= self.arena_cols, (self.top, self.arena_cols)
        if len(shape) == 2:
            ap = ap.rearrange("p (a b) -> p a b", a=shape[0])
        if len(shape) == 3:
            ap = ap.rearrange("p (a b c) -> p a b c", a=shape[0], b=shape[1])
        return ap

    def plan(self, src, kchunks, width):
        self.chunks.append((src, kchunks, width))
        return len(self.chunks) - 1

    def weights(self, n):
        _, k, w = self.chunks[n]
        return self.ring[:, n % 4, 0:k * w].rearrange("p (k w) -> p k w", k=k)

    def weights_wait(self, pe, n):
        pe.wait_ge(self.ring_in[n % 4], 16 * (n // 4 + 1))

    def chunk_used(self, n, signal):
        self.used[n] = (signal.sem, signal.base + signal.count)

    def feed(self, sp, upto):
        upto = min(upto, len(self.chunks))
        while self.fed < upto:
            n = self.fed
            src, k, w = self.chunks[n]
            if n >= 4:
                sp.wait_ge(*self.used[n - 4])
            sp.dma_start(self.weights(n), src.rearrange("(k p) w -> p k w", p=P)).then_inc(self.ring_in[n % 4], 16)
            self.fed += 1


def row_of_all(ap1d, n):
    return ap1d.rearrange("(a n) -> a n", a=1).to_broadcast([P, n])


def stage_load(g):
    nc, a = g.nc, g.a
    loaded, angled, sined, chain, zeroed = g.sig("inputs_loaded", "angles_ready", "sines_ready", "vector_step", "meta_rows_zeroed")
    g.sin = g.small[:, 0:160].rearrange("p (t f) -> p t f", t=4)
    g.cos = g.small[:, 160:320].rearrange("p (t f) -> p t f", t=4)
    mark = g.top
    pos_i = g.take(4).bitcast(I32)
    pos = g.take(4)
    ang, turns, red = g.take(4, 40), g.take(2, 160), g.take(2, 160)
    with nc.Block() as block:
        @block.sync
        def _(sp):
            sp.dma_start(pos_i, a["positions"].rearrange("b (t p) -> p (b t)", p=P), allow_slow_non_contiguous=True).then_inc(*loaded.up(16))
            sp.dma_start(g.const[:, :], a["constants"]).then_inc(*loaded.up(16))
            sp.dma_start(g.h[:, 1:5, :], a["x"].rearrange("b (t p) d -> p (b t) d", p=P)).then_inc(*loaded.up(16))
            sp.dma_start(g.gains[:, :], a["norm_gains"]).then_inc(*loaded.up(16))
            sp.wait_ge(*zeroed.at(1))
            sp.dma_start(g.h[0:META, 0, :], a["meta_tokens_2"]).then_inc(*loaded.up(16))
            g.feed(sp, 3)
            sp.wait_ge(*loaded.at(80))

        @block.gpsimd
        def _(pool):
            nc.gpsimd.memset(g.h[:, 0, :], 0.0).then_inc(*zeroed.up())
            nc.gpsimd.memset(g.small[:, 512:1024], 0.0).then_inc(*zeroed.up())

        @block.vector
        def _(dve):
            dve.wait_ge(*loaded.at(80))
            nc.vector.tensor_copy(pos, pos_i).then_inc(*chain.up())
            dve.wait_ge(*chain.last())
            nc.vector.tensor_tensor(ang, pos.unsqueeze(2).to_broadcast([P, 4, 40]), g.c("freq").unsqueeze(1).to_broadcast([P, 4, 40]), ALU.mult).then_inc(*chain.up())
            dve.wait_ge(*chain.last())
            flat = ang.rearrange("p t f -> p (t f)")
            magic = 1.5 * 2.0 ** 23
            c1 = 6.28125
            c2 = float(np.float32(TWO_PI - c1))
            c3 = float(TWO_PI - c1 - c2)
            for n, quarter in enumerate((0.0, 0.25)):
                nc.vector.tensor_scalar(turns[:, n, :], flat, 1 / TWO_PI, quarter, ALU.mult, ALU.add).then_inc(*chain.up())
                dve.wait_ge(*chain.last())
                nc.vector.tensor_scalar(turns[:, n, :], turns[:, n, :], magic, magic, ALU.add, ALU.subtract).then_inc(*chain.up())
                dve.wait_ge(*chain.last())
                nc.vector.scalar_tensor_tensor(red[:, n, :], turns[:, n, :], -c1, flat, ALU.mult, ALU.add).then_inc(*chain.up())
                dve.wait_ge(*chain.last())
                nc.vector.scalar_tensor_tensor(red[:, n, :], turns[:, n, :], -c2, red[:, n, :], ALU.mult, ALU.add).then_inc(*chain.up())
                dve.wait_ge(*chain.last())
                nc.vector.scalar_tensor_tensor(red[:, n, :], turns[:, n, :], -c3, red[:, n, :], ALU.mult, ALU.add).then_inc(*chain.up())
                dve.wait_ge(*chain.last())
                nc.vector.tensor_scalar(red[:, n, :], red[:, n, :], quarter * TWO_PI, 3.1415925, ALU.add, ALU.min).then_inc(*chain.up())
                dve.wait_ge(*chain.last())
                nc.vector.tensor_scalar(red[:, n, :], red[:, n, :], -3.1415925, None, ALU.max).then_inc(*angled.up())

        @block.scalar
        def _(act):
            for n, dst in enumerate((g.sin, g.cos)):
                act.wait_ge(*angled.at(n + 1))
                nc.scalar.activation(dst.rearrange("p t f -> p (t f)"), red[:, n, :], ACT.Sin).then_inc(*sined.up())
            act.wait_ge(*sined.at(2))
    g.top = mark


def zero_expert_rows(g, sp):
    g.x_rows_zeroed = g.sig("expert_rows_zeroed")
    zeros = g.small[:, 512:1024].unsqueeze(1)
    rows = g.a["x_rows"].rearrange("(p n) (two c) -> p (n two) c", p=P, c=512)
    sp.dma_start(rows, zeros.to_broadcast([P, SLOTS // P * 2, 512])).then_inc(*g.x_rows_zeroed.up(16))
    rows = g.a["y_rows"][NEXP * ROWS:].rearrange("(p n) (two c) -> p (n two) c", p=P, c=512)
    sp.dma_start(rows, zeros.to_broadcast([P, OVER * ROWS // P * 2, 512])).then_inc(*g.x_rows_zeroed.up(16))


def inverse_root(g, pool, out, sums, scale, chain, done, times=None):
    g.nc.gpsimd.tensor_scalar(out, sums, scale, EPS, ALU.mult, ALU.add).then_inc(*chain.up())
    pool.wait_ge(*chain.last())
    power = g.c("power")[0:out.shape[0], 0:1].to_broadcast(list(out.shape))
    if times is None:
        g.nc.gpsimd.tensor_tensor(out, out, power, ALU.pow).then_inc(*done.up())
    else:
        g.nc.gpsimd.tensor_tensor(out, out, power, ALU.pow).then_inc(*chain.up())
        pool.wait_ge(*chain.last())
        g.nc.gpsimd.tensor_scalar(out, out, times, None, ALU.mult).then_inc(*done.up())


def stage_norm(g, tiles, gain, ring_upto, keep=None, ahead=None):
    nc = g.nc
    mark = g.top
    squared_v = g.sig("rows_squared_by_vector")
    squared, rooted, scaled, transposed, moved, chain = g.sig("rows_squared", "norm_ready", "rows_scaled", "rows_transposed", "transposed_moved", "gpsimd_step")
    sq = g.take(2, D)
    rows = keep if keep is not None else g.take(2, D)
    nrows = 5 if keep is not None else 2
    ss, rs = g.take(5), g.take(5)
    normed = gain is not None
    with nc.Block() as block:
        @block.sync
        def _(sp):
            g.feed(sp, ring_upto)
            if ahead is not None:
                ahead(sp)

        @block.scalar
        def _(act):
            if normed:
                def square(i):
                    t = tiles[i]
                    n = TILES[t][1]
                    if i >= 2:
                        act.wait_ge(*squared.last())
                    nc.scalar.activation(sq[0:n, 0, :], g.h[0:n, t, :], ACT.Square, accum_out=ss[0:n, i:i + 1]).then_inc(*squared.up())

                square(0)
                for i, t in enumerate(tiles):
                    if i % 2 == 0 and i + 2 < len(tiles):
                        square(i + 2)
                    n = TILES[t][1]
                    act.wait_ge(*rooted.at(i + 1))
                    if nrows == 2:
                        if i - 1 > 0:
                            act.wait_ge(*transposed.at(i - 1))
                    nc.scalar.activation(rows[0:n, i % nrows, :], g.h[0:n, t, :], ACT.Copy, scale=rs[0:n, i:i + 1]).then_inc(*scaled.up())

        @block.vector
        def _(dve):
            if normed:
                for i in range(1, len(tiles), 2):
                    r = slice(0, TILES[tiles[i]][1])
                    if i >= 3:
                        dve.wait_ge(*squared_v.last())
                    nc.vector.tensor_tensor_reduce(out=sq[r, 1, :], in0=g.h[r, tiles[i], :], in1=g.h[r, tiles[i], :], scale=1.0, scalar=0.0,
                                                   op0=ALU.mult, op1=ALU.add, accum_out=ss[r, i:i + 1]).then_inc(*squared_v.up())
            for i, t in enumerate(tiles):
                a, n = TILES[t]
                for half in range(2):
                    dve.wait_ge(*transposed.at(i + 1))
                    src = g.psum[:, 2 * (i % 2) + half, :].rearrange("p (c n) -> p c n", c=4)[:, :, 0:n]
                    dst = g.hT[:, 4 * half:4 * half + 4, a:a + n]
                    if normed:
                        nc.vector.tensor_tensor(dst, src, gain[:, 4 * half:4 * half + 4].unsqueeze(2).to_broadcast([P, 4, n]), ALU.mult).then_inc(*moved.up())
                    else:
                        nc.vector.tensor_copy(dst, src).then_inc(*moved.up())

        @block.gpsimd
        def _(pool):
            if normed:
                for i, t in enumerate(tiles):
                    n = TILES[t][1]
                    pool.wait_ge(*(squared_v if i % 2 else squared).at(i // 2 + 1))
                    inverse_root(g, pool, rs[0:n, i:i + 1], ss[0:n, i:i + 1], 1.0 / D, chain, rooted)

        @block.tensor
        def _(pe):
            for i, t in enumerate(tiles):
                n = TILES[t][1]
                if normed:
                    pe.wait_ge(*scaled.at(i + 1))
                if 2 * (i - 1) > 0:
                    pe.wait_ge(*moved.at(2 * (i - 1)))
                for c in range(KD):
                    src = rows[0:n, i % nrows, c * P:(c + 1) * P] if normed else g.h[0:n, t, c * P:(c + 1) * P]
                    last = nc.tensor.transpose(g.psum[:, 2 * (i % 2) + c // 4, (c % 4) * P:(c % 4) * P + n], src, g.c("identity")[0:n, 0:n])
                last.then_inc(*transposed.up())
    g.top = mark


def products(nc, out, left, right):
    for i, (l, r) in enumerate(zip(left, right)):
        last = nc.tensor.matmul(out, l, r, start=i == 0, stop=i == len(left) - 1)
    return last


def rows_by_weights(g, pe, out, t, chunk, kchunks=KD, src=None):
    a, n = TILES[t]
    src = g.hT if src is None else src
    w = g.weights(chunk)
    return products(g.nc, out, [src[:, k, a:a + n] for k in range(kchunks)], [w[:, k, :] for k in range(kchunks)])


def stage_out(g, tiles, chunks, ring_upto):
    nc = g.nc
    ready, added = g.sig("product_ready", "residual_added")
    with nc.Block() as block:
        @block.tensor
        def _(pe):
            u = 0
            for half, chunk in enumerate(chunks):
                g.weights_wait(pe, chunk)
                for t in tiles:
                    n = TILES[t][1]
                    if u - 3 > 0:
                        pe.wait_ge(*added.at(u - 3))
                    last = rows_by_weights(g, pe, g.psum[0:n, u % 4, :], t, chunk)
                    last.then_inc(*ready.up())
                    u += 1
                g.chunk_used(chunk, ready)

        @block.sync
        def _(sp):
            g.feed(sp, ring_upto)

        @block.vector
        def _(dve):
            u = 0
            for half in range(2):
                for t in tiles:
                    n = TILES[t][1]
                    dve.wait_ge(*ready.at(u + 1))
                    dst = g.h[0:n, t, 512 * half:512 * half + 512]
                    nc.vector.tensor_tensor(dst, dst, g.psum[0:n, u % 4, :], ALU.add).then_inc(*added.up())
                    u += 1


def stage_ple(g, layer, chunks, proj_chunk, ring_upto):
    nc = g.nc
    mark = g.top
    p_in, ready, gated, multiplied, added, proj_ready = g.sig("ple_input_loaded", "product_ready", "gate_ready", "gate_applied", "residual_added", "ple_product_ready")
    pT = g.take(2, SEQ)
    gate = g.take(2, 512)
    gate2 = g.take(2, 512)
    with nc.Block() as block:
        @block.tensor
        def _(pe):
            u = 0
            pe.wait_ge(*p_in.at(16))
            g.weights_wait(pe, proj_chunk)
            for half, chunk in enumerate(chunks):
                g.weights_wait(pe, chunk)
                for t in XT:
                    a, n = TILES[t]
                    if u - 1 > 0:
                        pe.wait_ge(*gated.at(u - 1))
                    rows_by_weights(g, pe, g.psum[:, u % 2, :], t, chunk).then_inc(*ready.up())
                    if u - 1 > 0:
                        pe.wait_ge(*multiplied.at(u - 1))
                    w = g.weights(proj_chunk)
                    products(nc, g.psum[:, 2 + u % 2, :], [pT[:, k, a - META:a - META + n] for k in range(2)], [w[:, k, 512 * half:512 * half + 512] for k in range(2)]).then_inc(*proj_ready.up())
                    u += 1
                g.chunk_used(chunk, ready)
            g.chunk_used(proj_chunk, proj_ready)

        @block.sync
        def _(sp):
            sp.dma_start(pT, g.a["p_T"][layer].rearrange("(k p) t -> p k t", p=P)).then_inc(*p_in.up(16))
            g.feed(sp, ring_upto)

        @block.scalar
        def _(act):
            for u in range(8):
                act.wait_ge(*ready.at(u + 1))
                if u - 1 > 0:
                    act.wait_ge(*multiplied.at(u - 1))
                nc.scalar.activation(gate[:, u % 2, :], g.psum[:, u % 2, :], ACT.Sigmoid).then_inc(*gated.up())

        @block.vector
        def _(dve):
            for u in range(8):
                dve.wait_ge(*gated.at(u + 1))
                dve.wait_ge(*proj_ready.at(u + 1))
                if u - 1 > 0:
                    dve.wait_ge(*added.at(u - 1))
                nc.vector.tensor_tensor(gate2[:, u % 2, :], gate[:, u % 2, :], g.psum[:, 2 + u % 2, :], ALU.mult).then_inc(*multiplied.up())

        @block.gpsimd
        def _(pool):
            for u in range(8):
                half, t = u // 4, XT[u % 4]
                pool.wait_ge(*multiplied.at(u + 1))
                dst = g.h[:, t, 512 * half:512 * half + 512]
                nc.gpsimd.tensor_tensor(dst, dst, gate2[:, u % 2, :], ALU.add).then_inc(*added.up())
    g.top = mark


def stage_even_in(g, chunks, ring_upto):
    nc = g.nc
    ready, freed_a, freed_v, squared, summed, normed, rotated, transposed, placed, chain, gchain, gains_in, rooted = g.sig(
        "product_ready", "bank_read_by_scalar", "bank_read_by_vector", "heads_squared", "heads_summed", "heads_normed",
        "heads_rotated", "heads_transposed", "heads_placed", "vector_step", "gpsimd_step", "gains_loaded", "norm_ready")
    g.e_in = g.take(2, 16 + SEQ)
    g.e_gate = g.take(2, SEQ)
    g.e_qT, g.e_kT = g.take(HB, SEQ), g.take(HB, SEQ)
    g.e_v, g.e_bg = g.take(4, WB), g.take(4, WB)
    mark = g.top
    gain = g.take(2, 64)
    sq, qn = g.take(2, 384), g.take(2, 384)
    ss = g.take(2, 6)
    rope = g.take(4, 48)
    units = [("in" if f < 2 else "ingate", 0, f) for f in range(4)]
    for n, kind in enumerate(["q", "q", "k", "k", "v", "v", "b", "b"]):
        units += [(kind, n + 1, t) for t in XT]
    freed, na, nv = [], 0, 0
    for kind, *_ in units:
        if kind in ("in", "ingate", "b"):
            na += 1
            freed.append((freed_a, na))
        else:
            nv += 1
            freed.append((freed_v, nv))
    qk = [u for u in units if u[0] in "qk"]
    NB = 6
    heads = lambda ap: ap.rearrange("p (g d) -> p g d", d=64)
    with nc.Block() as block:
        @block.tensor
        def _(pe):
            def turn(i):
                pe.wait_ge(*rotated.at(i + 1))
                if i - 1 > 0:
                    pe.wait_ge(*placed.at(i - 1))
                for j in range(3):
                    last = nc.tensor.transpose(g.psum[:, 6 + i % 2, j * P:(j + 1) * P], qn[:, i % 2, j * P:(j + 1) * P], g.c("identity"))
                last.then_inc(*transposed.up())

            i = 0
            for u, (kind, c, x) in enumerate(units):
                if u == 0 or units[u - 1][1] != c:
                    g.weights_wait(pe, chunks[c])
                if u >= NB:
                    pe.wait_ge(*freed[u - NB][0].at(freed[u - NB][1]))
                w = g.weights(chunks[c])
                if c == 0:
                    products(nc, g.psum[:, u % NB, :], [w[:, k, x * P:(x + 1) * P] for k in range(KD)], [g.hT[:, k, META:] for k in range(KD)]).then_inc(*ready.up())
                else:
                    rows_by_weights(g, pe, g.psum[:, u % NB, 0:384], x, chunks[c]).then_inc(*ready.up())
                if u + 1 == len(units) or units[u + 1][1] != c:
                    g.chunk_used(chunks[c], ready)
                if kind in "qk":
                    if i >= 2:
                        turn(i - 2)
                    i += 1
                elif i < len(qk) + 2 and i >= len(qk):
                    turn(i - 2)
                    i += 1

        @block.sync
        def _(sp):
            sp.dma_start(gain[:, 0, :], g.a["ev_q_norm"].to_broadcast([P, 64])).then_inc(*gains_in.up(16))
            sp.dma_start(gain[:, 1, :], g.a["ev_k_norm"].to_broadcast([P, 64])).then_inc(*gains_in.up(16))
            g.feed(sp, ring_upto)

        @block.scalar
        def _(act):
            def place(i):
                kind, c, t = qk[i]
                dst = g.e_qT if kind == "q" else g.e_kT
                half = (c - 1) % 2
                act.wait_ge(*transposed.at(i + 1))
                nc.scalar.activation(dst[:, 3 * half:3 * half + 3, (t - 1) * P:t * P], g.psum[:, 6 + i % 2, 0:384].rearrange("p (h n) -> p h n", h=3), ACT.Copy).then_inc(*placed.up())

            i = 0
            for u, (kind, c, x) in enumerate(units):
                bank = g.psum[:, u % NB, :]
                if kind == "v":
                    if i < len(qk) + 2:
                        place(i - 2)
                        i += 1
                    continue
                act.wait_ge(*ready.at(u + 1))
                if kind == "in":
                    nc.scalar.activation(g.e_in[:, x, 16:], bank, ACT.Copy).then_inc(*freed_a.up())
                elif kind == "ingate":
                    nc.scalar.activation(g.e_gate[:, x - 2, :], bank, ACT.Silu).then_inc(*freed_a.up())
                elif kind == "b":
                    nc.scalar.activation(g.e_bg[:, x - 1, 384 * (c - 7):384 * (c - 6)], bank[:, 0:384], ACT.Silu).then_inc(*freed_a.up())
                else:
                    if i - 1 > 0:
                        act.wait_ge(*summed.at(i - 1))
                    nc.scalar.activation(sq[:, i % 2, :], bank[:, 0:384], ACT.Square).then_inc(*squared.up())
                    if i >= 2:
                        place(i - 2)
                    i += 1

        @block.vector
        def _(dve):
            nc_v = nc.vector
            nc_v.memset(g.e_in[:, :, 0:16], 0.0).then_inc(*chain.up())
            dve.wait_ge(*chain.last())
            dve.wait_ge(*gains_in.at(32))
            i = 0
            for u, (kind, c, x) in enumerate(units):
                bank = g.psum[:, u % NB, 0:384]
                if kind == "v":
                    dve.wait_ge(*ready.at(u + 1))
                    nc_v.tensor_copy(g.e_v[:, x - 1, 384 * (c - 5):384 * (c - 4)], bank).then_inc(*freed_v.up())
                elif kind in "qk":
                    s = ss[:, i % 2, :]
                    dve.wait_ge(*squared.at(i + 1))
                    nc_v.tensor_reduce(s, heads(sq[:, i % 2, :]), AX.X, ALU.add).then_inc(*summed.up())
                    dve.wait_ge(*summed.last())
                    dve.wait_ge(*rooted.at(i + 1))
                    if i - 1 > 0:
                        dve.wait_ge(*transposed.at(i - 1))
                    nc_v.tensor_tensor(heads(qn[:, i % 2, :]), heads(bank), s.unsqueeze(2).to_broadcast([P, 6, 64]), ALU.mult).then_inc(*freed_v.up())
                    dve.wait_ge(*freed_v.last())
                    gn = gain[:, 0 if kind == "q" else 1, :].unsqueeze(1).to_broadcast([P, 6, 64])
                    nc_v.tensor_tensor(heads(qn[:, i % 2, :]), heads(qn[:, i % 2, :]), gn, ALU.mult).then_inc(*normed.up())
                    i += 1

        @block.gpsimd
        def _(pool):
            for i in range(len(qk) + 1):
                if i < len(qk):
                    pool.wait_ge(*summed.at(i + 1))
                    inverse_root(g, pool, ss[:, i % 2, :], ss[:, i % 2, :], 1.0 / 64, gchain, rooted)
                if i == 0:
                    continue
                kind, c, t = qk[i - 1]
                if i > 0:
                    pool.wait_ge(*normed.at(i))
                v = heads(qn[:, (i - 1) % 2, :])
                rotate(g, pool, v[:, :, 0:8], v[:, :, 8:16], g.cos[:, t - 1, 0:8], g.sin[:, t - 1, 0:8], [rope[:, j, :] for j in range(4)], 6, 8, gchain, rotated)
    g.top = mark


def rotate(g, pool, x1, x2, cos, sin, tmp, groups, half, gchain, done):
    op = g.nc.gpsimd.tensor_tensor
    c = cos.unsqueeze(1).to_broadcast([P, groups, half])
    s = sin.unsqueeze(1).to_broadcast([P, groups, half])
    t = [a.rearrange("p (g d) -> p g d", g=groups) for a in tmp]
    if done.count:
        pool.wait_ge(*done.last())
    op(t[0], x1, c, ALU.mult).then_inc(*gchain.up())
    op(t[1], x2, s, ALU.mult).then_inc(*gchain.up())
    op(t[2], x2, c, ALU.mult).then_inc(*gchain.up())
    op(t[3], x1, s, ALU.mult).then_inc(*gchain.up())
    pool.wait_ge(*gchain.last())
    op(x1, t[0], t[1], ALU.subtract).then_inc(*gchain.up())
    pool.wait_ge(*gchain.last())
    op(x2, t[2], t[3], ALU.add).then_inc(*done.up())


class Pooling:

    def __init__(self, g):
        self.g = g
        self.loaded, self.zeroed, self.pooled, self.mixed, self.chain, self.done = g.sig(
            "pool_weights_loaded", "pool_weights_zeroed", "pooled", "pool_product_ready", "pool_step", "pool_gated")
        self.wp = g.take(2, P)
        self.scale = g.take(2)
        self.s = g.take(2, 2, 16 + SEQ)

    def load(self, sp):
        a = self.g.a
        sp.dma_start(self.scale, a["ev_pool_scale"].rearrange("a (n p) -> p (a n)", p=P), allow_slow_non_contiguous=True).then_inc(*self.loaded.up(16))
        sp.wait_ge(*self.zeroed.at(1))
        for n in range(2):
            for m in range(2):
                sp.dma_start(self.wp[64 * m:64 * m + 64, n, 64 * m:64 * m + 64], a["ev_pool_w"][2 * n + m]).then_inc(*self.loaded.up(16))

    def windows(self, pool):
        g, nc, s, chain, pooled = self.g, self.g.nc, self.s, self.chain, self.pooled
        wp, zeroed = self.wp, self.zeroed
        op = nc.gpsimd.tensor_tensor
        nc.gpsimd.memset(wp, 0.0).then_inc(*zeroed.up())
        nc.gpsimd.memset(s[:, :, :, 0:16], 0.0).then_inc(*chain.up())
        pool.wait_ge(*chain.last())
        for n in range(2):
            src, dst = g.e_in[:, n, :], s[:, n, 0, :]
            op(dst[:, 16:], src[:, 16:], src[:, 15:-1], ALU.add).then_inc(*chain.up())
            pool.wait_ge(*chain.last())
            for m, shift in enumerate((2, 4, 8)):
                if n == 0 and shift > 2:
                    break
                lo = 0 if shift == 4 or (shift == 2 and n == 1) else 64
                a, b = s[:, n, m % 2, :], s[:, n, (m + 1) % 2, :]
                op(b[lo:, 16:], a[lo:, 16:], a[lo:, 16 - shift:SEQ + 16 - shift], ALU.add).then_inc(*chain.up())
                pool.wait_ge(*chain.last())
            halves = [(0, 0), (64, 1)] if n == 0 else [(0, 0), (64, 1)]
            for lo, m in halves:
                r = g.c("pool").rearrange("p (n t) -> p n t", n=2)
                op(s[lo:lo + 64, n, 0, 16:], s[lo:lo + 64, n, m, 16:], r[lo:lo + 64, n, :], ALU.mult).then_inc(*chain.up())
                pool.wait_ge(*chain.last())
            op(s[:, n, 0, 16:], s[:, n, 0, 16:], src[:, 16:], ALU.subtract).then_inc(*pooled.up())
            pool.wait_ge(*pooled.last())

    def products(self, pe, banks_free):
        pe.wait_ge(*banks_free)
        pe.wait_ge(*self.loaded.at(80))
        for n in range(2):
            pe.wait_ge(*self.pooled.at(n + 1))
            products(self.g.nc, self.g.psum[:, n, :], [self.wp[:, n, :]], [self.s[:, n, 0, 16:]]).then_inc(*self.mixed.up())

    def gate(self, dve):
        g = self.g
        for n in range(2):
            dve.wait_ge(*self.mixed.at(n + 1))
            g.nc.vector.scalar_tensor_tensor(g.hT[:, n, META:], g.psum[:, n, :], self.scale[:, n:n + 1], g.e_gate[:, n, :], ALU.mult, ALU.mult).then_inc(*self.done.up())


def stage_even_attention(g, ring_upto):
    nc = g.nc
    mark = g.top
    lam_init = 0.8 - 0.6 * math.exp(-0.3 * 0)
    lam_in, exp_in, exp_out, scored, peaked, expd, combined, turned, placed, mixed, rows_ready, rows_turned, rows_placed, chain, taken, summed, rooted, gchain = g.sig(
        "lambda_loaded", "lambda_sums", "lambda_exps", "scores_ready", "row_peaks", "probabilities", "maps_combined", "heads_transposed", "heads_placed",
        "mixed_ready", "rows_scaled", "rows_transposed", "rows_placed", "vector_step", "mixed_taken", "heads_summed", "norm_ready", "gpsimd_step")
    pooling = Pooling(g)
    lv = g.take(4, 64)
    pair = g.take(2, 64)
    lam = g.take(4)
    subln = g.take(DVB)
    peak, total = g.take(4), g.take(2, 2)
    pr = g.take(2, 2, 512)
    am = g.take(2, 512)
    aT = g.hT[:, 0:2, META:]
    o, osq = g.take(2, WB), g.take(WB)
    so = g.take(HB)
    jobs = [(t, h) for t in range(4) for h in range(HB)]
    cw = lambda t: P * (t + 1)
    with nc.Block() as block:
        @block.tensor
        def _(pe):
            def scores(j):
                t, h = jobs[j]
                if j >= 2:
                    if 2 * (j - 1) > 0:
                        pe.wait_ge(*expd.at(2 * (j - 1)))
                for m in range(2):
                    r = slice(64 * m, 64 * m + 64)
                    bank = g.psum[:, 2 * (j % 2) + m, :]
                    nc.tensor.matmul(bank[:, 0:cw(t)], g.e_qT[r, h, t * P:(t + 1) * P], g.e_kT[r, h, 0:cw(t)], start=True, stop=False)
                    nc.tensor.matmul(bank[:, t * P:cw(t)], g.c("identity"), g.c("causal"), start=False, stop=True).then_inc(*scored.up())

            def mix(j):
                t, h = jobs[j]
                pe.wait_ge(*combined.at(j + 1))
                if j - 1 > 0:
                    pe.wait_ge(*placed.at(j - 1))
                for k in range(t + 1):
                    last = nc.tensor.transpose(g.psum[:, 4 + j % 2, k * P:(k + 1) * P], am[:, j % 2, k * P:(k + 1) * P], g.c("identity"))
                last.then_inc(*turned.up())

            def values(j):
                t, h = jobs[j]
                pe.wait_ge(*placed.at(j + 1))
                if j > 0:
                    pe.wait_ge(*taken.at(j))
                products(nc, g.psum[:, 6, (j % 2) * P:(j % 2) * P + P], [aT[:, j % 2, k * P:(k + 1) * P] for k in range(t + 1)], [g.e_v[:, k, h * DVB:(h + 1) * DVB] for k in range(t + 1)]).then_inc(*mixed.up())

            def turn_rows(t):
                pe.wait_ge(*rows_ready.at(t + 1))
                for half in range(2):
                    if 2 * t + half > 0:
                        pe.wait_ge(*rows_placed.at(2 * t + half))
                    for c in range(3):
                        last = nc.tensor.transpose(g.psum[:, 7, c * P:(c + 1) * P], o[:, t % 2, (3 * half + c) * P:(3 * half + c + 1) * P], g.c("identity"))
                    last.then_inc(*rows_turned.up())

            scores(0)
            for j in range(len(jobs)):
                if j + 1 < len(jobs):
                    scores(j + 1)
                mix(j)
                if j >= 1:
                    values(j - 1)
                if j % HB == 3 and j > HB:
                    turn_rows(j // HB - 1)
            values(len(jobs) - 1)
            turn_rows(3)
            pooling.products(pe, expd.at(2 * len(jobs)))

        @block.sync
        def _(sp):
            sp.dma_start(lv, g.a["ev_lambda"].rearrange("a b c -> a (b c)").to_broadcast([P, 256])).then_inc(*lam_in.up(16))
            sp.dma_start(subln, g.a["ev_subln"].to_broadcast([P, DVB])).then_inc(*lam_in.up(16))
            pooling.load(sp)
            g.feed(sp, ring_upto)

        @block.scalar
        def _(act):
            def copy_maps(j):
                t, h = jobs[j]
                act.wait_ge(*turned.at(j + 1))
                if j - 1 > 0:
                    act.wait_ge(*mixed.at(j - 1))
                nc.scalar.activation(aT[:, j % 2, 0:cw(t)], g.psum[:, 4 + j % 2, 0:cw(t)], ACT.Copy).then_inc(*placed.up())

            act.wait_ge(*exp_in.at(1))
            nc.scalar.activation(lam[:, 2:4], lam[:, 0:2], ACT.Exp).then_inc(*exp_out.up())
            for j, (t, h) in enumerate(jobs):
                for m in range(2):
                    act.wait_ge(*peaked.at(2 * j + m + 1))
                    if j - 1 > 0:
                        act.wait_ge(*combined.at(j - 1))
                    nc.scalar.activation(pr[:, j % 2, m, 0:cw(t)], g.psum[:, 2 * (j % 2) + m, 0:cw(t)], ACT.Exp, bias=peak[:, 2 * (j % 2) + m:2 * (j % 2) + m + 1],
                                                 scale=DKB ** -0.5, accum_out=total[:, j % 2, m:m + 1]).then_inc(*expd.up())
                if j:
                    copy_maps(j - 1)
            copy_maps(len(jobs) - 1)

        @block.gpsimd
        def _(pool):
            pooling.windows(pool)
            for t in range(4):
                pool.wait_ge(*summed.at(t + 1))
                inverse_root(g, pool, so, so, 1.0 / DVB, gchain, rooted, 1.0 - lam_init)

        @block.vector
        def _(dve):
            v = nc.vector
            dve.wait_ge(*lam_in.at(32))
            v.tensor_tensor(pair[:, 0, :], lv[:, 0, :], lv[:, 1, :], ALU.mult).then_inc(*chain.up())
            dve.wait_ge(*chain.last())
            v.tensor_tensor(pair[:, 1, :], lv[:, 2, :], lv[:, 3, :], ALU.mult).then_inc(*chain.up())
            dve.wait_ge(*chain.last())
            v.tensor_reduce(lam[:, 0:2], pair, AX.X, ALU.add).then_inc(*exp_in.up())
            dve.wait_ge(*exp_out.at(1))
            v.tensor_tensor(lam[:, 0:1], lam[:, 2:3], lam[:, 3:4], ALU.subtract).then_inc(*chain.up())
            dve.wait_ge(*chain.last())
            v.tensor_scalar(lam[:, 0:1], lam[:, 0:1], -1.0, -lam_init, ALU.mult, ALU.add).then_inc(*chain.up())
            dve.wait_ge(*chain.last())

            def peaks(j):
                t, h = jobs[j]
                for m in range(2):
                    q = peak[:, 2 * (j % 2) + m:2 * (j % 2) + m + 1]
                    dve.wait_ge(*scored.at(2 * j + m + 1))
                    if 2 * (j - 1) > 0:
                        dve.wait_ge(*expd.at(2 * (j - 1)))
                    v.tensor_reduce(q, g.psum[:, 2 * (j % 2) + m, 0:cw(t)], AX.X, ALU.max).then_inc(*chain.up())
                    dve.wait_ge(*chain.last())
                    v.tensor_scalar(q, q, -DKB ** -0.5, None, ALU.mult).then_inc(*peaked.up())

            def combine(j):
                t, h = jobs[j]
                dve.wait_ge(*expd.at(2 * j + 2))
                v.reciprocal(total[:, j % 2, :], total[:, j % 2, :]).then_inc(*chain.up())
                dve.wait_ge(*chain.last())
                v.tensor_tensor(total[:, j % 2, 1:2], total[:, j % 2, 1:2], lam[:, 0:1], ALU.mult).then_inc(*chain.up())
                dve.wait_ge(*chain.last())
                if j - 1 > 0:
                    dve.wait_ge(*turned.at(j - 1))
                v.tensor_scalar(pr[:, j % 2, 0, 0:cw(t)], pr[:, j % 2, 0, 0:cw(t)], total[:, j % 2, 0:1], None, ALU.mult).then_inc(*chain.up())
                dve.wait_ge(*chain.last())
                v.scalar_tensor_tensor(am[:, j % 2, 0:cw(t)], pr[:, j % 2, 1, 0:cw(t)], total[:, j % 2, 1:2], pr[:, j % 2, 0, 0:cw(t)], ALU.mult, ALU.add).then_inc(*combined.up())

            def take(j):
                t, h = jobs[j]
                dve.wait_ge(*mixed.at(j + 1))
                if h == 0 and t >= 2:
                    if 2 * (t - 1) > 0:
                        dve.wait_ge(*rows_turned.at(2 * (t - 1)))
                v.tensor_copy(o[:, t % 2, h * DVB:(h + 1) * DVB], g.psum[:, 6, (j % 2) * P:(j % 2) * P + P]).then_inc(*taken.up())
                if h == HB - 1:
                    dve.wait_ge(*taken.at(j + 1))
                    hv = lambda a: a.rearrange("p (h d) -> p h d", h=HB)
                    r = o[:, t % 2, :]
                    v.tensor_tensor(osq, r, r, ALU.mult).then_inc(*chain.up())
                    dve.wait_ge(*chain.last())
                    v.tensor_reduce(so, hv(osq), AX.X, ALU.add).then_inc(*summed.up())
                    dve.wait_ge(*rooted.at(t + 1))
                    v.tensor_tensor(hv(r), hv(r), so.unsqueeze(2).to_broadcast([P, HB, DVB]), ALU.mult).then_inc(*chain.up())
                    dve.wait_ge(*chain.last())
                    v.tensor_tensor(hv(r), hv(r), subln.unsqueeze(1).to_broadcast([P, HB, DVB]), ALU.mult).then_inc(*chain.up())
                    dve.wait_ge(*chain.last())
                    v.tensor_tensor(r, r, g.e_bg[:, t, :], ALU.mult).then_inc(*rows_ready.up())

            def place_rows(t):
                for half in range(2):
                    dve.wait_ge(*rows_turned.at(2 * t + half + 1))
                    v.tensor_copy(g.hT[:, 2 + 3 * half:5 + 3 * half, META + t * P:META + (t + 1) * P], g.psum[:, 7, 0:384].rearrange("p (c n) -> p c n", c=3)).then_inc(*rows_placed.up())

            peaks(0)
            for j in range(len(jobs)):
                if j % HB == 4 and j > HB:
                    place_rows(j // HB - 1)
                combine(j)
                if j + 1 < len(jobs):
                    peaks(j + 1)
                if j >= 2:
                    take(j - 2)
            take(len(jobs) - 2)
            take(len(jobs) - 1)
            place_rows(3)
            pooling.gate(dve)
    g.top = mark


def plan_odd(g):
    w = g.a["od_w_in"][0]
    chunks = [g.plan(w[:, 0:448], KD, 448), g.plan(w[:, 448:960], KD, 512)]
    chunks += [g.plan(w[:, 960 + 512 * n:1472 + 512 * n], KD, 512) for n in range(3)]
    chunks += [g.plan(w[:, 2496:2504], KD, 8), g.plan(w[:, 2504:3016], KD, 512)]
    up = [g.plan(g.a["od_w_uq"][0], 2, HC * DQK), g.plan(g.a["od_w_ukv"][0], 1, 1024)]
    out = [g.plan(g.a["od_w_out"][0][:, 512 * n:512 * n + 512], KD, 512) for n in range(2)]
    return chunks, up, out


def odd_layer(g, plans):
    chunks, up, out = plans
    g.top = 0
    g.o_conv = g.take(12, 4 + SEQ)
    g.o_dgate = g.take(4, 512)
    g.o_small = g.take(4, 8)
    keep = g.top
    g.o_cgate = g.take(4, 512)
    g.o_low = g.take(4, 448)
    stage_norm(g, XT, g.gain(1), chunks[0] + 4)
    stage_odd_in(g, chunks, up[0] + 2)
    stage_mla_low(g, up[0] + 4)
    stage_mla_up(g, up, out[0] + 4)
    stage_mla_attention(g, out[0] + 4)
    g.top = keep
    stage_delta(g, out[0] + 4)
    stage_out(g, XT, out, out[1] + 4)
    g.top = 0


def stage_odd_in(g, chunks, ring_upto):
    nc = g.nc
    mark = g.top
    ready, freed_a, freed_v, zeroed, taps_in, convd, silud, chain = g.sig(
        "product_ready", "bank_read_by_scalar", "bank_read_by_vector", "history_zeroed", "taps_loaded", "channels_convolved", "channels_activated", "vector_step")
    taps = g.take(12, 4)
    acc = g.take(2, SEQ)
    units = [("low", 0, t) for t in XT] + [("cgate", 1, t) for t in XT]
    units += [("conv", 2 + f // 4, f) for f in range(12)]
    units += [("small", 5, t) for t in XT] + [("dgate", 6, t) for t in XT]
    width = {"low": 448, "cgate": 512, "conv": 512, "small": 8, "dgate": 512}
    scalar = lambda kind, x: kind in ("cgate", "dgate", "conv")
    freed, na, nv = [], 0, 0
    for kind, c, x in units:
        if scalar(kind, x):
            na += 1
            freed.append((freed_a, na))
        else:
            nv += 1
            freed.append((freed_v, nv))
    NB = 8
    with nc.Block() as block:
        @block.tensor
        def _(pe):
            for u, (kind, c, x) in enumerate(units):
                if u == 0 or units[u - 1][1] != c:
                    g.weights_wait(pe, chunks[c])
                if u >= NB:
                    pe.wait_ge(*freed[u - NB][0].at(freed[u - NB][1]))
                bank = g.psum[:, u % NB, 0:width[kind]]
                if kind == "conv":
                    w = g.weights(chunks[c])
                    f = x % 4
                    products(nc, bank, [w[:, k, f * P:(f + 1) * P] for k in range(KD)], [g.hT[:, k, META:] for k in range(KD)]).then_inc(*ready.up())
                else:
                    rows_by_weights(g, pe, bank, x, chunks[c]).then_inc(*ready.up())
                if u + 1 == len(units) or units[u + 1][1] != c:
                    g.chunk_used(chunks[c], ready)

        @block.sync
        def _(sp):
            sp.dma_start(taps, g.a["od_conv_T"].rearrange("(f p) k -> p f k", p=P)).then_inc(*taps_in.up(16))
            g.feed(sp, ring_upto)

        @block.scalar
        def _(act):
            def activate(f):
                act.wait_ge(*convd.at(f + 1))
                nc.scalar.activation(g.o_conv[:, f, 0:SEQ], acc[:, f % 2, :], ACT.Silu).then_inc(*silud.up())

            for u, (kind, c, x) in enumerate(units):
                if not scalar(kind, x):
                    continue
                act.wait_ge(*ready.at(u + 1))
                bank = g.psum[:, u % NB, :]
                if kind == "conv":
                    nc.scalar.activation(g.o_conv[:, x, 4:], bank, ACT.Copy).then_inc(*freed_a.up())
                    if x:
                        activate(x - 1)
                else:
                    dst = g.o_cgate if kind == "cgate" else g.o_dgate
                    nc.scalar.activation(dst[:, x - 1, :], bank, ACT.Silu).then_inc(*freed_a.up())
            activate(11)

        @block.vector
        def _(dve):
            v = nc.vector
            v.memset(g.o_conv[:, :, 0:4], 0.0).then_inc(*zeroed.up())
            dve.wait_ge(*zeroed.at(1))
            dve.wait_ge(*taps_in.at(16))
            for u, (kind, c, x) in enumerate(units):
                if kind == "conv":
                    z, a = g.o_conv[:, x, :], acc[:, x % 2, :]
                    dve.wait_ge(*freed_a.at(freed[u][1]))
                    if x >= 2:
                        dve.wait_ge(*silud.at(x - 1))
                    v.tensor_scalar(a, z[:, 1:1 + SEQ], taps[:, x, 0:1], None, ALU.mult).then_inc(*chain.up())
                    dve.wait_ge(*chain.last())
                    for k in range(1, 3):
                        v.scalar_tensor_tensor(a, z[:, 1 + k:1 + k + SEQ], taps[:, x, k:k + 1], a, ALU.mult, ALU.add).then_inc(*chain.up())
                        dve.wait_ge(*chain.last())
                    v.scalar_tensor_tensor(a, z[:, 4:4 + SEQ], taps[:, x, 3:4], a, ALU.mult, ALU.add).then_inc(*convd.up())
                elif not scalar(kind, x):
                    dve.wait_ge(*ready.at(u + 1))
                    dst = g.o_low[:, x - 1, :] if kind == "low" else g.o_small[:, x - 1, :]
                    v.tensor_copy(dst, g.psum[:, u % NB, 0:width[kind]]).then_inc(*freed_v.up())
    g.top = mark


def stage_mla_low(g, ring_upto):
    nc = g.nc
    g.m_low = g.take(3, SEQ)
    mark = g.top
    loaded, squared, rooted, scaled, transposed, moved, gchain = g.sig("gain_loaded", "rows_squared", "norm_ready", "rows_scaled", "rows_transposed", "transposed_moved", "gpsimd_step")
    gain = g.take(3)
    junk, rows = g.take(4, 384), g.take(4, 384)
    ss = g.take(8)
    with nc.Block() as block:
        @block.tensor
        def _(pe):
            for t in range(4):
                pe.wait_ge(*scaled.at(2 * t + 2))
                if t - 1 > 0:
                    pe.wait_ge(*moved.at(t - 1))
                for c in range(3):
                    last = nc.tensor.transpose(g.psum[:, t % 2, c * P:(c + 1) * P], rows[:, t, c * P:(c + 1) * P], g.c("identity"))
                last.then_inc(*transposed.up())

        @block.sync
        def _(sp):
            sp.dma_start(gain[:, 0:2], g.a["od_q_a_norm"].rearrange("a (k p) -> p (a k)", p=P), allow_slow_non_contiguous=True).then_inc(*loaded.up(16))
            sp.dma_start(gain[:, 2:3], g.a["od_kv_a_norm"].rearrange("a (k p) -> p (a k)", p=P), allow_slow_non_contiguous=True).then_inc(*loaded.up(16))
            g.feed(sp, ring_upto)

        @block.scalar
        def _(act):
            parts = [(t, part) for t in range(4) for part in (slice(0, 256), slice(256, 384))]
            for n, (t, part) in enumerate(parts):
                nc.scalar.activation(junk[:, t, part], g.o_low[:, t, part], ACT.Square, accum_out=ss[:, n:n + 1]).then_inc(*squared.up())
            for n, (t, part) in enumerate(parts):
                act.wait_ge(*rooted.at(2))
                nc.scalar.activation(rows[:, t, part], g.o_low[:, t, part], ACT.Copy, scale=ss[:, n:n + 1]).then_inc(*scaled.up())

        @block.gpsimd
        def _(pool):
            pool.wait_ge(*squared.at(8))
            pairs = ss.rearrange("p (t n) -> p n t", n=2)
            for n, width in enumerate((256, 128)):
                inverse_root(g, pool, pairs[:, n, :], pairs[:, n, :], 1.0 / width, gchain, rooted)

        @block.vector
        def _(dve):
            dve.wait_ge(*loaded.at(32))
            for t in range(4):
                dve.wait_ge(*transposed.at(t + 1))
                nc.vector.tensor_tensor(g.m_low[:, :, t * P:(t + 1) * P], g.psum[:, t % 2, 0:384].rearrange("p (c n) -> p c n", c=3), gain.unsqueeze(2).to_broadcast([P, 3, P]), ALU.mult).then_inc(*moved.up())
    g.top = mark


def stage_mla_up(g, up, ring_upto):
    nc = g.nc
    g.m_qn, g.m_kn = g.take(HC, SEQ), g.take(HC, SEQ)
    g.m_qr, g.m_kr = g.take(HC, SEQ), g.take(HC, SEQ)
    g.m_v = g.hT[:, 4:8, 0:HC * 128]
    mark = g.top
    ready, copied, values_out, squared, summed, rooted, normed, rotated, transposed, placed, chain, gchain, gains_in = g.sig(
        "product_ready", "heads_copied", "values_copied", "heads_squared", "heads_summed", "norm_ready", "heads_normed",
        "heads_rotated", "heads_transposed", "heads_placed", "vector_step", "gpsimd_step", "gains_loaded")
    gain = [g.small[:, 320:512], g.take(DQK)]
    b = g.hT[:, 0:4, 0:2 * DQK].rearrange("p a (h d) -> p a h d", h=2)
    sq = g.take(2, 2, DQK)
    ss = g.take(4, 2)
    rope = g.take(4, 64)
    units = [("q", t, half) for t in range(4) for half in range(2)] + [("k", t, half) for t in range(4) for half in range(2)]
    with nc.Block() as block:
        @block.tensor
        def _(pe):
            def turn(i):
                pe.wait_ge(*rotated.at(i + 1))
                if i > 1:
                    pe.wait_ge(*placed.at(2 * (i - 1)))
                for j in range(2):
                    nc.tensor.transpose(g.psum[:, 4 + i % 2, j * P:(j + 1) * P], b[:, i % 4, j, 0:128], g.c("identity"))
                    last = nc.tensor.transpose(g.psum[0:64, 4 + i % 2, 256 + j * P:256 + (j + 1) * P], b[:, i % 4, j, 128:DQK], g.c("identity"))
                last.then_inc(*transposed.up())

            for i, (kind, t, half) in enumerate(units):
                if i in (0, 8):
                    g.weights_wait(pe, up[i // 8])
                if i - 1 > 0:
                    pe.wait_ge(*copied.at(i - 1))
                if kind == "q":
                    w = g.weights(up[0])
                    products(nc, g.psum[:, i % 2, 0:384], [g.m_low[:, k, t * P:(t + 1) * P] for k in range(2)], [w[:, k, 384 * half:384 * half + 384] for k in range(2)]).then_inc(*ready.up())
                else:
                    if i - 8 - 1 > 0:
                        pe.wait_ge(*values_out.at(i - 8 - 1))
                    w = g.weights(up[1])
                    products(nc, g.psum[:, i % 2, :], [g.m_low[:, 2, t * P:(t + 1) * P]], [w[:, 0, 512 * half:512 * half + 512]]).then_inc(*ready.up())
                if i in (7, 15):
                    g.chunk_used(up[i // 8], ready)
                if i >= 3:
                    turn(i - 3)
            for i in range(len(units) - 3, len(units)):
                turn(i)

        @block.sync
        def _(sp):
            sp.dma_start(gain[0], g.a["od_q_norm"].to_broadcast([P, DQK])).then_inc(*gains_in.up(16))
            sp.dma_start(gain[1], g.a["od_k_norm"].to_broadcast([P, DQK])).then_inc(*gains_in.up(16))
            g.feed(sp, ring_upto)

        @block.scalar
        def _(act):
            def place(i):
                kind, t, half = units[i]
                cols = slice(t * P, (t + 1) * P)
                n_, r_ = (g.m_qn, g.m_qr) if kind == "q" else (g.m_kn, g.m_kr)
                act.wait_ge(*transposed.at(i + 1))
                nc.scalar.activation(n_[:, 2 * half:2 * half + 2, cols], g.psum[:, 4 + i % 2, 0:256].rearrange("p (h n) -> p h n", h=2), ACT.Copy).then_inc(*placed.up())
                nc.scalar.activation(r_[0:64, 2 * half:2 * half + 2, cols], g.psum[0:64, 4 + i % 2, 256:512].rearrange("p (h n) -> p h n", h=2), ACT.Copy).then_inc(*placed.up())

            for i, (kind, t, half) in enumerate(units):
                act.wait_ge(*copied.at(i + 1))
                if i - 1 > 0:
                    act.wait_ge(*summed.at(i - 1))
                nc.scalar.activation(sq[:, i % 2, :, :], b[:, i % 4, :, :], ACT.Square).then_inc(*squared.up())
                if i >= 4:
                    place(i - 4)
            for i in range(len(units) - 4, len(units)):
                place(i)

        @block.vector
        def _(dve):
            v = nc.vector
            dve.wait_ge(*gains_in.at(32))
            for i in range(len(units) + 2):
                if i < len(units):
                    kind, t, half = units[i]
                    buf, bank = b[:, i % 4, :, :], g.psum[:, i % 2, :]
                    dve.wait_ge(*ready.at(i + 1))
                    if i >= 4:
                        dve.wait_ge(*transposed.at(i - 3))
                    if kind == "q":
                        v.tensor_copy(buf, bank[:, 0:384].rearrange("p (h d) -> p h d", h=2)).then_inc(*copied.up())
                    else:
                        kv = bank.rearrange("p (h d) -> p h d", h=2)
                        v.tensor_copy(g.m_v[:, t, 256 * half:256 * half + 256].rearrange("p (h d) -> p h d", h=2), kv[:, :, 128:256]).then_inc(*values_out.up())
                        v.tensor_copy(buf[:, :, 128:DQK], g.o_low[:, t, 384:448].unsqueeze(1).to_broadcast([P, 2, 64])).then_inc(*chain.up())
                        dve.wait_ge(*chain.last())
                        v.tensor_copy(buf[:, :, 0:128], kv[:, :, 0:128]).then_inc(*copied.up())
                if 1 <= i <= len(units):
                    n = i - 1
                    dve.wait_ge(*squared.at(n + 1))
                    v.tensor_reduce(ss[:, n % 4, :], sq[:, n % 2, :, :], AX.X, ALU.add).then_inc(*summed.up())
                if i >= 2:
                    n = i - 2
                    buf = b[:, n % 4, :, :]
                    dve.wait_ge(*rooted.at(n + 1))
                    v.tensor_tensor(buf, buf, ss[:, n % 4, :].unsqueeze(2).to_broadcast([P, 2, DQK]), ALU.mult).then_inc(*chain.up())
                    dve.wait_ge(*chain.last())
                    v.tensor_tensor(buf, buf, gain[0 if units[n][0] == "q" else 1].unsqueeze(1).to_broadcast([P, 2, DQK]), ALU.mult).then_inc(*normed.up())

        @block.gpsimd
        def _(pool):
            for i in range(len(units) + 1):
                if i < len(units):
                    pool.wait_ge(*summed.at(i + 1))
                    inverse_root(g, pool, ss[:, i % 4, :], ss[:, i % 4, :], 1.0 / DQK, gchain, rooted)
                if i == 0:
                    continue
                kind, t, half = units[i - 1]
                pool.wait_ge(*normed.at(i))
                v = b[:, (i - 1) % 4, :, :]
                rotate(g, pool, v[:, :, 128:160], v[:, :, 160:192], g.cos[:, t, 8:40], g.sin[:, t, 8:40], [rope[:, j, :] for j in range(4)], 2, 32, gchain, rotated)
    g.top = mark


def stage_mla_attention(g, ring_upto):
    nc = g.nc
    mark = g.top
    scored, peaked, expd, turned, placed, mixed, rows_turned, rows_placed, chain, taken = g.sig(
        "scores_ready", "row_peaks", "probabilities", "heads_transposed", "heads_placed",
        "mixed_ready", "rows_transposed", "rows_placed", "vector_step", "mixed_taken")
    peak, total = g.take(2), g.take(2)
    pr = g.m_low[:, 0:2, :]
    pT = g.o_low.rearrange("p t n -> p (t n)")[:, 0:1024].rearrange("p (a n) -> p a n", a=2)
    o = g.take(2, 512)
    jobs = [(t, h) for t in range(4) for h in range(HC)]
    cw = lambda t: P * (t + 1)
    N = len(jobs)
    with nc.Block() as block:
        @block.tensor
        def _(pe):
            def scores(j):
                t, h = jobs[j]
                if j - 1 > 0:
                    pe.wait_ge(*expd.at(j - 1))
                bank = g.psum[:, j % 2, :]
                q = slice(t * P, (t + 1) * P)
                nc.tensor.matmul(bank[:, 0:cw(t)], g.m_qn[:, h, q], g.m_kn[:, h, 0:cw(t)], start=True, stop=False)
                nc.tensor.matmul(bank[:, 0:cw(t)], g.m_qr[0:64, h, q], g.m_kr[0:64, h, 0:cw(t)], start=False, stop=False)
                nc.tensor.matmul(bank[:, t * P:cw(t)], g.c("identity"), g.c("causal"), start=False, stop=True).then_inc(*scored.up())

            def turn(j):
                t, h = jobs[j]
                pe.wait_ge(*expd.at(j + 1))
                if j - 1 > 0:
                    pe.wait_ge(*placed.at(j - 1))
                for k in range(t + 1):
                    last = nc.tensor.transpose(g.psum[:, 2 + j % 2, k * P:(k + 1) * P], pr[:, j % 2, k * P:(k + 1) * P], g.c("identity"))
                last.then_inc(*turned.up())

            def values(j):
                t, h = jobs[j]
                pe.wait_ge(*placed.at(j + 1))
                if j - 1 > 0:
                    pe.wait_ge(*taken.at(j - 1))
                products(nc, g.psum[:, 4 + j % 2, 0:P], [pT[:, j % 2, k * P:(k + 1) * P] for k in range(t + 1)], [g.m_v[:, k, h * P:(h + 1) * P] for k in range(t + 1)]).then_inc(*mixed.up())

            def turn_rows(t):
                pe.wait_ge(*taken.at(HC * (t + 1)))
                if t - 1 > 0:
                    pe.wait_ge(*rows_placed.at(t - 1))
                for c in range(4):
                    last = nc.tensor.transpose(g.psum[:, 6 + t % 2, c * P:(c + 1) * P], o[:, t % 2, c * P:(c + 1) * P], g.c("identity"))
                last.then_inc(*rows_turned.up())

            scores(0)
            for j in range(N):
                if j + 1 < N:
                    scores(j + 1)
                turn(j)
                if j:
                    values(j - 1)
                if j % HC == 2 and j > HC:
                    turn_rows(j // HC - 1)
            values(N - 1)
            turn_rows(3)

        @block.sync
        def _(sp):
            g.feed(sp, ring_upto)

        @block.scalar
        def _(act):
            def copy_map(j):
                t, h = jobs[j]
                act.wait_ge(*turned.at(j + 1))
                if j - 1 > 0:
                    act.wait_ge(*mixed.at(j - 1))
                nc.scalar.activation(pT[:, j % 2, 0:cw(t)], g.psum[:, 2 + j % 2, 0:cw(t)], ACT.Copy).then_inc(*placed.up())

            for j, (t, h) in enumerate(jobs):
                act.wait_ge(*peaked.at(j + 1))
                if j - 1 > 0:
                    act.wait_ge(*turned.at(j - 1))
                if j - 1 > 0:
                    act.wait_ge(*taken.at(j - 1))
                nc.scalar.activation(pr[:, j % 2, 0:cw(t)], g.psum[:, j % 2, 0:cw(t)], ACT.Exp, bias=peak[:, j % 2:j % 2 + 1], scale=DQK ** -0.5, accum_out=total[:, j % 2:j % 2 + 1]).then_inc(*expd.up())
                if j:
                    copy_map(j - 1)
            copy_map(N - 1)

        @block.vector
        def _(dve):
            v = nc.vector

            def peaks(j):
                t, h = jobs[j]
                q = peak[:, j % 2:j % 2 + 1]
                dve.wait_ge(*scored.at(j + 1))
                if j - 1 > 0:
                    dve.wait_ge(*expd.at(j - 1))
                v.tensor_reduce(q, g.psum[:, j % 2, 0:cw(t)], AX.X, ALU.max).then_inc(*chain.up())
                dve.wait_ge(*chain.last())
                v.tensor_scalar(q, q, -DQK ** -0.5, None, ALU.mult).then_inc(*peaked.up())

            def take(j):
                t, h = jobs[j]
                dve.wait_ge(*mixed.at(j + 1))
                if h == 0 and t >= 2:
                    if t - 1 > 0:
                        dve.wait_ge(*rows_turned.at(t - 1))
                s = total[:, j % 2:j % 2 + 1]
                v.reciprocal(s, s).then_inc(*chain.up())
                dve.wait_ge(*chain.last())
                v.scalar_tensor_tensor(o[:, t % 2, h * P:(h + 1) * P], g.psum[:, 4 + j % 2, 0:P], s, g.o_cgate[:, t, h * P:(h + 1) * P], ALU.mult, ALU.mult).then_inc(*taken.up())

            def place_rows(t):
                dve.wait_ge(*rows_turned.at(t + 1))
                v.tensor_copy(g.hT[:, 0:4, META + t * P:META + (t + 1) * P], g.psum[:, 6 + t % 2, :].rearrange("p (c n) -> p c n", c=4)).then_inc(*rows_placed.up())

            for j in range(N + 2):
                if j % HC == 3 and j > HC:
                    place_rows(j // HC - 1)
                if j < N:
                    peaks(j)
                if j >= 2:
                    take(j - 2)
            place_rows(3)
    g.top = mark


def stage_delta(g, ring_upto):
    nc = g.nc
    NCH = 4
    tok = g.take(4, 8, P)
    vt = g.take(4, 4, P)
    qkT = g.take(8, SEQ)
    beta, gl = g.take(4, HD), g.take(4, HD)
    mark = g.top
    loaded, turned, copied, chain, achain, gchain, betas, decays, squared, rooted, scaled, back, backed = g.sig(
        "delta_weights_loaded", "channels_transposed", "channels_placed", "vector_step", "scalar_step", "gpsimd_step",
        "betas_ready", "decays_ready", "heads_summed", "norm_ready", "heads_scaled", "heads_transposed", "heads_placed")
    gate_in = g.take(2, HD)
    tmp = g.take(4, 16)
    sq = g.take(8, P)
    ss = g.take(4, 8)
    with nc.Block() as block:
        @block.tensor
        def _(pe):
            for f in range(12):
                if f >= 2:
                    pe.wait_ge(*copied.at(f - 1))
                for t in range(4):
                    last = nc.tensor.transpose(g.psum[:, f % 2, t * P:(t + 1) * P], g.o_conv[:, f, t * P:(t + 1) * P], g.c("identity"))
                last.then_inc(*turned.up())
            for t in range(4):
                pe.wait_ge(*scaled.at(t + 1))
                for half in range(2):
                    u = 2 * t + half
                    if u - 1 > 0:
                        pe.wait_ge(*backed.at(u - 1))
                    for c in range(4):
                        last = nc.tensor.transpose(g.psum[:, 2 + u % 2, c * P:(c + 1) * P], tok[:, t, 4 * half + c, :], g.c("identity"))
                    last.then_inc(*back.up())

        @block.sync
        def _(sp):
            sp.dma_start(gate_in[:, 0, :], g.a["od_a_log"].to_broadcast([P, HD])).then_inc(*loaded.up(16))
            sp.dma_start(gate_in[:, 1, :], g.a["od_dt_bias"].to_broadcast([P, HD])).then_inc(*loaded.up(16))
            g.feed(sp, ring_upto)

        @block.scalar
        def _(act):
            def place(n):
                act.wait_ge(*turned.at(n + 1))
                dst = tok[:, :, n, :] if n < 8 else vt[:, :, n - 8, :]
                nc.scalar.activation(dst, g.psum[:, n % 2, :].rearrange("p (t d) -> p t d", t=4), ACT.Copy).then_inc(*copied.up())

            for f in range(12):
                place(f)
            act.wait_ge(*loaded.at(32))
            nc.scalar.activation(beta, g.o_small[:, :, 0:4], ACT.Sigmoid).then_inc(*betas.up())
            act.wait_ge(*decays.at(1))
            nc.scalar.activation(tmp[:, 1, :], tmp[:, 1, :], ACT.Exp, scale=-1.0).then_inc(*achain.up())
            act.wait_ge(*achain.last())
            nc.scalar.activation(tmp[:, 2, 0:4], gate_in[:, 0, :], ACT.Exp).then_inc(*achain.up())
            act.wait_ge(*achain.last())
            act.wait_ge(*decays.at(2))
            nc.scalar.activation(tmp[:, 1, :], tmp[:, 1, :], ACT.Ln).then_inc(*achain.up())

        @block.gpsimd
        def _(pool):
            for t in range(4):
                pool.wait_ge(*squared.at(t + 1))
                for n, factor in enumerate((128 ** -0.5, None)):
                    s = ss[:, t, 4 * n:4 * n + 4]
                    inverse_root(g, pool, s, s, 1.0, gchain, rooted, factor)

        @block.vector
        def _(dve):
            v = nc.vector
            def place(t):
                for half in range(2):
                    u = 2 * t + half
                    dve.wait_ge(*back.at(u + 1))
                    v.tensor_copy(qkT[:, 4 * half:4 * half + 4, t * P:(t + 1) * P], g.psum[:, 2 + u % 2, :].rearrange("p (c n) -> p c n", c=4)).then_inc(*backed.up())

            dve.wait_ge(*loaded.at(32))
            dve.wait_ge(*copied.at(12))
            for t in range(4):
                v.tensor_tensor(sq, tok[:, t, :, :], tok[:, t, :, :], ALU.mult).then_inc(*chain.up())
                dve.wait_ge(*chain.last())
                v.tensor_reduce(ss[:, t, :], sq, AX.X, ALU.add).then_inc(*squared.up())
                dve.wait_ge(*rooted.at(2 * t + 2))
                v.tensor_tensor(tok[:, t, :, :], tok[:, t, :, :], ss[:, t, :].unsqueeze(2).to_broadcast([P, 8, P]), ALU.mult).then_inc(*scaled.up())
                if t:
                    place(t - 1)
            place(3)
            fl = lambda n: tmp[:, n, :].rearrange("p (t h) -> p t h", t=4)
            v.tensor_tensor(fl(0), g.o_small[:, :, 4:8], gate_in[:, 1, :].unsqueeze(1).to_broadcast([P, 4, HD]), ALU.add).then_inc(*chain.up())
            dve.wait_ge(*chain.last())
            v.tensor_scalar(tmp[:, 1, :], tmp[:, 0, :], -1.0, None, ALU.mult).then_inc(*chain.up())
            dve.wait_ge(*chain.last())
            v.tensor_tensor(tmp[:, 1, :], tmp[:, 0, :], tmp[:, 1, :], ALU.max).then_inc(*decays.up())
            dve.wait_ge(*achain.at(2))
            v.tensor_scalar(tmp[:, 1, :], tmp[:, 1, :], 1.0, None, ALU.add).then_inc(*decays.up())
            dve.wait_ge(*achain.at(3))
            v.scalar_tensor_tensor(tmp[:, 0, :], tmp[:, 0, :], 0.0, tmp[:, 1, :], ALU.max, ALU.add).then_inc(*chain.up())
            dve.wait_ge(*chain.last())
            v.tensor_scalar(tmp[:, 2, 0:4], tmp[:, 2, 0:4], -1.0, None, ALU.mult).then_inc(*chain.up())
            dve.wait_ge(*chain.last())
            v.tensor_tensor(gl, fl(0), tmp[:, 2, 0:4].unsqueeze(1).to_broadcast([P, 4, HD]), ALU.mult).then_inc(*chain.up())
            dve.wait_ge(*chain.last())
    g.top = mark
    level_prod, t_prod, u_prod, og_ready, o_ready = g.sig("level_product", "inverse_product", "inverse_T_product", "output_rows_ready", "outputs_ready")
    cum_ready, cols, expd, kq, ut, tt, prod, red, scanned, done, rows_turned, rows_placed, rooted, gains_in, summed = g.sig(
        "cumulated", "exponents_ready", "decays_exped", "key_products", "inverse_T", "inverse", "product_ready", "reduced", "scan_product", "scan_step",
        "rows_transposed", "rows_placed", "norm_ready", "gains_loaded", "heads_summed")
    H4 = lambda ap: ap.rearrange("p (h d) -> p h d", h=HD)
    col, nlast, egc, dlast, elast = (g.take(HD) for _ in range(5))
    spare = g.o_conv.rearrange("p f n -> p (f n)")[:, 0:12 * HD * P].rearrange("p (n h d) -> p n h d", n=12, h=HD)
    osq, gamT, LT = (spare[:, n, :, :] for n in (0, 1, 2))
    U, T, Lv, X = (spare[:, n, :, :] for n in (3, 4, 5, 6))
    qkg, kb, vb, kd = (spare[:, n, :, :] for n in (7, 8, 9, 10))
    uu = spare[:, 11, :, :]
    wT, vn = g.take(HD, P), g.take(HD, P)
    S = g.take(HD, P)
    o, og = g.take(HD, P), g.take(HD, P)
    so = g.take(HD)
    onorm = g.take(P)
    bc = lambda ap: ap.unsqueeze(2).to_broadcast([P, HD, P])
    mid = lambda name: g.c(name).unsqueeze(1).to_broadcast([P, HD, P])
    pq = lambda n: H4(g.psum[:, n, :])
    with nc.Block() as block:
        @block.tensor
        def _(pe):
            mm, tr = nc.tensor.matmul, nc.tensor.transpose

            def decays(n):
                q = slice(n * P, (n + 1) * P)
                if n:
                    pe.wait_ge(*scanned.at(2 * n))
                mm(g.psum[:, 5, 0:HD], g.c("upto"), gl[:, n, :], start=True, stop=True)
                for h in range(HD):
                    last = mm(pq(1)[:, h, :], gl[:, n, h:h + 1].to_broadcast([P, P]), g.c("upto"), start=True, stop=True)
                last.then_inc(*cum_ready.up())
                for h in range(HD):
                    mm(pq(2)[:, h, :], qkT[:, 4 + h, q], qkT[:, 4 + h, q], start=True, stop=True)
                    last = mm(pq(3)[:, h, :], qkT[:, 4 + h, q], qkT[:, h, q], start=True, stop=True)
                for h in range(HD):
                    last = mm(pq(4)[:, h, :], beta[:, n, h:h + 1].to_broadcast([P, P]), g.c("identity"), start=True, stop=True)
                last.then_inc(*kq.up())

            def turn_rows(n):
                pe.wait_ge(*og_ready.at(n + 1))
                for h in range(HD):
                    last = tr(pq(7)[:, h, :], og[:, h, :], g.c("identity"))
                last.then_inc(*rows_turned.up())

            decays(0)
            for n in range(NCH):
                q = slice(n * P, (n + 1) * P)
                pe.wait_ge(*ut.at(7 * n + 1))
                for h in range(HD):
                    last = tr(pq(5)[:, h, :], U[:, h, :], g.c("identity"))
                last.then_inc(*prod.up())
                for level in range(1, 7):
                    pe.wait_ge(*tt.at(6 * n + level))
                    for h in range(HD):
                        last = mm(pq(2)[:, h, :], Lv[:, h, :], T[:, h, :], start=True, stop=True)
                    last.then_inc(*level_prod.up())
                    pe.wait_ge(*red.at(6 * n + level))
                    pe.wait_ge(*ut.at(7 * n + level))
                    if level < 6:
                        for h in range(HD):
                            last = mm(pq(4)[:, h, :], U[:, h, :], X[:, h, :], start=True, stop=True)
                        last.then_inc(*t_prod.up())
                    for h in range(HD):
                        last = mm(pq(3)[:, h, :], X[:, h, :], U[:, h, :], start=True, stop=True)
                    last.then_inc(*u_prod.up())
                    if level == 2 and n:
                        turn_rows(n - 1)
                pe.wait_ge(*ut.at(7 * n + 7))
                for h in range(HD):
                    last = mm(pq(1)[:, h, :], kb[:, h, :], U[:, h, :], start=True, stop=True)
                last.then_inc(*prod.up())
                for h in range(HD):
                    last = mm(pq(0)[:, h, :], U[:, h, :], vb[:, h, :], start=True, stop=True)
                last.then_inc(*prod.up())
                pe.wait_ge(*scanned.at(2 * n + 1))
                for h in range(HD):
                    last = mm(pq(5)[:, h, :], wT[:, h, :], S[:, h, :], start=True, stop=True)
                last.then_inc(*prod.up())
                for h in range(HD):
                    last = mm(pq(6)[:, h, :], qkT[:, h, q], S[:, h, :], start=True, stop=True)
                last.then_inc(*prod.up())
                pe.wait_ge(*scanned.at(2 * n + 2))
                if n:
                    pe.wait_ge(*done.at(n))
                for h in range(HD):
                    mm(pq(7)[:, h, :], qkg[:, h, :], vn[:, h, :], start=True, stop=True)
                    last = mm(pq(0)[:, h, :], kd[:, h, :], vn[:, h, :], start=True, stop=True)
                last.then_inc(*prod.up())
                if n + 1 < NCH:
                    decays(n + 1)
            turn_rows(NCH - 1)

        @block.sync
        def _(sp):
            sp.dma_start(onorm, g.a["od_o_norm"].to_broadcast([P, P])).then_inc(*gains_in.up(16))
            g.feed(sp, ring_upto)

        @block.scalar
        def _(act):
            def exponentials(n):
                act.wait_ge(*cols.at(n + 1))
                nc.scalar.activation(gamT, gamT, ACT.Exp).then_inc(*expd.up())
                nc.scalar.activation(egc, col, ACT.Exp).then_inc(*expd.up())
                nc.scalar.activation(dlast, dlast, ACT.Exp).then_inc(*expd.up())
                nc.scalar.activation(elast, nlast, ACT.Exp).then_inc(*expd.up())

            exponentials(0)
            for n in range(NCH):
                act.wait_ge(*o_ready.at(n + 1))
                if n:
                    act.wait_ge(*og_ready.at(n))
                for h in range(HD):
                    nc.scalar.activation(osq[:, h, :], o[:, h, :], ACT.Square, accum_out=so[:, h:h + 1]).then_inc(*summed.up())
                if n + 1 < NCH:
                    exponentials(n + 1)
                act.wait_ge(*rows_turned.at(n + 1))
                nc.scalar.activation(g.hT[:, 4:8, META + n * P:META + (n + 1) * P], pq(7), ACT.Copy).then_inc(*done.up())

        @block.gpsimd
        def _(pool):
            pool.wait_ge(*gains_in.at(16))
            for n in range(NCH):
                gate = H4(g.o_dgate[:, n, :])
                nc.gpsimd.tensor_tensor(gate, gate, onorm.unsqueeze(1).to_broadcast([P, HD, P]), ALU.mult).then_inc(*gchain.up())
            for n in range(NCH):
                pool.wait_ge(*summed.at(HD * (n + 1)))
                inverse_root(g, pool, so, so, 1.0 / P, gchain, rooted)
                pool.wait_ge(*rooted.at(n + 1))
                if n:
                    pool.wait_ge(*rows_turned.at(n))
                nc.gpsimd.tensor_tensor(og, o, bc(so), ALU.mult).then_inc(*gchain.up())
                pool.wait_ge(*gchain.last())
                nc.gpsimd.tensor_tensor(og, og, H4(g.o_dgate[:, n, :]), ALU.mult).then_inc(*og_ready.up())

        @block.vector
        def _(dve):
            v = nc.vector
            v.memset(S, 0.0).then_inc(*chain.up())
            dve.wait_ge(*chain.last())
            per = 6
            for n in range(NCH):
                p0 = per * n
                dve.wait_ge(*cum_ready.at(n + 1))
                v.tensor_copy(col, g.psum[:, 5, 0:HD]).then_inc(*chain.up())
                v.tensor_copy(nlast, pq(1)[:, :, P - 1]).then_inc(*chain.up())
                dve.wait_ge(*chain.last())
                v.tensor_tensor(dlast, nlast, col, ALU.subtract).then_inc(*chain.up())
                for h in range(HD):
                    v.scalar_tensor_tensor(gamT[:, h, :], pq(1)[:, h, :], col[:, h:h + 1], g.c("later"), ALU.subtract, ALU.min).then_inc(*(cols if h == HD - 1 else chain).up())
                dve.wait_ge(*expd.at(4 * n + 4))
                dve.wait_ge(*kq.at(n + 1))
                v.tensor_tensor(LT, gamT, pq(2), ALU.mult).then_inc(*chain.up())
                dve.wait_ge(*chain.last())
                v.tensor_tensor(LT, LT, pq(4), ALU.mult).then_inc(*chain.up())
                dve.wait_ge(*chain.last())
                v.tensor_tensor(Lv, LT, mid("half0"), ALU.mult).then_inc(*chain.up())
                dve.wait_ge(*chain.last())
                v.scalar_tensor_tensor(U, Lv, -1.0, mid("identity"), ALU.mult, ALU.add).then_inc(*ut.up())
                v.tensor_tensor(qkg, gamT, pq(3), ALU.mult).then_inc(*chain.up())
                dve.wait_ge(*ut.last())
                v.tensor_tensor(Lv, LT, mid("half1"), ALU.mult).then_inc(*chain.up())
                dve.wait_ge(*chain.last())
                dve.wait_ge(*prod.at(p0 + 1))
                v.tensor_copy(T, pq(5)).then_inc(*tt.up())
                b = bc(beta[:, n, :])
                for level in range(1, 7):
                    dve.wait_ge(*level_prod.at(6 * n + level))
                    v.tensor_copy(X, pq(2)).then_inc(*red.up())
                    if level < 6:
                        v.tensor_tensor(Lv, LT, mid(f"half{level + 1}"), ALU.mult).then_inc(*chain.up())
                        dve.wait_ge(*t_prod.at(5 * n + level))
                        dve.wait_ge(*tt.last())
                        dve.wait_ge(*chain.last())
                        v.tensor_tensor(T, T, pq(4), ALU.subtract).then_inc(*tt.up())
                    dve.wait_ge(*u_prod.at(6 * n + level))
                    dve.wait_ge(*ut.last())
                    dve.wait_ge(*chain.last())
                    v.tensor_tensor(U, U, pq(3), ALU.subtract).then_inc(*ut.up())
                    if level == 1:
                        v.tensor_tensor(vb, vt[:, n, :, :], b, ALU.mult).then_inc(*chain.up())
                    if level == 2:
                        v.tensor_tensor(kb, tok[:, n, 4:8, :], b, ALU.mult).then_inc(*chain.up())
                    if level == 3:
                        v.tensor_tensor(kb, kb, bc(egc), ALU.mult).then_inc(*chain.up())
                    if level == 4:
                        v.tensor_tensor(kd, tok[:, n, 4:8, :], bc(dlast), ALU.mult).then_inc(*chain.up())
                dve.wait_ge(*prod.at(p0 + 2))
                v.tensor_copy(wT, pq(1)).then_inc(*scanned.up())
                dve.wait_ge(*prod.at(p0 + 3))
                v.tensor_copy(uu, pq(0)).then_inc(*chain.up())
                dve.wait_ge(*prod.at(p0 + 4))
                dve.wait_ge(*chain.last())
                v.tensor_tensor(vn, uu, pq(5), ALU.subtract).then_inc(*scanned.up())
                dve.wait_ge(*prod.at(p0 + 5))
                if n:
                    dve.wait_ge(*og_ready.at(n))
                v.tensor_tensor(o, pq(6), bc(egc), ALU.mult).then_inc(*chain.up())
                v.tensor_tensor(S, S, bc(elast), ALU.mult).then_inc(*chain.up())
                dve.wait_ge(*chain.last())
                dve.wait_ge(*prod.at(p0 + 6))
                v.tensor_tensor(S, S, pq(0), ALU.add).then_inc(*chain.up())
                v.tensor_tensor(o, o, pq(7), ALU.add).then_inc(*o_ready.up())
                dve.wait_ge(*chain.last())
                dve.wait_ge(*o_ready.last())
    g.top = mark


def plan_fox(g):
    w = g.a["fox_w_in_2"][0]
    chunks = [g.plan(w[:, 512 * n:512 * n + 512], KD, 512) for n in range(6)] + [g.plan(w[:, 3072:3088], KD, 16)]
    out = [g.plan(g.a["fox_w_out_2"][0][:, 512 * n:512 * n + 512], KD, 512) for n in range(2)]
    return chunks, out


def fox_layer(g, plans):
    chunks, out = plans
    g.top = 0
    stage_norm(g, ALLT, g.gain(2), chunks[0] + 4)
    stage_fox_in(g, chunks, out[0] + 2)
    stage_fox_attention(g, out[0] + 2)
    stage_out(g, ALLT, out, out[0] + 2)
    g.top = 0


def stage_fox_in(g, chunks, ring_upto):
    nc = g.nc
    ready, freed_a, freed_v, squared, summed, rooted, normed, transposed, placed, chain, gchain, gains_in = g.sig(
        "product_ready", "bank_read_by_scalar", "bank_read_by_vector", "heads_squared", "heads_summed", "norm_ready", "heads_normed",
        "heads_transposed", "heads_placed", "vector_step", "gpsimd_step", "gains_loaded")
    g.f_qT, g.f_kT = g.take(8, TOKENS), g.take(8, TOKENS)
    g.f_v = g.take(5, D)
    g.f_logit = g.take(5, FH)
    mark = g.top
    gain = g.take(2, FD)
    sq, qn = g.take(2, 512), g.take(2, 512)
    ss = g.take(2, 8)
    units = [(kind, 2 * "qkv".index(kind) + half, t) for kind in "qkv" for half in range(2) for t in ALLT] + [("f", 6, t) for t in ALLT]
    freed, na, nv = [], 0, 0
    for kind, *_ in units:
        if kind in "vf":
            na += 1
            freed.append((freed_a, na))
        else:
            nv += 1
            freed.append((freed_v, nv))
    qk = [u for u in units if u[0] in "qk"]
    NB = 6
    heads = lambda ap: ap.rearrange("p (g d) -> p g d", d=FD)
    with nc.Block() as block:
        @block.tensor
        def _(pe):
            def turn(i):
                n = TILES[qk[i][2]][1]
                pe.wait_ge(*normed.at(i + 1))
                if i - 1 > 0:
                    pe.wait_ge(*placed.at(i - 1))
                for j in range(4):
                    last = nc.tensor.transpose(g.psum[:, 6 + i % 2, j * P:j * P + n], qn[0:n, i % 2, j * P:(j + 1) * P], g.c("identity")[0:n, 0:n])
                last.then_inc(*transposed.up())

            i = 0
            for u, (kind, c, t) in enumerate(units):
                n = TILES[t][1]
                if u == 0 or units[u - 1][1] != c:
                    g.weights_wait(pe, chunks[c])
                if u >= NB:
                    pe.wait_ge(*freed[u - NB][0].at(freed[u - NB][1]))
                rows_by_weights(g, pe, g.psum[0:n, u % NB, 0:FH if kind == "f" else 512], t, chunks[c]).then_inc(*ready.up())
                if u + 1 == len(units) or units[u + 1][1] != c:
                    g.chunk_used(chunks[c], ready)
                if 2 <= i + (kind in "qk") and i < len(qk) + 2:
                    if i >= 2:
                        turn(i - 2)
                i += 1

        @block.sync
        def _(sp):
            sp.dma_start(gain[:, 0, :], g.a["fox_q_norm_2"].to_broadcast([P, FD])).then_inc(*gains_in.up(16))
            sp.dma_start(gain[:, 1, :], g.a["fox_k_norm_2"].to_broadcast([P, FD])).then_inc(*gains_in.up(16))
            g.feed(sp, ring_upto)

        @block.scalar
        def _(act):
            def place(i):
                kind, c, t = qk[i]
                a, n = TILES[t]
                dst = g.f_qT if kind == "q" else g.f_kT
                act.wait_ge(*transposed.at(i + 1))
                nc.scalar.activation(dst[:, 4 * (c % 2):4 * (c % 2) + 4, a:a + n], g.psum[:, 6 + i % 2, :].rearrange("p (h n) -> p h n", h=4)[:, :, 0:n], ACT.Copy).then_inc(*placed.up())

            for u, (kind, c, t) in enumerate(units):
                n = TILES[t][1]
                act.wait_ge(*ready.at(u + 1))
                bank = g.psum[0:n, u % NB, :]
                if kind in "qk":
                    if u - 1 > 0:
                        act.wait_ge(*summed.at(u - 1))
                    nc.scalar.activation(sq[0:n, u % 2, :], bank, ACT.Square).then_inc(*squared.up())
                elif kind == "v":
                    nc.scalar.activation(g.f_v[0:n, t, 512 * (c - 4):512 * (c - 3)], bank, ACT.Copy).then_inc(*freed_a.up())
                else:
                    nc.scalar.activation(g.f_logit[0:n, t, :], bank[:, 0:FH], ACT.Copy).then_inc(*freed_a.up())
                if 2 <= u < len(qk) + 2:
                    place(u - 2)

        @block.gpsimd
        def _(pool):
            for i, (kind, c, t) in enumerate(qk):
                n = TILES[t][1]
                pool.wait_ge(*summed.at(i + 1))
                inverse_root(g, pool, ss[0:n, i % 2, :], ss[0:n, i % 2, :], 1.0 / FD, gchain, rooted)

        @block.vector
        def _(dve):
            v = nc.vector
            dve.wait_ge(*gains_in.at(32))
            for i, (kind, c, t) in enumerate(qk):
                n = TILES[t][1]
                dve.wait_ge(*squared.at(i + 1))
                v.tensor_reduce(ss[0:n, i % 2, :], heads(sq[0:n, i % 2, :]), AX.X, ALU.add).then_inc(*summed.up())
                dve.wait_ge(*rooted.at(i + 1))
                if i - 1 > 0:
                    dve.wait_ge(*transposed.at(i - 1))
                buf = heads(qn[0:n, i % 2, :])
                v.tensor_tensor(buf, heads(g.psum[0:n, i % NB, :]), ss[0:n, i % 2, :].unsqueeze(2).to_broadcast([n, 8, FD]), ALU.mult).then_inc(*freed_v.up())
                dve.wait_ge(*freed_v.last())
                v.tensor_tensor(buf, buf, gain[0:n, 0 if kind == "q" else 1, :].unsqueeze(1).to_broadcast([n, 8, FD]), ALU.mult).then_inc(*normed.up())
    g.top = mark


def stage_fox_attention(g, ring_upto):
    nc = g.nc
    mark = g.top
    bias_in, gate, cums, rows, rows_out, scored, peaked, expd, turned, placed, mixed, o_turned, o_placed, chain, achain, taken = g.sig(
        "forget_bias_loaded", "forget_exponents", "cumulated", "gate_row_ready", "gate_row_placed", "scores_ready", "row_peaks", "probabilities",
        "heads_transposed", "heads_placed", "mixed_ready", "rows_transposed", "rows_placed", "vector_step", "scalar_step", "mixed_taken")
    bf = g.take(FH)
    lf = g.take(2, 5 * FH)
    cum = g.take(TOKENS)
    ones = g.take(TOKENS)
    row = g.take(2, TOKENS)
    sc = g.take(2, TOKENS)
    pT = g.take(1, 5 * P)
    peak, total = g.take(2), g.take(2)
    jobs = [(0, 4), (0, 3), (0, 2)] + [job for h in range(1, FH) for job in ((h, 4), (h - 1, 1), (h, 3), (h - 1, 0), (h, 2))] + [(FH - 1, 1), (FH - 1, 0)]
    N = len(jobs)
    keys = lambda t: TILES[t][0] + TILES[t][1]
    window = lambda j: g.psum[:, 2 * (j % 2):2 * (j % 2) + 2, :].rearrange("p b n -> p (b n)")
    flat = lambda n: lf[:, n, :]
    with nc.Block() as block:
        @block.tensor
        def _(pe):
            mm, tr = nc.tensor.matmul, nc.tensor.transpose
            pe.wait_ge(*gate.at(3))
            for t in ALLT:
                a, n = TILES[t]
                dst = g.psum[0:FH, 4, 0:n] if t == 0 else g.psum[0:FH, 5, a - META:a - META + n]
                last = tr(dst, flat(0)[0:n, t * FH:(t + 1) * FH], g.c("identity")[0:n, 0:n])
            last.then_inc(*cums.up())

            def gate_row(h):
                if h >= 1:
                    pe.wait_ge(*rows_out.at(2 * h))
                pick = g.c("identity")[0:FH, h:h + 1].to_broadcast([FH, P])
                mm(g.psum[:, 7, :], pick, cum[0:FH, META:], start=True, stop=True).then_inc(*rows.up())
                pe.wait_ge(*rows_out.at(2 * h + 1))
                mm(g.psum[:, 7, 0:META], pick, cum[0:FH, 0:META], start=True, stop=True).then_inc(*rows.up())

            def scores(j):
                h, t = jobs[j]
                a, n = TILES[t]
                if j - 1 > 0:
                    pe.wait_ge(*peaked.at(j - 1))
                r = slice(64 * (h % 2), 64 * (h % 2) + 64)
                w, q, c = window(j), g.f_qT[r, h // 2, a:a + n], h // 2
                if t == 0:
                    mm(w[0:n, 496:512], q, g.f_kT[r, c, 0:META], start=True, stop=False)
                    mm(w[0:n, 496:512], g.c("identity")[0:n, 0:n], g.c("causal")[0:n, 0:n], start=False, stop=True).then_inc(*scored.up())
                else:
                    mm(w[:, 496:512], q, g.f_kT[r, c, 0:META], start=True, stop=True)
                    mm(w[:, 512:512 + t * P], q, g.f_kT[r, c, META:keys(t)], start=True, stop=False)
                    mm(w[:, 512 + (t - 1) * P:512 + t * P], g.c("identity"), g.c("causal"), start=False, stop=True).then_inc(*scored.up())

            def turn(j):
                h, t = jobs[j]
                n = TILES[t][1]
                pe.wait_ge(*expd.at(j + 1))
                if j > 0:
                    pe.wait_ge(*placed.at(j))
                for k in range(t + 1):
                    a, m = TILES[k]
                    dst = g.psum[0:META, 5, 0:n] if k == 0 else g.psum[:, 4, (k - 1) * P:(k - 1) * P + n]
                    last = tr(dst, sc[0:n, j % 2, a:a + m], g.c("identity")[0:n, 0:n])
                last.then_inc(*turned.up())

            def values(j):
                h, t = jobs[j]
                n = TILES[t][1]
                pe.wait_ge(*placed.at(j + 1))
                if j > 0:
                    pe.wait_ge(*taken.at(j))
                left = [pT[0:META, 0, 4 * P:4 * P + n]] + [pT[:, 0, (k - 1) * P:k * P] for k in range(1, t + 1)]
                right = [g.f_v[0:TILES[k][1], k, h * FD:(h + 1) * FD] for k in range(t + 1)]
                products(nc, g.psum[0:n, 6, 0:FD], left, right).then_inc(*mixed.up())

            pe.wait_ge(*cums.at(2))
            gate_row(0)
            gate_row(1)
            scores(0)
            for j in range(N):
                h, t = jobs[j]
                if t == 0 and h + 2 < FH:
                    gate_row(h + 2)
                if j + 1 < N:
                    scores(j + 1)
                if j:
                    values(j - 1)
                turn(j)
            values(N - 1)
            if N > 0:
                pe.wait_ge(*taken.at(N))
            for i, t in enumerate(ALLT):
                n = TILES[t][1]
                if 2 * (i - 1) > 0:
                    pe.wait_ge(*o_placed.at(2 * (i - 1)))
                for c in range(KD):
                    last = tr(g.psum[:, 2 * (i % 2) + c // 4, (c % 4) * P:(c % 4) * P + n], g.f_v[0:n, t, c * P:(c + 1) * P], g.c("identity")[0:n, 0:n])
                last.then_inc(*o_turned.up())

        @block.sync
        def _(sp):
            sp.dma_start(bf, g.a["fox_b_f_2"].to_broadcast([P, FH])).then_inc(*bias_in.up(16))
            g.feed(sp, ring_upto)
            zero_expert_rows(g, sp)

        @block.scalar
        def _(act):
            act.wait_ge(*gate.at(1))
            nc.scalar.activation(flat(1), flat(1), ACT.Exp, scale=-1.0).then_inc(*achain.up())
            act.wait_ge(*achain.last())
            act.wait_ge(*gate.at(2))
            nc.scalar.activation(flat(1), flat(1), ACT.Ln).then_inc(*achain.up())

            def place_row(h):
                if h >= 2:
                    act.wait_ge(*peaked.at(jobs.index((h - 2, 0)) + 1))
                act.wait_ge(*rows.at(2 * h + 1))
                nc.scalar.activation(row[:, h % 2, META:], g.psum[:, 7, :], ACT.Copy).then_inc(*rows_out.up())
                act.wait_ge(*rows.at(2 * h + 2))
                nc.scalar.activation(row[:, h % 2, 0:META], g.psum[:, 7, 0:META], ACT.Copy).then_inc(*rows_out.up())

            def place(j):
                h, t = jobs[j]
                n = TILES[t][1]
                act.wait_ge(*turned.at(j + 1))
                if j > 0:
                    act.wait_ge(*mixed.at(j))
                first = nc.scalar.activation(pT[0:META, 0, 4 * P:4 * P + n], g.psum[0:META, 5, 0:n], ACT.Copy)
                if t:
                    nc.scalar.activation(pT[:, 0, 0:t * P], g.psum[:, 4, 0:t * P], ACT.Copy).then_inc(*placed.up())
                else:
                    first.then_inc(*placed.up())

            place_row(0)
            place_row(1)
            for j, (h, t) in enumerate(jobs):
                n, w = TILES[t][1], keys(t)
                act.wait_ge(*peaked.at(j + 1))
                if j - 1 > 0:
                    act.wait_ge(*taken.at(j - 1))
                nc.scalar.activation(sc[0:n, j % 2, 0:w], sc[0:n, j % 2, 0:w], ACT.Exp, bias=peak[0:n, j % 2:j % 2 + 1], accum_out=total[0:n, j % 2:j % 2 + 1]).then_inc(*expd.up())
                if t == 0 and h + 2 < FH:
                    place_row(h + 2)
                place(j)

        @block.vector
        def _(dve):
            v = nc.vector
            dve.wait_ge(*bias_in.at(16))
            v.memset(lf, 0.0).then_inc(*chain.up())
            dve.wait_ge(*chain.last())
            for t in ALLT:
                n = TILES[t][1]
                v.tensor_tensor(flat(0)[0:n, t * FH:(t + 1) * FH], g.f_logit[0:n, t, :], bf[0:n, :], ALU.add).then_inc(*chain.up())
                dve.wait_ge(*chain.last())
            v.tensor_scalar(flat(1), flat(0), -1.0, None, ALU.mult).then_inc(*chain.up())
            dve.wait_ge(*chain.last())
            v.tensor_tensor(flat(1), flat(0), flat(1), ALU.max).then_inc(*gate.up())
            v.memset(ones, 1.0).then_inc(*chain.up())
            v.tensor_scalar(g.f_qT, g.f_qT, FD ** -0.5, None, ALU.mult).then_inc(*chain.up())
            dve.wait_ge(*chain.last())
            dve.wait_ge(*achain.at(1))
            v.tensor_scalar(flat(1), flat(1), 1.0, None, ALU.add).then_inc(*gate.up())
            dve.wait_ge(*achain.at(2))
            v.scalar_tensor_tensor(flat(0), flat(0), 0.0, flat(1), ALU.min, ALU.subtract).then_inc(*gate.up())
            dve.wait_ge(*cums.at(1))
            v.tensor_tensor_scan(cum[0:FH, 0:META], ones[0:FH, 0:META], g.psum[0:FH, 4, 0:META], 0.0, ALU.mult, ALU.add).then_inc(*chain.up())
            dve.wait_ge(*chain.last())
            v.tensor_tensor_scan(cum[0:FH, META:], ones[0:FH, META:], g.psum[0:FH, 5, :], cum[0:FH, META - 1:META], ALU.mult, ALU.add).then_inc(*cums.up())

            def peaks(j):
                h, t = jobs[j]
                n, w = TILES[t][1], keys(t)
                q = peak[0:n, j % 2:j % 2 + 1]
                dve.wait_ge(*scored.at(j + 1))
                dve.wait_ge(*rows_out.at(2 * h + 2))
                if j - 1 > 0:
                    dve.wait_ge(*turned.at(j - 1))
                v.tensor_tensor_reduce(out=sc[0:n, j % 2, 0:w], in0=window(j)[0:n, 496:496 + w], in1=row[0:n, h % 2, 0:w], scale=1.0, scalar=-3e38,
                                            op0=ALU.subtract, op1=ALU.max, accum_out=q).then_inc(*chain.up())
                dve.wait_ge(*chain.last())
                v.tensor_scalar(q, q, -1.0, None, ALU.mult).then_inc(*peaked.up())

            def take(j):
                h, t = jobs[j]
                n = TILES[t][1]
                dve.wait_ge(*mixed.at(j + 1))
                s = total[0:n, j % 2:j % 2 + 1]
                v.reciprocal(s, s).then_inc(*chain.up())
                dve.wait_ge(*chain.last())
                v.tensor_scalar(g.f_v[0:n, t, h * FD:(h + 1) * FD], g.psum[0:n, 6, 0:FD], s, None, ALU.mult).then_inc(*taken.up())

            for j in range(N + 1):
                if j < N:
                    peaks(j)
                if j >= 1:
                    take(j - 1)
            for i, t in enumerate(ALLT):
                a, n = TILES[t]
                for half in range(2):
                    dve.wait_ge(*o_turned.at(i + 1))
                    v.tensor_copy(g.hT[:, 4 * half:4 * half + 4, a:a + n], g.psum[:, 2 * (i % 2) + half, :].rearrange("p (c n) -> p c n", c=4)[:, :, 0:n]).then_inc(*o_placed.up())
    g.top = mark



class ExpertWeights:

    def __init__(self, g, layer):
        self.up = [g.ring[:, 0:2, :].rearrange("p a (k n) -> p (a k) n", k=4), g.take(KD, D)]
        self.down = [g.ring[:, 2 + n, :].rearrange("p (k n) -> p k n", k=4) for n in range(2)]
        self.up_in = g.sig("up_loaded_0", "up_loaded_1")
        self.down_in = g.sig("down_loaded_0", "down_loaded_1")
        self.wu, self.wd = g.a["moe_w_up_2"][layer], g.a["moe_w_down_2"][layer]

    def load_up(self, sp, e, n):
        return sp.dma_start(self.up[n], self.wu[bass.ds(e, 1)].rearrange("a (k p) f -> p (a k) f", p=P))

    def load_down(self, sp, e, n):
        return sp.dma_start(self.down[n], self.wd[bass.ds(e, 1)].rearrange("a (k p) f -> p (a k) f", p=P))

    def first_pair(self, sp):
        for n in range(2):
            self.load_up(sp, n, n).then_inc(self.up_in[n].sem, 16)
            self.load_down(sp, n, n).then_inc(self.down_in[n].sem, 16)


class Router:

    def __init__(self, g, layer):
        self.layer, self.a = layer, g.a
        self.w = g.take(KD, GROUPS + NEXP)
        self.bias = g.take(GROUPS + NEXP)
        self.loaded = g.sig("router_loaded")

    def load(self, sp):
        w, bias, a, n = self.w, self.bias, self.a, self.layer
        sp.dma_start(w[:, :, 0:GROUPS], a["moe_w_grp_2"][n].rearrange("(k p) n -> p k n", p=P), allow_slow_non_contiguous=True).then_inc(*self.loaded.up(16))
        sp.dma_start(w[:, :, GROUPS:], a["moe_w_rt_2"][n].rearrange("(k p) n -> p k n", p=P)).then_inc(*self.loaded.up(16))
        sp.dma_start(bias[:, 0:GROUPS], a["moe_b_grp_2"][n:n + 1].to_broadcast([P, GROUPS])).then_inc(*self.loaded.up(16))
        sp.dma_start(bias[:, GROUPS:], a["moe_b_rt_2"][n:n + 1].to_broadcast([P, NEXP])).then_inc(*self.loaded.up(16))


def moe_layer(g, layer, ring_upto):
    g.top = 0
    keep = g.take(5, D)
    gw = g.take(2, 5)
    dest = g.take(2, 5).bitcast(I32)
    over = g.take(OVER + 1).bitcast(I32)
    g.top += (-g.top) % 8
    weights = ExpertWeights(g, layer)
    router = Router(g, layer)

    def ahead(sp):
        router.load(sp)
        weights.first_pair(sp)

    stage_norm(g, ALLT, g.gain(4 + layer), g.fed, keep, ahead)
    stage_route(g, router, gw, dest, over)
    stage_dispatch(g, keep, dest)
    stage_experts(g, layer, over, weights)
    g.top = 5 * D + 64
    stage_combine(g, gw, dest, ring_upto)
    g.top = 0


def stage_route(g, router, gw, dest, over):
    nc = g.nc
    mark = g.top
    loaded = router.loaded
    ready, chain, gated, gate_exp, counted, counts_ready, placed = g.sig(
        "product_ready", "vector_step", "group_shifts", "gate_exps", "assignments_ready", "counts_ready", "logits_placed")
    NL = GROUPS + NEXP
    w, bias = router.w, router.bias
    L = g.take(5, NL)
    one = g.take(P)
    gs, ge = g.take(5, GROUPS), g.take(5, GROUPS)
    goh = g.take(5, GROUPS)
    gm, gsum = g.take(5), g.take(5)
    pick = g.take(5, NEXP)
    el, e2 = g.take(5, EPG), g.take(5, EPG)
    oh = g.take(2, 5 * EPG)
    m1, m2, ex, den, idx = (g.take(5) for _ in range(5))
    OH = g.take(2, 5 * NEXP)
    both = g.take(5, NEXP)
    C = g.take(5, NEXP)
    cnt, ovb, inc, base, obase = (g.take(NEXP) for _ in range(5))
    big = g.take(OVER * NEXP)
    t1, t2 = g.take(5, NEXP), g.take(5, NEXP)
    rank, lo, hi, past = (g.take(5) for _ in range(4))
    ovf = g.take(OVER + 1)
    bc = lambda ap, n: ap.unsqueeze(2).to_broadcast([P, 5, n])
    row = lambda ap, n: ap.unsqueeze(1).to_broadcast([P, 5, n])
    with nc.Block() as block:
        @block.tensor
        def _(pe):
            pe.wait_ge(*loaded.at(64))
            for i, t in enumerate(ALLT):
                a, n = TILES[t]
                last = products(nc, g.psum[0:n, i, 0:NL], [g.hT[:, k, a:a + n] for k in range(KD)], [w[:, k, :] for k in range(KD)])
                last.then_inc(*ready.up())
            pe.wait_ge(*counted.at(1))
            for i, t in enumerate(ALLT):
                n = TILES[t][1]
                left = [one[0:TILES[k][1], 0:n] for k in range(t)] + [g.c("before")[0:n, 0:n]]
                products(nc, g.psum[0:n, 5, i * NEXP:(i + 1) * NEXP], left, [both[0:TILES[k][1], k, :] for k in range(t + 1)])
            products(nc, g.psum[:, 6, 0:NEXP], [one[0:TILES[k][1], :] for k in ALLT], [both[0:TILES[k][1], k, :] for k in ALLT]).then_inc(*counts_ready.up())

        @block.scalar
        def _(act):
            act.wait_ge(*gated.at(1))
            nc.scalar.activation(ge, gs, ACT.Exp).then_inc(*gate_exp.up())
            act.wait_ge(*gated.at(2))
            nc.scalar.activation(ex, ex, ACT.Exp).then_inc(*gate_exp.up())

        @block.vector
        def _(dve):
            v = nc.vector
            TT, TS = v.tensor_tensor, v.tensor_scalar

            def first(onehot, values, peak, index, n):
                it = row(g.c("iota")[:, 0:n], n)
                TT(onehot, values, bc(peak, n), ALU.is_equal).then_inc(*chain.up())
                dve.wait_ge(*chain.last())
                TS(onehot, onehot, -1000.0, 1000.0, ALU.mult, ALU.add).then_inc(*chain.up())
                dve.wait_ge(*chain.last())
                TT(onehot, onehot, it, ALU.add).then_inc(*chain.up())
                dve.wait_ge(*chain.last())
                v.tensor_reduce(index, onehot, AX.X, ALU.min).then_inc(*chain.up())
                dve.wait_ge(*chain.last())
                TT(onehot, it, bc(index, n), ALU.is_equal).then_inc(*chain.up())
                dve.wait_ge(*chain.last())

            v.memset(L, 0.0).then_inc(*chain.up())
            dve.wait_ge(*chain.last())
            v.memset(one, 1.0).then_inc(*chain.up())
            dve.wait_ge(*chain.last())
            v.memset(C, 0.0).then_inc(*chain.up())
            dve.wait_ge(*chain.last())
            dve.wait_ge(*loaded.at(64))
            for i, t in enumerate(ALLT):
                n = TILES[t][1]
                dve.wait_ge(*ready.at(i + 1))
                TT(L[0:n, t, :], g.psum[0:n, i, 0:NL], bias[0:n, :], ALU.add).then_inc(*chain.up())
                dve.wait_ge(*chain.last())
            G = L[:, :, 0:GROUPS]
            v.tensor_reduce(gm, G, AX.X, ALU.max).then_inc(*chain.up())
            dve.wait_ge(*chain.last())
            TT(gs, G, bc(gm, GROUPS), ALU.subtract).then_inc(*gated.up())
            first(goh, G, gm, idx, GROUPS)
            E = L[:, :, GROUPS:].rearrange("p t (g e) -> p t g e", g=GROUPS)
            pk = pick.rearrange("p t (g e) -> p t g e", g=GROUPS)
            for t in ALLT:
                TT(pk[:, t, :, :], E[:, t, :, :], goh[:, t, :].unsqueeze(2).to_broadcast([P, GROUPS, EPG]), ALU.mult).then_inc(*chain.up())
                dve.wait_ge(*chain.last())
            v.tensor_reduce(el, pick.rearrange("p t (g e) -> p t e g", g=GROUPS), AX.X, ALU.add).then_inc(*chain.up())
            dve.wait_ge(*chain.last())
            o1 = oh[:, 0, :].rearrange("p (t e) -> p t e", t=5)
            o2 = oh[:, 1, :].rearrange("p (t e) -> p t e", t=5)
            v.tensor_reduce(m1, el, AX.X, ALU.max).then_inc(*chain.up())
            dve.wait_ge(*chain.last())
            first(o1, el, m1, idx, EPG)
            TS(e2, o1, -3e38, None, ALU.mult).then_inc(*chain.up())
            dve.wait_ge(*chain.last())
            TT(e2, e2, el, ALU.add).then_inc(*chain.up())
            dve.wait_ge(*chain.last())
            v.tensor_reduce(m2, e2, AX.X, ALU.max).then_inc(*chain.up())
            dve.wait_ge(*chain.last())
            first(o2, e2, m2, idx, EPG)
            TT(ex, m2, m1, ALU.subtract).then_inc(*gated.up())
            for k, o in enumerate((o1, o2)):
                for t in ALLT:
                    dst = OH[:, k, t * NEXP:(t + 1) * NEXP].rearrange("p (g e) -> p g e", g=GROUPS)
                    TT(dst, goh[:, t, :].unsqueeze(2).to_broadcast([P, GROUPS, EPG]), o[:, t, :].unsqueeze(1).to_broadcast([P, GROUPS, EPG]), ALU.mult).then_inc(*chain.up())
                    dve.wait_ge(*chain.last())
            TT(both.rearrange("p t e -> p (t e)"), OH[:, 0, :], OH[:, 1, :], ALU.add).then_inc(*counted.up())
            dve.wait_ge(*gate_exp.at(2))
            v.tensor_reduce(gsum, ge, AX.X, ALU.add).then_inc(*chain.up())
            dve.wait_ge(*chain.last())
            TS(den, ex, 1.0, None, ALU.add).then_inc(*chain.up())
            dve.wait_ge(*chain.last())
            TT(den, den, gsum, ALU.mult).then_inc(*chain.up())
            dve.wait_ge(*chain.last())
            v.reciprocal(gw[:, 0, :], den).then_inc(*chain.up())
            dve.wait_ge(*chain.last())
            TT(gw[:, 1, :], gw[:, 0, :], ex, ALU.mult).then_inc(*chain.up())
            dve.wait_ge(*chain.last())
            dve.wait_ge(*counts_ready.at(1))
            for i, t in enumerate(ALLT):
                n = TILES[t][1]
                v.tensor_copy(C[0:n, t, :], g.psum[0:n, 5, i * NEXP:(i + 1) * NEXP]).then_inc(*chain.up())
                dve.wait_ge(*chain.last())
            v.tensor_copy(cnt, g.psum[:, 6, 0:NEXP]).then_inc(*chain.up())
            dve.wait_ge(*chain.last())
            bg = big[:, 0:NEXP * 8].rearrange("p (e j) -> p e j", e=NEXP)
            TT(bg, cnt.unsqueeze(2).to_broadcast([P, NEXP, 8]), g.c("steps").unsqueeze(1).to_broadcast([P, NEXP, 8]), ALU.is_gt).then_inc(*chain.up())
            dve.wait_ge(*chain.last())
            v.tensor_reduce(ovb, bg, AX.X, ALU.add).then_inc(*chain.up())
            dve.wait_ge(*chain.last())
            v.tensor_tensor_scan(inc, one[:, 0:NEXP], ovb, 0.0, ALU.mult, ALU.add).then_inc(*chain.up())
            dve.wait_ge(*chain.last())
            TS(base, g.c("iota"), float(ROWS), None, ALU.mult).then_inc(*chain.up())
            dve.wait_ge(*chain.last())
            TT(obase, inc, ovb, ALU.subtract).then_inc(*chain.up())
            dve.wait_ge(*chain.last())
            TS(obase, obase, float(ROWS), float(NEXP * ROWS - ROWS), ALU.mult, ALU.add).then_inc(*chain.up())
            dve.wait_ge(*chain.last())
            for k in range(2):
                oh_k = OH[:, k, :].rearrange("p (t e) -> p t e", t=5)
                for dst, src in ((rank, C), (lo, row(base, NEXP)), (hi, row(obase, NEXP))):
                    TT(t1, oh_k, src, ALU.mult).then_inc(*chain.up())
                    dve.wait_ge(*chain.last())
                    v.tensor_reduce(dst, t1, AX.X, ALU.add).then_inc(*chain.up())
                    dve.wait_ge(*chain.last())
                TS(past, rank, float(ROWS), None, ALU.is_ge).then_inc(*chain.up())
                dve.wait_ge(*chain.last())
                TT(hi, hi, lo, ALU.subtract).then_inc(*chain.up())
                dve.wait_ge(*chain.last())
                TT(hi, hi, past, ALU.mult).then_inc(*chain.up())
                dve.wait_ge(*chain.last())
                TT(lo, lo, hi, ALU.add).then_inc(*chain.up())
                dve.wait_ge(*chain.last())
                TT(lo, lo, rank, ALU.add).then_inc(*chain.up())
                dve.wait_ge(*chain.last())
                v.tensor_copy(dest[:, k, :], lo).then_inc(*chain.up())
                dve.wait_ge(*chain.last())
            bo = big.rearrange("p (j e) -> p j e", j=OVER)
            TT(bo, inc.unsqueeze(1).to_broadcast([P, OVER, NEXP]), g.c("overs").unsqueeze(2).to_broadcast([P, OVER, NEXP]), ALU.is_le).then_inc(*chain.up())
            dve.wait_ge(*chain.last())
            v.tensor_reduce(ovf[:, 0:OVER], bo, AX.X, ALU.add).then_inc(*chain.up())
            dve.wait_ge(*chain.last())
            TS(ovf[:, 0:OVER], ovf[:, 0:OVER], float(NEXP - 1), None, ALU.min).then_inc(*chain.up())
            dve.wait_ge(*chain.last())
            v.tensor_copy(ovf[:, OVER:], inc[:, NEXP - 1:]).then_inc(*chain.up())
            dve.wait_ge(*chain.last())
            v.tensor_copy(over, ovf).then_inc(*placed.up())
    g.top = mark


def stage_dispatch(g, keep, dest):
    nc = g.nc
    sent = g.sig("rows_sent")
    with nc.Block() as block:
        @block.gpsimd
        def _(pool):
            pool.wait_ge(*g.x_rows_zeroed.at(32))
            for k in range(2):
                for t in ALLT:
                    n = TILES[t][1]
                    nc.gpsimd.indirect_dma_start(out=g.a["x_rows"], out_offset=bass.IndirectOffsetOnAxis(ap=dest[0:n, k, t:t + 1], axis=0),
                                                         in_=keep[0:n, t, :], in_offset=None).then_inc(*sent.up(16))
            pool.wait_ge(*sent.last())


def stage_experts(g, layer, over, weights):
    nc = g.nc
    mark = g.top
    names = ["rows_loaded", "rows_transposed", "rows_placed", "up_ready",
             "gated", "gate_silu", "hidden_transposed", "hidden_placed", "down_ready", "result_placed", "result_free_0", "result_free_1"]
    x_in, x_turned, x_placed, up_ready, hid, silu, h_turned, h_placed, dn_ready, y_placed, y_free0, y_free1 = g.sig(*names)
    up_in, dn_in, y_free = weights.up_in, weights.down_in, (y_free0, y_free1)
    gain = g.gain(4 + layer)
    up, down = weights.up, weights.down
    x = g.hT[:, 0:2, 0:512]
    xT = g.hT[:, 2:4, 0:512].rearrange("p a (k r) -> p a k r", k=4)
    s = g.hT[:, 6, 0:256]
    act_ = g.hT[:, 6, 256:512]
    aT = g.hT[:, 7, 0:256].rearrange("p (j r) -> p j r", j=2)
    y = [g.take(512), g.take(512)]
    xr, yr = g.a["x_rows"], g.a["y_rows"]
    PAIRS = NEXP // 2

    def load_rows(sp, blk, rows):
        return sp.dma_start(x[0:rows, :, :], xr[bass.ds(blk * ROWS, rows)].rearrange("r (a c) -> r a c", a=2))

    def tensor_rows():
        for c in range(KD):
            last = nc.tensor.transpose(g.psum[:, c // 4, (c % 4) * P:(c % 4 + 1) * P], x[:, c // 4, (c % 4) * P:(c % 4 + 1) * P], g.c("identity"))
        return last

    def place_rows():
        for a in range(2):
            last = nc.vector.tensor_tensor(xT[:, a, :, :], g.psum[:, a, :].rearrange("p (k r) -> p k r", k=4), gain[:, 4 * a:4 * a + 4].unsqueeze(2).to_broadcast([P, 4, P]), ALU.mult)
        return last

    def tensor_up(n):
        wv = up[n].rearrange("p k (s q c) -> p k q s c", s=2, q=2)
        for k in range(KD):
            for q in range(2):
                last = nc.tensor.matmul(g.psum[64 * q:64 * q + 64, 2 + n, :].rearrange("p (s c) -> p s c", s=2), xT[:, k // 4, k % 4, ROWS * n:ROWS * n + ROWS], wv[:, k, q, :, :], start=k == 0, stop=k == KD - 1)
        return last

    def tensor_hidden():
        for j in range(2):
            last = nc.tensor.transpose(g.psum[:, 4, j * P:(j + 1) * P], act_[:, j * P:(j + 1) * P], g.c("identity"))
        return last

    def tensor_down(n):
        for k in range(4):
            for q in range(2):
                last = nc.tensor.matmul(g.psum[64 * q:64 * q + 64, 6 + n, :], aT[:, k % 2, 64 * (k // 2):64 * (k // 2) + 64], down[n][:, k, 512 * q:512 * q + 512], start=k == 0, stop=k == 3)
        return last

    def store(eng, blk, n):
        rows = yr[bass.ds(blk * ROWS, ROWS)]
        a = eng.dma_start(rows[:, 0:512], y[n][0:64, :])
        b = eng.dma_start(rows[:, 512:], y[n][64:128, :])
        return a, b

    with nc.Block() as block:
        @block.sync
        def _(sp):
            load_rows(sp, 0, P).then_inc(x_in.sem, 16)
            with sp.Fori(1, PAIRS) as i:
                sp.wait_ge(x_turned.sem, i + x_turned.base)
                load_rows(sp, 2 * i, P).then_inc(x_in.sem, 16)
                for n in range(2):
                    sp.wait_ge(up_ready.sem, 2 * i + (up_ready.base + n - 1))
                    weights.load_up(sp, 2 * i + n, n).then_inc(up_in[n].sem, 16)
                    sp.wait_ge(dn_ready.sem, 2 * i + (dn_ready.base + n - 1))
                    weights.load_down(sp, 2 * i + n, n).then_inc(dn_in[n].sem, 16)

        @block.tensor
        def _(pe):
            with pe.Fori(0, PAIRS) as i:
                pe.wait_ge(x_in.sem, 16 * i + (x_in.base + 16))
                tensor_rows().then_inc(x_turned.sem, 1)
                pe.wait_ge(x_placed.sem, i + (x_placed.base + 1))
                for n in range(2):
                    pe.wait_ge(up_in[n].sem, 16 * i + (up_in[n].base + 16))
                    tensor_up(n).then_inc(up_ready.sem, 1)
                    pe.wait_ge(hid.sem, 2 * i + (hid.base + n + 1))
                    tensor_hidden().then_inc(h_turned.sem, 1)
                    pe.wait_ge(h_placed.sem, 2 * i + (h_placed.base + n + 1))
                    pe.wait_ge(dn_in[n].sem, 16 * i + (dn_in[n].base + 16))
                    tensor_down(n).then_inc(dn_ready.sem, 1)

        @block.scalar
        def _(act):
            with act.Fori(0, PAIRS) as i:
                for n in range(2):
                    act.wait_ge(up_ready.sem, 2 * i + (up_ready.base + n + 1))
                    nc.scalar.activation(s, g.psum[:, 2 + n, 0:256], ACT.Silu).then_inc(silu.sem, 1)
                    act.wait_ge(h_turned.sem, 2 * i + (h_turned.base + n + 1))
                    nc.scalar.activation(aT.rearrange("p j r -> p (j r)"), g.psum[:, 4, 0:256], ACT.Copy).then_inc(h_placed.sem, 1)
                    act.wait_ge(y_placed.sem, 2 * i + (y_placed.base + n + 1))
                    for ins in store(act, 2 * i + n, n):
                        ins.then_inc(y_free[n].sem, 16)
            for n in range(2):
                act.wait_ge(y_free[n].sem, y_free[n].base + 1 + 32 * PAIRS)

        @block.vector
        def _(dve):
            for n in range(2):
                nc.vector.memset(y[n], 0.0).then_inc(y_free[n].sem, 1)
            with dve.Fori(0, PAIRS) as i:
                dve.wait_ge(x_turned.sem, i + (x_turned.base + 1))
                place_rows().then_inc(x_placed.sem, 1)
                for n in range(2):
                    dve.wait_ge(silu.sem, 2 * i + (silu.base + n + 1))
                    nc.vector.tensor_tensor(act_, s, g.psum[:, 2 + n, 256:512], ALU.mult).then_inc(hid.sem, 1)
                    dve.wait_ge(dn_ready.sem, 2 * i + (dn_ready.base + n + 1))
                    dve.wait_ge(y_free[n].sem, 32 * i + (y_free[n].base + 1))
                    nc.vector.tensor_copy(y[n], g.psum[:, 6 + n, :]).then_inc(y_placed.sem, 1)
    for sig in (x_in, *up_in, *dn_in):
        sig.count = 16 * PAIRS
    x_turned.count = x_placed.count = PAIRS
    for sig in (up_ready, hid, silu, h_turned, h_placed, dn_ready, y_placed):
        sig.count = NEXP
    for sig in y_free:
        sig.count = 1 + 32 * PAIRS

    if not g.over_sems:
        g.over_sems = [g.sem("over_" + n) for n in ("done", "rows", "up", "down", "rows_T", "rows_placed", "up_ready", "silu", "gated", "hidden_T", "hidden_placed", "down_ready", "placed", "stored")]
    done, rows_l, up_l, down_l, rT, rp, ur, si, ga, hT_, hp, dr, pl, st = g.over_sems
    with nc.Block() as block:
        def each(eng, body):
            count = eng.value_load(over[0:1, OVER:OVER + 1], min_val=0, max_val=OVER)
            with eng.If(count > 0):
                with eng.Fori(0, OVER) as j:
                    with eng.If(j < count):
                        body(j)

        @block.sync
        def _(sp):
            def body(j):
                e = sp.value_load(over[0:1, bass.ds(j, 1)], min_val=0, max_val=NEXP - 1)
                sp.wait_ge(done, j + 1)
                load_rows(sp, j + NEXP, ROWS).then_inc(rows_l, 16)
                weights.load_up(sp, e, 0).then_inc(up_l, 16)
                weights.load_down(sp, e, 0).then_inc(down_l, 16)
            each(sp, body)

        @block.tensor
        def _(pe):
            def body(j):
                pe.wait_ge(rows_l, 16 * j + 16)
                tensor_rows().then_inc(rT, 1)
                pe.wait_ge(rp, j + 1)
                pe.wait_ge(up_l, 16 * j + 16)
                tensor_up(0).then_inc(ur, 1)
                pe.wait_ge(ga, j + 1)
                tensor_hidden().then_inc(hT_, 1)
                pe.wait_ge(hp, j + 1)
                pe.wait_ge(down_l, 16 * j + 16)
                tensor_down(0).then_inc(dr, 1)
            each(pe, body)

        @block.scalar
        def _(act):
            def body(j):
                act.wait_ge(ur, j + 1)
                nc.scalar.activation(s, g.psum[:, 2, 0:256], ACT.Silu).then_inc(si, 1)
                act.wait_ge(hT_, j + 1)
                nc.scalar.activation(aT.rearrange("p j r -> p (j r)"), g.psum[:, 4, 0:256], ACT.Copy).then_inc(hp, 1)
                act.wait_ge(pl, j + 1)
                for ins in store(act, j + NEXP, 0):
                    ins.then_inc(st, 16)
                act.wait_ge(st, 32 * j + 32)
                act.sem_inc(done, 1)
            each(act, body)

        @block.vector
        def _(dve):
            nc.vector.memset(y[0], 0.0).then_inc(done, 1)

            def body(j):
                dve.wait_ge(rT, j + 1)
                place_rows().then_inc(rp, 1)
                dve.wait_ge(si, j + 1)
                nc.vector.tensor_tensor(act_, s, g.psum[:, 2, 256:512], ALU.mult).then_inc(ga, 1)
                dve.wait_ge(dr, j + 1)
                nc.vector.tensor_copy(y[0], g.psum[:, 6, :]).then_inc(pl, 1)
            each(dve, body)

    with nc.Block() as block:
        @block.sync
        def _(sp):
            for sem in g.over_sems:
                sp.sem_clear(sem)
    g.top = mark


def stage_combine(g, gw, dest, ring_upto):
    nc = g.nc
    added = g.sig("results_added")
    yb = g.take(10, D)
    jobs = [(t, k) for t in ALLT for k in range(2)]
    if not g.gather_sems:
        g.gather_sems = [g.sem(f"gathered_{n}") for n in range(10)]
    g.gathers += 1
    with nc.Block() as block:
        @block.sync
        def _(sp):
            sp.wait_ge(g.gather_sems[-1], 16 * g.gathers)
            g.feed(sp, ring_upto)

        @block.gpsimd
        def _(pool):
            for n, (t, k) in enumerate(jobs):
                r = TILES[t][1]
                nc.gpsimd.indirect_dma_start(out=yb[0:r, n, :], out_offset=None, in_=g.a["y_rows"],
                                             in_offset=bass.IndirectOffsetOnAxis(ap=dest[0:r, k, t:t + 1], axis=0)).then_inc(g.gather_sems[n], 16)

        @block.vector
        def _(dve):
            for n, (t, k) in enumerate(jobs):
                r = TILES[t][1]
                dve.wait_ge(g.gather_sems[n], 16 * g.gathers)
                if n > 0:
                    dve.wait_ge(*added.at(n))
                nc.vector.scalar_tensor_tensor(g.h[0:r, t, :], yb[0:r, n, :], gw[0:r, k, t:t + 1], g.h[0:r, t, :], ALU.mult, ALU.add).then_inc(*added.up())


def plan_hg(g):
    w = g.a["hg_w_in_2"][0]
    chunks = [g.plan(w[:, 512 * n:512 * n + 512], KD, 512) for n in range(8)]
    out = [g.plan(g.a["hg_w_out_2"][0][:, 512 * n:512 * n + 512], KD, 512) for n in range(2)]
    return chunks, out


def hg_layer(g, plans):
    chunks, out = plans
    g.top = 0
    stage_norm(g, ALLT, g.gain(3), chunks[0] + 4)
    stage_hg_in(g, chunks, out[0] + 1)
    stage_hg_scores(g, out)
    stage_hg_scan(g, out)
    stage_out(g, ALLT, out, out[0] + 2)
    g.top = 0


def stage_hg_in(g, chunks, ring_upto):
    nc = g.nc
    ready, freed, loaded, bound, exps, sig, kept, logs, chain, vfreed = g.sig("product_ready", "bank_read_by_scalar", "gate_weights_loaded", "bound_steps", "bound_exps", "forget_sigmoids", "keys_ready",
                                                                              "log_gates", "vector_step", "bank_read_by_vector")
    g.g_q, g.g_k, g.g_b = g.take(HG, TOKENS), g.take(HG, TOKENS), g.take(HG, TOKENS)
    g.g_v, g.g_g = g.take(5, D), g.take(5, D)
    bf = g.small[:, 400:408]
    lbl = g.small[:, 408:424].rearrange("p (l k) -> p l k", l=2)
    lb, oml = g.small[:, 424:432], g.small[:, 432:440]
    mx = g.small[:, 440:448]
    units = [("q", f // 4, f) for f in range(8)] + [("f", 2 + f // 4, f) for f in range(8)]
    units += [(kind, c, t) for kind, c in (("v", 4), ("v", 5), ("g", 6), ("g", 7)) for t in ALLT]
    window = lambda u: g.psum[:, 2 * (u % 4):2 * (u % 4) + 2, :].rearrange("p b n -> p (b n)")
    order, na, nv = [], 0, 0
    for kind, *_ in units:
        if kind == "v":
            nv += 1
            order.append((vfreed, nv))
        else:
            na += 1
            order.append((freed, na))
    with nc.Block() as block:
        @block.tensor
        def _(pe):
            for u, (kind, c, x) in enumerate(units):
                if u == 0 or units[u - 1][1] != c:
                    g.weights_wait(pe, chunks[c])
                if u >= 4:
                    pe.wait_ge(*order[u - 4][0].at(order[u - 4][1]))
                if kind in "qf":
                    w = g.weights(chunks[c])
                    left = [w[:, k, (x % 4) * P:(x % 4 + 1) * P] for k in range(KD)]
                    products(nc, window(u)[:, 496:512], left, [g.hT[:, k, 0:META] for k in range(KD)])
                    products(nc, window(u)[:, 512:1024], left, [g.hT[:, k, META:] for k in range(KD)]).then_inc(*ready.up())
                else:
                    n = TILES[x][1]
                    rows_by_weights(g, pe, window(u)[0:n, 0:512], x, chunks[c]).then_inc(*ready.up())
                if u + 1 == len(units) or units[u + 1][1] != c:
                    g.chunk_used(chunks[c], ready)

        @block.sync
        def _(sp):
            sp.dma_start(bf, g.a["hg_b_f_2"].rearrange("a (k p) -> p (a k)", p=P), allow_slow_non_contiguous=True).then_inc(*loaded.up(16))
            for n in range(2):
                sp.dma_start(lbl[:, n, :], g.a["hg_lb_logits_2"][n].rearrange("(k p) -> p k", p=P), allow_slow_non_contiguous=True).then_inc(*loaded.up(16))
            g.feed(sp, ring_upto)

        @block.scalar
        def _(act):
            act.wait_ge(*bound.at(1))
            nc.scalar.activation(lbl, lbl, ACT.Exp).then_inc(*exps.up())
            for u, (kind, c, x) in enumerate(units):
                if kind == "v":
                    continue
                if (kind, c, x) == ("g", 6, 0):
                    act.wait_ge(*kept.at(8))
                    nc.scalar.activation(g.g_b, g.g_b, ACT.Ln).then_inc(*logs.up())
                act.wait_ge(*ready.at(u + 1))
                if kind == "q":
                    nc.scalar.activation(g.g_q[:, x, :], window(u)[:, 496:1024], ACT.Silu).then_inc(*freed.up())
                elif kind == "f":
                    nc.scalar.activation(g.g_k[:, x, :], window(u)[:, 496:1024], ACT.Sigmoid, bias=bf[:, x:x + 1]).then_inc(*sig.up())
                    nc.scalar.activation(g.g_b[:, x, 0:1], window(u)[:, 496:497], ACT.Copy).then_inc(*freed.up())
                else:
                    n = TILES[x][1]
                    nc.scalar.activation(g.g_g[0:n, x, 512 * (c - 6):512 * (c - 5)], window(u)[0:n, 0:512], ACT.Silu).then_inc(*freed.up())

        @block.vector
        def _(dve):
            v = nc.vector
            dve.wait_ge(*loaded.at(48))
            v.tensor_tensor(mx, lbl[:, 0, :], lbl[:, 1, :], ALU.max).then_inc(*chain.up())
            dve.wait_ge(*chain.last())
            v.tensor_tensor(lbl, lbl, mx.unsqueeze(1).to_broadcast([P, 2, KD]), ALU.subtract).then_inc(*bound.up())
            dve.wait_ge(*exps.at(1))
            v.tensor_tensor(mx, lbl[:, 0, :], lbl[:, 1, :], ALU.add).then_inc(*chain.up())
            dve.wait_ge(*chain.last())
            v.reciprocal(mx, mx).then_inc(*chain.up())
            dve.wait_ge(*chain.last())
            v.tensor_tensor(lb, lbl[:, 1, :], mx, ALU.mult).then_inc(*chain.up())
            dve.wait_ge(*chain.last())
            v.tensor_scalar(oml, lb, -1.0, 1.0, ALU.mult, ALU.add).then_inc(*chain.up())
            dve.wait_ge(*chain.last())
            for x in range(8):
                dve.wait_ge(*sig.at(x + 1))
                dve.wait_ge(*freed.at(8 + x + 1))
                v.tensor_scalar(g.g_b[:, x, :], g.g_k[:, x, :], oml[:, x:x + 1], lb[:, x:x + 1], ALU.mult, ALU.add).then_inc(*chain.up())
                dve.wait_ge(*chain.last())
                v.tensor_scalar(g.g_k[:, x, :], g.g_b[:, x, :], -1.0, 1.0, ALU.mult, ALU.add).then_inc(*kept.up())
            for u, (kind, c, x) in enumerate(units):
                if kind == "v":
                    n = TILES[x][1]
                    dve.wait_ge(*ready.at(u + 1))
                    v.tensor_copy(g.g_v[0:n, x, 512 * (c - 4):512 * (c - 3)], window(u)[0:n, 0:512]).then_inc(*vfreed.up())
            dve.wait_ge(*logs.at(1))
            for x in range(8):
                v.tensor_tensor_scan(g.g_b[:, x, :], g.c("carry"), g.g_b[:, x, :], 0.0, ALU.mult, ALU.add).then_inc(*chain.up())
            dve.wait_ge(*chain.last())


def stage_hg_scores(g, out):
    nc = g.nc
    spare = g.ring[:, (out[0] + 2) % 4, :]
    cut = lambda n: spare[:, n * TOKENS:(n + 1) * TOKENS]
    diff, xx, masked = [cut(0), cut(1), cut(6)], [cut(2), cut(3)], [cut(4), cut(5)]
    summed, chain = g.sig("first_levels_added", "vector_step")
    subbed, exped, built, producted, maskd, added, applied = g.sig("exponents_ready", "decays_exped", "operands_ready", "product_ready", "scores_masked", "scores_added", "decays_applied")
    A = g.hT
    DIAG, QE, KE = 7, 8, 9
    SPLIT = 3
    jobs = [(h, n) for h in range(HG) for n in range(10)]
    N = len(jobs)
    lev = [j for j, (h, n) in enumerate(jobs) if n < 7]
    prod = [j for j, (h, n) in enumerate(jobs) if n <= DIAG]
    subs = [j for j, (h, n) in enumerate(jobs) if n < 7]
    exps = [j for j, (h, n) in enumerate(jobs) if n != DIAG]
    rank = lambda seq, j: sum(1 for x in seq if x < j)
    window = lambda i: g.psum[:, 2 * (i % 2):2 * (i % 2) + 2, :].rearrange("p b n -> p (b n)")

    def halves(ap, n):
        lo = 0 if n < 4 else META
        return ap[:, lo:].rearrange("p (g two b) -> p g two b", two=2, b=1 << n)

    def built_wait(eng, j):
        if j < 0 or jobs[j][1] == DIAG:
            return
        if jobs[j][1] < 7:
            eng.wait_ge(*built.at(2 * rank(lev, j) + 2))
        else:
            if 2 * jobs[j][0] + jobs[j][1] - QE + 1 > 0:
                eng.wait_ge(*applied.at(2 * jobs[j][0] + jobs[j][1] - QE + 1))

    def added_wait(eng, i):
        if i < 0:
            return
        n = 0
        for j in prod[:i + 1]:
            level = jobs[j][1]
            n += 0 if level < SPLIT else 2 if level < 4 or level == DIAG else 1
        if n > 0:
            eng.wait_ge(*added.at(n))

    with nc.Block() as block:
        @block.gpsimd
        def _(pool):
            op = nc.gpsimd.tensor_tensor

            def add(i):
                h, n = jobs[prod[i]]
                pool.wait_ge(*maskd.at(i + 1))
                m = masked[i % 2]
                lo = 0 if n < 4 or n == DIAG else META
                if n < SPLIT:
                    return
                pool.wait_ge(*summed.at(h + 1))
                pool.wait_ge(*added.last())
                if lo == 0:
                    op(A[0:META, h, 0:META], A[0:META, h, 0:META], m[0:META, 0:META], ALU.add).then_inc(*added.up())
                    op(A[:, h, META:], A[:, h, META:], m[:, META:], ALU.add).then_inc(*added.up())
                else:
                    op(A[:, h, META:], A[:, h, META:], m[:, META:], ALU.add).then_inc(*added.up())

            done = 0
            for j, (h, n) in enumerate(jobs):
                d, b = diff[j % 3], g.g_b[:, h, :]
                if n < 7:
                    built_wait(pool, j - 3)
                    dv, bv = halves(d, n), halves(b, n)
                    mid = bv[:, :, 0, (1 << n) - 1:1 << n].to_broadcast(list(bv[:, :, 0, :].shape))
                    op(dv[:, :, 0, :], mid, bv[:, :, 0, :], ALU.subtract).then_inc(*subbed.up())
                    op(dv[:, :, 1, :], bv[:, :, 1, :], mid, ALU.subtract).then_inc(*subbed.up())
                while done < len(prod) and prod[done] <= j - 3:
                    add(done)
                    done += 1
            while done < len(prod):
                add(done)
                done += 1
            if added.count:
                pool.wait_ge(*added.last())

        @block.scalar
        def _(act):
            for j, (h, n) in enumerate(jobs):
                if n == DIAG:
                    continue
                d = diff[j % 3]
                if n == QE:
                    built_wait(act, j - 3)
                    nc.scalar.activation(d, g.g_b[:, h, :], ACT.Exp).then_inc(*exped.up())
                elif n == KE:
                    built_wait(act, j - 3)
                    for a, m in TILES:
                        last = nc.scalar.activation(d[:, a:a + m], g.g_b[:, h, a:a + m], ACT.Exp, scale=-1.0, bias=g.g_b[:, h, a + m - 1:a + m])
                    last.then_inc(*exped.up())
                else:
                    lo = 0 if n < 4 else META
                    act.wait_ge(*subbed.at(2 * rank(subs, j) + 2))
                    nc.scalar.activation(d[:, lo:], d[:, lo:], ACT.Exp).then_inc(*exped.up())

        @block.vector
        def _(dve):
            v = nc.vector

            def mask(i):
                h, n = jobs[prod[i]]
                name = "identity" if n == DIAG else f"half{n}"
                dve.wait_ge(*producted.at(i + 1))
                added_wait(dve, i - 2)
                dst = A[:, h, :] if n == 0 else masked[i % 2]
                main = lambda ap: ap[:, META:].rearrange("p (t n) -> p t n", t=4)
                if n < 4 or n == DIAG:
                    v.tensor_tensor(dst[0:META, 0:META], window(i)[0:META, 496:512], g.c(name)[0:META, 0:META], ALU.mult).then_inc(*chain.up())
                v.tensor_tensor(main(dst), window(i)[:, 512:].rearrange("p (t n) -> p t n", t=4), g.c(name).unsqueeze(1).to_broadcast([P, 4, P]), ALU.mult).then_inc(*maskd.up())
                if 0 < n < SPLIT:
                    dve.wait_ge(*maskd.last())
                    dve.wait_ge(*chain.last())
                    v.tensor_tensor(A[0:META, h, 0:META], A[0:META, h, 0:META], dst[0:META, 0:META], ALU.add).then_inc(*chain.up())
                    v.tensor_tensor(A[:, h, META:], A[:, h, META:], dst[:, META:], ALU.add).then_inc(*(summed if n == SPLIT - 1 else chain).up())

            done = 0
            for j, (h, n) in enumerate(jobs):
                d = diff[j % 3]
                if n < 7:
                    dve.wait_ge(*exped.at(rank(exps, j) + 1))
                    i = rank(lev, j)
                    if i >= 2:
                        if rank(prod, lev[i - 2]) + 1 > 0:
                            dve.wait_ge(*producted.at(rank(prod, lev[i - 2]) + 1))
                    dv, xv = halves(d, n), halves(xx[i % 2], n)
                    v.tensor_tensor(xv[:, :, 0, :], dv[:, :, 0, :], halves(g.g_k[:, h, :], n)[:, :, 0, :], ALU.mult).then_inc(*built.up())
                    v.tensor_tensor(xv[:, :, 1, :], dv[:, :, 1, :], halves(g.g_q[:, h, :], n)[:, :, 1, :], ALU.mult).then_inc(*built.up())
                elif n == QE or n == KE:
                    dve.wait_ge(*exped.at(rank(exps, j) + 1))
                    if rank(prod, j) > 0:
                        dve.wait_ge(*producted.at(rank(prod, j)))
                    x = g.g_q if n == QE else g.g_k
                    v.tensor_tensor(x[:, h, :], x[:, h, :], d, ALU.mult).then_inc(*applied.up())
                while done < len(prod) and prod[done] <= j - 1:
                    mask(done)
                    done += 1
            while done < len(prod):
                mask(done)
                done += 1

        @block.tensor
        def _(pe):
            for i, j in enumerate(prod):
                h, n = jobs[j]
                if i - 1 > 0:
                    pe.wait_ge(*maskd.at(i - 1))
                if n == DIAG:
                    left, right, tiles = g.g_k[:, h, :], g.g_q[:, h, :], ALLT
                else:
                    pe.wait_ge(*built.at(2 * rank(lev, j) + 2))
                    left = right = xx[rank(lev, j) % 2]
                    tiles = ALLT if n < 4 else XT
                for t in tiles:
                    a, m = TILES[t]
                    out_ = window(i)[0:META, 496:512] if t == 0 else window(i)[:, 512 + (t - 1) * P:512 + t * P]
                    last = nc.tensor.matmul(out_, left[:, a:a + m], right[:, a:a + m], start=True, stop=True)
                last.then_inc(*producted.up())

        @block.sync
        def _(sp):
            g.feed(sp, out[0] + 2)


def stage_hg_scan(g, out):
    nc = g.nc
    spare, second = g.ring[:, (out[0] + 3) % 4, :], g.ring[:, (out[0] + 2) % 4, :]
    cut = lambda ap, n: ap[:, n * D:(n + 1) * D].rearrange("p (h d) -> p h d", h=HG)
    S, kT, osq = (cut(spare, n) for n in range(3))
    o = [cut(spare, 3), cut(second, 1)]
    eb = g.small[:, 450:490].rearrange("p (h t) -> p h t", h=HG)
    so = g.small[:, 490:498]
    gain = second[:, 0:P]
    chain, exped, kturned, kplaced, outs, upds, state, summed, gchain, rooted, normed, turned, moved, gained, copied, gates = g.sig(
        "vector_step", "decays_exped", "keys_transposed", "keys_placed", "outputs_ready", "updates_ready", "state_ready", "heads_summed",
        "gpsimd_step", "norm_ready", "rows_normed", "rows_transposed", "transposed_moved", "gains_loaded", "outputs_copied", "gates_scaled")
    pair = lambda n, m: g.psum[0:m, n:n + 2, :].rearrange("p b (h d) -> p (b h) d", d=P)
    with nc.Block() as block:
        @block.tensor
        def _(pe):
            mm, tr = nc.tensor.matmul, nc.tensor.transpose

            def finish(t):
                a, n = TILES[t]
                pe.wait_ge(*normed.at(t + 1))
                if t:
                    pe.wait_ge(*moved.at(2 * t))
                for c in range(KD):
                    last = tr(g.psum[:, 6 + c // 4, (c % 4) * P:(c % 4) * P + n], o[t % 2][0:n, c, :], g.c("identity")[0:n, 0:n])
                last.then_inc(*turned.up())

            for t in ALLT:
                a, n = TILES[t]
                if t:
                    pe.wait_ge(*kplaced.at(2 * t))
                for h in range(HG):
                    last = tr(pair(0, n)[:, h, :], g.g_k[:, h, a:a + n], g.c("identity"))
                last.then_inc(*kturned.up())
                pe.wait_ge(*state.at(2 * t + 1))
                for h in range(HG):
                    mm(pair(2, n)[:, h, :], g.hT[0:n, h, a:a + n], g.g_v[0:n, t, h * P:(h + 1) * P], start=True, stop=False)
                    last = mm(pair(2, n)[:, h, :], g.g_q[:, h, a:a + n], S[:, h, :], start=False, stop=True)
                last.then_inc(*outs.up())
                pe.wait_ge(*kplaced.at(2 * t + 2))
                for h in range(HG):
                    last = mm(pair(4, P)[:, h, :], kT[0:n, h, :], g.g_v[0:n, t, h * P:(h + 1) * P], start=True, stop=True)
                last.then_inc(*upds.up())
                if t:
                    finish(t - 1)
            finish(ALLT[-1])

        @block.sync
        def _(sp):
            sp.dma_start(gain, g.a["hg_o_norm_2"].to_broadcast([P, P])).then_inc(*gained.up(16))

        @block.scalar
        def _(act):
            b = g.g_b
            nc.scalar.activation(eb[:, :, 0], b[:, :, META - 1], ACT.Exp).then_inc(*exped.up())
            nc.scalar.activation(eb[:, :, 1:5], b[:, :, META + P - 1::P], ACT.Exp).then_inc(*exped.up())

            def move(t):
                a, n = TILES[t]
                act.wait_ge(*turned.at(t + 1))
                for half in range(2):
                    nc.scalar.activation(g.hT[:, 4 * half:4 * half + 4, a:a + n], g.psum[:, 6 + half, :].rearrange("p (c m) -> p c m", c=4)[:, :, 0:n], ACT.Copy).then_inc(*moved.up())

            for t in ALLT:
                a, n = TILES[t]
                act.wait_ge(*kturned.at(t + 1))
                if t:
                    act.wait_ge(*upds.at(t))
                for half in range(2):
                    nc.scalar.activation(kT[0:n, 4 * half:4 * half + 4, :], pair(0, n)[:, 4 * half:4 * half + 4, :], ACT.Copy).then_inc(*kplaced.up())
                act.wait_ge(*copied.at(2 * t + 2))
                if t:
                    act.wait_ge(*normed.at(t))
                for h in range(HG):
                    nc.scalar.activation(osq[0:n, h, :], o[t % 2][0:n, h, :], ACT.Square, accum_out=so[0:n, h:h + 1]).then_inc(*summed.up())
                if t:
                    move(t - 1)
            move(ALLT[-1])

        @block.gpsimd
        def _(pool):
            pool.wait_ge(*gained.at(16))
            for t in ALLT:
                n = TILES[t][1]
                gate = g.g_g[0:n, t, :].rearrange("p (h d) -> p h d", h=HG)
                nc.gpsimd.tensor_tensor(gate, gate, gain[0:n, :].unsqueeze(1).to_broadcast([n, HG, P]), ALU.mult).then_inc(*gates.up())
                pool.wait_ge(*summed.at(HG * (t + 1)))
                inverse_root(g, pool, so[0:n, :], so[0:n, :], 1.0 / P, gchain, rooted)

        @block.vector
        def _(dve):
            v = nc.vector
            v.memset(S, 0.0).then_inc(*state.up())
            dve.wait_ge(*state.at(1))
            dve.wait_ge(*exped.at(2))
            for t in ALLT:
                a, n = TILES[t]
                on = o[t % 2][0:n, :, :]
                dve.wait_ge(*outs.at(t + 1))
                if t >= 2:
                    dve.wait_ge(*turned.at(t - 1))
                for half in range(2):
                    v.tensor_copy(on[:, 4 * half:4 * half + 4, :], pair(2, n)[:, 4 * half:4 * half + 4, :]).then_inc(*copied.up())
                v.tensor_tensor(S, S, eb[:, :, t:t + 1].to_broadcast([P, HG, P]), ALU.mult).then_inc(*chain.up())
                dve.wait_ge(*copied.last())
                dve.wait_ge(*chain.last())
                dve.wait_ge(*upds.at(t + 1))
                v.tensor_tensor(S[:, 0:4, :], S[:, 0:4, :], pair(4, P)[:, 0:4, :], ALU.add).then_inc(*state.up())
                v.tensor_tensor(S[:, 4:8, :], S[:, 4:8, :], pair(4, P)[:, 4:8, :], ALU.add).then_inc(*state.up())
                dve.wait_ge(*state.last())
                dve.wait_ge(*rooted.at(t + 1))
                v.tensor_tensor(on, on, so[0:n, :].unsqueeze(2).to_broadcast([n, HG, P]), ALU.mult).then_inc(*chain.up())
                dve.wait_ge(*chain.last())
                dve.wait_ge(*gates.at(t + 1))
                v.tensor_tensor(on, on, g.g_g[0:n, t, :].rearrange("p (h d) -> p h d", h=HG), ALU.mult).then_inc(*normed.up())


def plan_first_half(g):
    a = g.a
    even = [g.plan(a["ev_w_in"][0][:, 0:512], KD, 512)] + [g.plan(a["ev_w_in"][0][:, 512 + 384 * n:896 + 384 * n], KD, 384) for n in range(8)]
    even_out = [g.plan(a["ev_w_out"][0][:, 512 * n:512 * n + 512], KD, 512) for n in range(2)]
    return even, even_out


def plan_ple(g, layer):
    proj = g.plan(g.a["ple_w_proj"][layer], 2, D)
    return [g.plan(g.a["ple_w_gate"][layer][:, 512 * n:512 * n + 512], KD, 512) for n in range(2)], proj


def build(nc, a, const_at):
    with ExitStack() as ctx:
        g = Program(nc, ctx, a, const_at)
        plans = {}
        plans["even"] = plan_first_half(g)
        plans["ple0"] = plan_ple(g, 0)
        plans["odd"] = plan_odd(g)
        plans["ple1"] = plan_ple(g, 1)
        plans["fox"] = plan_fox(g)
        plans["hg"] = plan_hg(g)
        stage_load(g)
        even, even_out = plans["even"]
        stage_norm(g, XT, g.gain(0), even[3])
        stage_even_in(g, even, even_out[0] + 2)
        stage_even_attention(g, even_out[0] + 4)
        stage_out(g, XT, even_out, even_out[1] + 4)
        g.top = 0
        gate, proj = plans["ple0"]
        stage_norm(g, XT, None, g.fed)
        stage_ple(g, 0, gate, proj, gate[1] + 4)
        odd_layer(g, plans["odd"])
        gate, proj = plans["ple1"]
        stage_norm(g, XT, None, g.fed)
        stage_ple(g, 1, gate, proj, gate[1] + 4)
        fox_layer(g, plans["fox"])
        moe_layer(g, 0, plans["hg"][0][0] + 1)
        hg_layer(g, plans["hg"])
        moe_layer(g, 1, g.fed)
        stage_store(g)


def stage_store(g):
    stored = g.sig("output_stored")
    with g.nc.Block() as block:
        @block.sync
        def _(sp):
            sp.dma_start(g.a["out"].rearrange("b (t p) d -> p (b t) d", p=P), g.h[:, 1:5, :]).then_inc(*stored.up(16))
            sp.wait_ge(*stored.last())


_INS = ["x", "positions", "ple_w_gate", "ple_w_proj", "ev_w_in", "ev_pool_w", "ev_pool_scale",
        "ev_q_norm", "ev_k_norm", "ev_lambda", "ev_subln", "ev_w_out", "od_w_in", "od_q_a_norm", "od_w_uq",
        "od_kv_a_norm", "od_w_ukv", "od_q_norm", "od_k_norm", "od_a_log", "od_dt_bias", "od_o_norm",
        "od_w_out", "meta_tokens_2", "fox_w_in_2", "fox_b_f_2", "fox_q_norm_2", "fox_k_norm_2",
        "fox_w_out_2", "hg_w_in_2", "hg_b_f_2", "hg_lb_logits_2", "hg_o_norm_2", "hg_w_out_2",
        "moe_w_grp_2", "moe_b_grp_2", "moe_w_rt_2", "moe_b_rt_2", "moe_w_up_2", "moe_w_down_2"]


def kernel(**inputs):
    import numpy as _np
    import concourse.bacc as _bacc
    from concourse import mybir as _mybir

    nc = _bacc.Bacc("TRN2", target_bir_lowering=False, num_devices=1)
    arrays, args = {}, {}
    at, constants = host_constants()
    laid = {name: _np.ascontiguousarray(inputs[name]) for name in _INS}
    laid["p_T"] = _np.ascontiguousarray(_np.transpose(_np.asarray(inputs["p"])[:, 0], (0, 2, 1)))
    laid["od_conv_T"] = _np.ascontiguousarray(_np.transpose(_np.asarray(inputs["od_conv_w"])[0], (1, 0)))
    laid["ev_pool_w"] = _np.ascontiguousarray(_np.asarray(inputs["ev_pool_w"])[0])
    norms = _np.concatenate([_np.asarray(inputs[n]).reshape(-1, D) for n in ("norm_g", "fox_norm_2", "hg_norm_2", "moe_norm_2")])
    laid["norm_gains"] = _np.ascontiguousarray(norms.reshape(-1, KD, P).transpose(2, 0, 1).reshape(P, -1))
    laid["constants"] = constants
    for name, v in laid.items():
        arrays[f"in_{name}"] = v
        args[name] = nc.dram_tensor(f"in_{name}", v.shape, _mybir.dt.from_np(v.dtype), kind="ExternalInput").ap()
    args["out"] = nc.dram_tensor("out_0", (1, SEQ, D), F32, kind="ExternalOutput").ap()
    args["x_rows"] = nc.dram_tensor("expert_rows_in", (SLOTS, D), F32).ap()
    args["y_rows"] = nc.dram_tensor("expert_rows_out", (SLOTS, D), F32).ap()
    build(nc, args, at)
    from concourse.bass_utils import run_bass_kernel_spmd as _run
    r = _run(nc, [arrays], core_ids=[0])
    return r.results[0]["out_0"]
```
